# Optimizing a Trainium2 kernel written in Bass

```python
import math
import jax, jax.numpy as jnp
from jax import lax
import numpy as np

D_MODEL = 1024
BATCH = 1
SEQ = 512
DEPTH = 2

HEAD_DIM = 64
ATTN_Q_HEADS = D_MODEL // (2 * HEAD_DIM)
ATTN_KV_HEADS = max(1, ATTN_Q_HEADS // 4)
RET_HEADS = D_MODEL // (2 * HEAD_DIM)
ATTN_WIDTH = ATTN_Q_HEADS * HEAD_DIM
KV_WIDTH = ATTN_KV_HEADS * HEAD_DIM
RET_WIDTH = RET_HEADS * HEAD_DIM
MIX_WIDTH = ATTN_WIDTH + RET_WIDTH
IN_SPLITS = (ATTN_WIDTH,
             ATTN_WIDTH + KV_WIDTH,
             ATTN_WIDTH + 2 * KV_WIDTH,
             ATTN_WIDTH + 2 * KV_WIDTH + RET_WIDTH,
             ATTN_WIDTH + 2 * KV_WIDTH + 2 * RET_WIDTH,
             ATTN_WIDTH + 2 * KV_WIDTH + 3 * RET_WIDTH)
IN_WIDTH = ATTN_WIDTH + 2 * KV_WIDTH + 4 * RET_WIDTH
WINDOW = 128
ATTN_BLOCK = 128
RET_CHUNK = 128
ROPE_THETA = 10000.0
RET_THETA = 10000.0
D_FF = ((8 * D_MODEL // 3 + 127) // 128) * 128
LN_EPS = 1e-5
GN_EPS = 1e-6
DEEPNORM_ALPHA = (2 * DEPTH) ** 0.25
DEEPNORM_BETA = (8 * DEPTH) ** -0.25


def layer_norm(x, g, b):
    xf = x.astype(jnp.float32)
    mu = jnp.mean(xf, axis=-1, keepdims=True)
    var = jnp.mean(jnp.square(xf - mu), axis=-1, keepdims=True)
    return ((xf - mu) * lax.rsqrt(var + LN_EPS)).astype(x.dtype) * g + b

def swiglu_ffn(x, w_gu, w_down):
    a, u = jnp.split(x @ w_gu, 2, axis=-1)
    return (jax.nn.silu(a) * u) @ w_down

def rope_tables(seq):
    pos = jnp.arange(seq, dtype=jnp.float32)
    inv_freq = ROPE_THETA ** (-jnp.arange(0, HEAD_DIM, 2, dtype=jnp.float32) / HEAD_DIM)
    ang = pos[:, None] * inv_freq[None, :]
    return jnp.cos(ang), jnp.sin(ang)

def retention_rotation_tables(seq):
    pos = jnp.arange(seq, dtype=jnp.float32)
    ang_freq = 1.0 / (RET_THETA ** jnp.linspace(0.0, 1.0, HEAD_DIM // 2, dtype=jnp.float32))
    ang = pos[:, None] * ang_freq[None, :]
    return jnp.cos(ang), jnp.sin(ang)

def apply_rope(x, cos, sin):
    c = cos[:, None, :].astype(x.dtype)
    s = sin[:, None, :].astype(x.dtype)
    x1, x2 = jnp.split(x, 2, axis=-1)
    return jnp.concatenate([x1 * c - x2 * s, x2 * c + x1 * s], axis=-1)

def apply_pair_rotation(x, cos, sin):
    c = cos[:, None, :].astype(x.dtype)
    s = sin[:, None, :].astype(x.dtype)
    xe = x[..., 0::2]
    xo = x[..., 1::2]
    return jnp.stack([xe * c - xo * s, xo * c + xe * s], axis=-1).reshape(x.shape)

def sliding_window_sink_attention(q, k, v, sinks):
    B, S, Hq, D = q.shape
    Hkv = k.shape[2]
    G = Hq // Hkv
    C = ATTN_BLOCK
    N = S // C
    qb = (q * (HEAD_DIM ** -0.5)).reshape(B, N, C, Hkv, G, D)

    def with_prev_block(t):
        tb = t.reshape(B, N, C, Hkv, D)
        prev = jnp.pad(tb, ((0, 0), (1, 0), (0, 0), (0, 0), (0, 0)))[:, :-1]
        return jnp.concatenate([prev, tb], axis=2)

    kk = with_prev_block(k)
    vv = with_prev_block(v)
    s = jnp.einsum('bnqhgd,bnkhd->bnhgqk', qb, kk).astype(jnp.float32)
    q_idx = jnp.arange(C)[:, None]
    k_rel = jnp.arange(2 * C)[None, :] - C
    rel = q_idx - k_rel
    band = (rel >= 0) & (rel < WINDOW)
    valid = (jnp.arange(N)[:, None] * C + k_rel) >= 0
    mask = band[None, :, :] & valid[:, None, :]
    s = jnp.where(mask[None, :, None, None, :, :], s, -jnp.inf)
    sink = sinks.astype(jnp.float32).reshape(Hkv, G)[None, None, :, :, None, None]
    m = jnp.maximum(jnp.max(s, axis=-1, keepdims=True), sink)
    p = jnp.exp(s - m)
    denom = jnp.sum(p, axis=-1, keepdims=True) + jnp.exp(sink - m)
    o = jnp.einsum('bnhgqk,bnkhd->bnqhgd', (p / denom).astype(v.dtype), vv)
    return o.reshape(B, S, Hq * D)

def multiscale_retention(q, k, v, gate):
    B, S, H, D = q.shape
    C = RET_CHUNK
    N = S // C
    log_gamma = jnp.log1p(-jnp.exp2(-5.0 - jnp.arange(H, dtype=jnp.float32)))
    idx = jnp.arange(C, dtype=jnp.float32)
    diff = idx[:, None] - idx[None, :]
    decay = jnp.where(diff[None] >= 0,
                      jnp.exp(jnp.maximum(diff, 0.0)[None] * log_gamma[:, None, None]), 0.0)
    w_k = jnp.exp((C - 1.0 - idx)[None, :] * log_gamma[:, None])
    w_q = jnp.exp((idx + 1.0)[None, :] * log_gamma[:, None])
    g_chunk = jnp.exp(C * log_gamma)
    qc = q.reshape(B, N, C, H, D)
    kc = k.reshape(B, N, C, H, D)
    vc = v.reshape(B, N, C, H, D)
    scores = jnp.einsum('bnihd,bnjhd->bnhij', qc, kc) * decay
    intra = jnp.einsum('bnhij,bnjhe->bnihe', scores, vc)
    kv = jnp.einsum('bnjhd,hj,bnjhe->bnhde', kc, w_k, vc)

    def step(state, kv_n):
        return state * g_chunk[None, :, None, None] + kv_n, state

    init = jnp.zeros((B, H, D, D), dtype=kv.dtype)
    _, states = lax.scan(step, init, jnp.moveaxis(kv, 1, 0))
    states = jnp.moveaxis(states, 0, 1)
    cross = jnp.einsum('bnihd,hi,bnhde->bnihe', qc, w_q, states)
    o = (intra + cross).reshape(B, S, H, D).astype(jnp.float32)
    mu = jnp.mean(o, axis=-1, keepdims=True)
    var = jnp.mean(jnp.square(o - mu), axis=-1, keepdims=True)
    o = ((o - mu) * lax.rsqrt(var + GN_EPS)).reshape(B, S, H * D).astype(gate.dtype)
    return jax.nn.silu(gate) * o

def hybrid_mixer(x, w_in, w_out, sinks, rope_cos, rope_sin, ret_cos, ret_sin):
    B, S, _ = x.shape
    h = x @ w_in
    qa, ka, va, qr, kr, vr, gr = jnp.split(h, IN_SPLITS, axis=-1)
    qa = apply_rope(qa.reshape(B, S, ATTN_Q_HEADS, HEAD_DIM), rope_cos, rope_sin)
    ka = apply_rope(ka.reshape(B, S, ATTN_KV_HEADS, HEAD_DIM), rope_cos, rope_sin)
    va = va.reshape(B, S, ATTN_KV_HEADS, HEAD_DIM)
    y_attn = sliding_window_sink_attention(qa, ka, va, sinks)
    qr = apply_pair_rotation(qr.reshape(B, S, RET_HEADS, HEAD_DIM), ret_cos, ret_sin)
    kr = apply_pair_rotation(kr.reshape(B, S, RET_HEADS, HEAD_DIM), ret_cos, ret_sin) * (HEAD_DIM ** -0.5)
    y_ret = multiscale_retention(qr, kr, vr.reshape(B, S, RET_HEADS, HEAD_DIM), gr)
    return jnp.concatenate([y_attn, y_ret], axis=-1) @ w_out

def first_inputs(seed: int = 0) -> dict:
    key = jax.random.key(seed)
    ks = jax.random.split(key, 16)
    f32 = jnp.float32
    x = jax.random.normal(ks[0], (BATCH, SEQ, D_MODEL), f32)
    col_scale = jnp.concatenate([
        jnp.ones((ATTN_WIDTH + KV_WIDTH,), f32),
        jnp.full((KV_WIDTH,), DEEPNORM_BETA, f32),
        jnp.ones((2 * RET_WIDTH,), f32),
        jnp.full((RET_WIDTH,), DEEPNORM_BETA, f32),
        jnp.ones((RET_WIDTH,), f32)])
    w_in = jax.random.normal(ks[1], (DEPTH, D_MODEL, IN_WIDTH), f32) * (D_MODEL ** -0.5) * col_scale
    w_out = jax.random.normal(ks[2], (DEPTH, MIX_WIDTH, D_MODEL), f32) * (MIX_WIDTH ** -0.5) * DEEPNORM_BETA
    attn_sinks = 0.5 * jax.random.normal(ks[3], (DEPTH, ATTN_Q_HEADS), f32)
    ffn1_w_gu = jax.random.normal(ks[4], (DEPTH, D_MODEL, 2 * D_FF), f32) * (D_MODEL ** -0.5) * DEEPNORM_BETA
    ffn1_w_down = jax.random.normal(ks[5], (DEPTH, D_FF, D_MODEL), f32) * (D_FF ** -0.5) * DEEPNORM_BETA
    ffn2_w_gu = jax.random.normal(ks[6], (DEPTH, D_MODEL, 2 * D_FF), f32) * (D_MODEL ** -0.5) * DEEPNORM_BETA
    ffn2_w_down = jax.random.normal(ks[7], (DEPTH, D_FF, D_MODEL), f32) * (D_FF ** -0.5) * DEEPNORM_BETA
    ln1_g = 1.0 + 0.02 * jax.random.normal(ks[8], (DEPTH, D_MODEL), f32)
    ln1_b = 0.02 * jax.random.normal(ks[9], (DEPTH, D_MODEL), f32)
    ln2_g = 1.0 + 0.02 * jax.random.normal(ks[10], (DEPTH, D_MODEL), f32)
    ln2_b = 0.02 * jax.random.normal(ks[11], (DEPTH, D_MODEL), f32)
    ln3_g = 1.0 + 0.02 * jax.random.normal(ks[12], (DEPTH, D_MODEL), f32)
    ln3_b = 0.02 * jax.random.normal(ks[13], (DEPTH, D_MODEL), f32)
    return {"x": x, "w_in": w_in, "w_out": w_out, "attn_sinks": attn_sinks,
            "ffn1_w_gu": ffn1_w_gu, "ffn1_w_down": ffn1_w_down,
            "ffn2_w_gu": ffn2_w_gu, "ffn2_w_down": ffn2_w_down,
            "ln1_g": ln1_g, "ln1_b": ln1_b, "ln2_g": ln2_g, "ln2_b": ln2_b,
            "ln3_g": ln3_g, "ln3_b": ln3_b}

def first_block(x, w_in, w_out, attn_sinks, ffn1_w_gu, ffn1_w_down, ffn2_w_gu, ffn2_w_down,
              ln1_g, ln1_b, ln2_g, ln2_b, ln3_g, ln3_b):
    S = x.shape[1]
    rope_cos, rope_sin = rope_tables(S)
    ret_cos, ret_sin = retention_rotation_tables(S)
    for l in range(DEPTH):
        x = layer_norm(DEEPNORM_ALPHA * x + 0.5 * swiglu_ffn(x, ffn1_w_gu[l], ffn1_w_down[l]),
                       ln1_g[l], ln1_b[l])
        x = layer_norm(DEEPNORM_ALPHA * x + hybrid_mixer(x, w_in[l], w_out[l], attn_sinks[l],
                                                         rope_cos, rope_sin, ret_cos, ret_sin),
                       ln2_g[l], ln2_b[l])
        x = layer_norm(DEEPNORM_ALPHA * x + 0.5 * swiglu_ffn(x, ffn2_w_gu[l], ffn2_w_down[l]),
                       ln3_g[l], ln3_b[l])
    return x


DEPTH_2 = 1

N_META = 16
A_HEADS = 4
A_DK = 64
A_DV = 2 * A_DK
B_HEADS = 4
B_DQ = 128
B_DC = 256
B_DV = 128
IDX_HEADS = 8
IDX_DIM = 64
IDX_TOPK_MAX = 256
REL_BUCKETS = 32
REL_MAX_DIST = 128
N_BIAS_HEADS = A_HEADS + B_HEADS
D_FF_2 = 2816
Q_BLOCK = 128
EPS = 1e-6
A_SCALE = A_DK ** -0.5
B_SCALE = B_DC ** -0.5

IN_SIZES = (
    A_HEADS * 2 * A_DK,
    A_HEADS * 2 * A_DK,
    A_HEADS * A_DV,
    B_HEADS * B_DQ,
    B_DC,
    IDX_HEADS * IDX_DIM,
    IDX_DIM,
    IDX_HEADS,
)
N_IN = sum(IN_SIZES)
IN_SPLITS_2 = [int(v) for v in np.cumsum(IN_SIZES)[:-1]]
D_MIX = A_HEADS * A_DV + B_HEADS * B_DV


def rmsnorm(x, g):
    xf = x.astype(jnp.float32)
    y = xf * lax.rsqrt(jnp.mean(xf * xf, axis=-1, keepdims=True) + EPS)
    return (y * g.astype(jnp.float32)).astype(x.dtype)

def swiglu(x, w_gate, w_up, w_down):
    return (jax.nn.silu(x @ w_gate) * (x @ w_up)) @ w_down

def rel_bucket(q_pos, k_pos):
    max_exact = REL_BUCKETS // 2
    n = jnp.maximum(q_pos - k_pos, 0)
    nf = jnp.maximum(n, 1).astype(jnp.float32)
    large = max_exact + (jnp.log(nf / max_exact) / math.log(REL_MAX_DIST / max_exact)
                         * (REL_BUCKETS - max_exact)).astype(jnp.int32)
    large = jnp.minimum(large, REL_BUCKETS - 1)
    return jnp.where(n < max_exact, n, large)

def diff_attention(q, k, v, lam, bias_a, subln_g, lam_init):
    bsz, length = q.shape[0], q.shape[1]
    outs = []
    for start in range(0, length, Q_BLOCK):
        stop = min(start + Q_BLOCK, length)
        q_pos = jnp.arange(start, stop)
        k_pos = jnp.arange(stop)
        bias = bias_a[rel_bucket(q_pos[:, None], k_pos[None, :])].transpose(2, 0, 1)
        s = jnp.einsum('bqhmd,bkhmd->bhmqk', q[:, start:stop], k[:, :stop]).astype(jnp.float32)
        s = s * A_SCALE + bias[None, :, None].astype(jnp.float32)
        s = jnp.where(k_pos[None, :] <= q_pos[:, None], s, -jnp.inf)
        p = jax.nn.softmax(s, axis=-1)
        a = p[:, :, 0] - lam * p[:, :, 1]
        outs.append(jnp.einsum('bhqk,bkhd->bqhd', a.astype(v.dtype), v[:, :stop]))
    o = jnp.concatenate(outs, axis=1)
    o = rmsnorm(o, subln_g) * (1.0 - lam_init)
    return o.reshape(bsz, length, A_HEADS * A_DV)

def dsa_attention(q_lat, c, iq, ik, iw, w_uv, bias_b, topk):
    bsz, length = q_lat.shape[0], q_lat.shape[1]
    gather = jax.vmap(lambda cb, ib: cb[ib])
    outs = []
    for start in range(0, length, Q_BLOCK):
        stop = min(start + Q_BLOCK, length)
        q_pos = jnp.arange(start, stop)
        k_pos = jnp.arange(stop)
        dots = jnp.einsum('bqhd,bkd->bqhk', iq[:, start:stop], ik[:, :stop]).astype(jnp.float32)
        w = iw[:, start:stop].astype(jnp.float32) * (IDX_HEADS ** -0.5)
        score = jnp.einsum('bqh,bqhk->bqk', w, jax.nn.relu(dots * (IDX_DIM ** -0.5)))
        score = jnp.where(k_pos[None, None, :] <= q_pos[None, :, None], score, -jnp.inf)
        _, sel = lax.top_k(score, min(topk, stop))
        valid = sel <= q_pos[None, :, None]
        g = gather(c, sel)
        bias = bias_b[rel_bucket(q_pos[None, :, None], sel)].transpose(0, 3, 1, 2)
        s = jnp.einsum('bqhc,bqkc->bhqk', q_lat[:, start:stop], g).astype(jnp.float32)
        s = s * B_SCALE + bias.astype(jnp.float32)
        s = jnp.where(valid[:, None], s, -jnp.inf)
        p = jax.nn.softmax(s, axis=-1)
        o_lat = jnp.einsum('bhqk,bqkc->bqhc', p.astype(g.dtype), g)
        outs.append(jnp.einsum('bqhc,hcd->bqhd', o_lat, w_uv))
    o = jnp.concatenate(outs, axis=1)
    return o.reshape(bsz, length, B_HEADS * B_DV)

def second_inputs(seed: int = 0) -> dict:
    key = jax.random.key(seed)
    ks = jax.random.split(key, 32)
    f32 = jnp.float32

    def nrm(k, shape, scale):
        return jax.random.normal(k, shape, f32) * scale

    def gain(k, shape):
        return 1.0 + 0.02 * jax.random.normal(k, shape, f32)

    L = DEPTH_2
    return {
        'x': nrm(ks[0], (BATCH, SEQ, D_MODEL), 1.0),
        'meta_tokens': nrm(ks[1], (N_META, D_MODEL), 1.0),
        'rel_bias': nrm(ks[2], (REL_BUCKETS, N_BIAS_HEADS), 0.1),
        'ffn1_norm': gain(ks[3], (L, D_MODEL)),
        'ffn1_w_gate': nrm(ks[4], (L, D_MODEL, D_FF_2), D_MODEL ** -0.5),
        'ffn1_w_up': nrm(ks[5], (L, D_MODEL, D_FF_2), D_MODEL ** -0.5),
        'ffn1_w_down': nrm(ks[6], (L, D_FF_2, D_MODEL), D_FF_2 ** -0.5),
        'mix_norm': gain(ks[7], (L, D_MODEL)),
        'w_in': nrm(ks[8], (L, D_MODEL, N_IN), D_MODEL ** -0.5),
        'a_q_norm': gain(ks[9], (L, A_DK)),
        'a_k_norm': gain(ks[10], (L, A_DK)),
        'a_lambda_q1': nrm(ks[11], (L, A_DK), 0.1),
        'a_lambda_k1': nrm(ks[12], (L, A_DK), 0.1),
        'a_lambda_q2': nrm(ks[13], (L, A_DK), 0.1),
        'a_lambda_k2': nrm(ks[14], (L, A_DK), 0.1),
        'a_subln': gain(ks[15], (L, A_DV)),
        'b_kv_norm': gain(ks[16], (L, B_DC)),
        'b_w_uk': nrm(ks[17], (L, B_HEADS, B_DQ, B_DC), B_DQ ** -0.5),
        'b_q_norm': gain(ks[18], (L, B_DC)),
        'b_w_uv': nrm(ks[19], (L, B_HEADS, B_DC, B_DV), B_DC ** -0.5),
        'w_out': nrm(ks[20], (L, D_MIX, D_MODEL), D_MIX ** -0.5),
        'ffn2_norm': gain(ks[21], (L, D_MODEL)),
        'ffn2_w_gate': nrm(ks[22], (L, D_MODEL, D_FF_2), D_MODEL ** -0.5),
        'ffn2_w_up': nrm(ks[23], (L, D_MODEL, D_FF_2), D_MODEL ** -0.5),
        'ffn2_w_down': nrm(ks[24], (L, D_FF_2, D_MODEL), D_FF_2 ** -0.5),
    }

def second_block(x, meta_tokens, rel_bias, ffn1_norm, ffn1_w_gate, ffn1_w_up, ffn1_w_down,
              mix_norm, w_in, a_q_norm, a_k_norm, a_lambda_q1, a_lambda_k1, a_lambda_q2,
              a_lambda_k2, a_subln, b_kv_norm, b_w_uk, b_q_norm, b_w_uv, w_out,
              ffn2_norm, ffn2_w_gate, ffn2_w_up, ffn2_w_down):
    bsz, seq = x.shape[0], x.shape[1]
    topk = min(IDX_TOPK_MAX, seq // 4)
    meta = jnp.broadcast_to(meta_tokens.astype(x.dtype)[None], (bsz, N_META, D_MODEL))
    h = jnp.concatenate([meta, x], axis=1)
    length = h.shape[1]
    bias_a = rel_bias[:, :A_HEADS]
    bias_b = rel_bias[:, A_HEADS:]

    for l in range(DEPTH_2):
        h = h + 0.5 * swiglu(rmsnorm(h, ffn1_norm[l]), ffn1_w_gate[l], ffn1_w_up[l], ffn1_w_down[l])

        u = rmsnorm(h, mix_norm[l]) @ w_in[l]
        qa, ka, va, qb, ckv, iq, ik, iw = jnp.split(u, IN_SPLITS_2, axis=-1)

        qa = rmsnorm(qa.reshape(bsz, length, A_HEADS, 2, A_DK), a_q_norm[l])
        ka = rmsnorm(ka.reshape(bsz, length, A_HEADS, 2, A_DK), a_k_norm[l])
        va = va.reshape(bsz, length, A_HEADS, A_DV)
        lam_init = 0.8 - 0.6 * math.exp(-0.3 * l)
        lam = (jnp.exp(jnp.sum(a_lambda_q1[l].astype(jnp.float32) * a_lambda_k1[l].astype(jnp.float32)))
               - jnp.exp(jnp.sum(a_lambda_q2[l].astype(jnp.float32) * a_lambda_k2[l].astype(jnp.float32)))
               + lam_init)
        o_a = diff_attention(qa, ka, va, lam, bias_a, a_subln[l], lam_init)

        qb = qb.reshape(bsz, length, B_HEADS, B_DQ)
        q_lat = rmsnorm(jnp.einsum('blhd,hdc->blhc', qb, b_w_uk[l]), b_q_norm[l])
        c = rmsnorm(ckv, b_kv_norm[l])
        iq = iq.reshape(bsz, length, IDX_HEADS, IDX_DIM)
        o_b = dsa_attention(q_lat, c, iq, ik, iw, b_w_uv[l], bias_b, topk)

        h = h + jnp.concatenate([o_a, o_b], axis=-1) @ w_out[l]

        h = h + 0.5 * swiglu(rmsnorm(h, ffn2_norm[l]), ffn2_w_gate[l], ffn2_w_up[l], ffn2_w_down[l])

    return h[:, N_META:]


def setup_inputs(seed=0):
    out = dict(first_inputs(seed))
    for name, value in second_inputs(seed + 1).items():
        if name != "x":
            out[name + "_2"] = value
    return out


def reference(
    x, w_in, w_out, attn_sinks, ffn1_w_gu, ffn1_w_down, ffn2_w_gu, ffn2_w_down, ln1_g, ln1_b,
    ln2_g, ln2_b, ln3_g, ln3_b, meta_tokens_2, rel_bias_2, ffn1_norm_2, ffn1_w_gate_2,
    ffn1_w_up_2, ffn1_w_down_2, mix_norm_2, w_in_2, a_q_norm_2, a_k_norm_2, a_lambda_q1_2,
    a_lambda_k1_2, a_lambda_q2_2, a_lambda_k2_2, a_subln_2, b_kv_norm_2, b_w_uk_2, b_q_norm_2,
    b_w_uv_2, w_out_2, ffn2_norm_2, ffn2_w_gate_2, ffn2_w_up_2, ffn2_w_down_2,
):
    x = first_block(
        x, w_in, w_out, attn_sinks, ffn1_w_gu, ffn1_w_down, ffn2_w_gu, ffn2_w_down, ln1_g,
        ln1_b, ln2_g, ln2_b, ln3_g, ln3_b,
    )
    return second_block(
        x, meta_tokens_2, rel_bias_2, ffn1_norm_2, ffn1_w_gate_2, ffn1_w_up_2, ffn1_w_down_2,
        mix_norm_2, w_in_2, a_q_norm_2, a_k_norm_2, a_lambda_q1_2, a_lambda_k1_2, a_lambda_q2_2,
        a_lambda_k2_2, a_subln_2, b_kv_norm_2, b_w_uk_2, b_q_norm_2, b_w_uv_2, w_out_2,
        ffn2_norm_2, ffn2_w_gate_2, ffn2_w_up_2, ffn2_w_down_2,
    )


_drawn_inputs = setup_inputs


def setup_inputs(seed=0):
    import zlib

    import numpy as np

    out = dict(_drawn_inputs(seed))
    spreads = {}
    factors = {'attn_sinks': 8.0,
     'ffn1_norm_2': 4.47,
     'a_q_norm_2': 5.986,
     'a_k_norm_2': 6.563,
     'a_subln_2': 7.926,
     'b_kv_norm_2': 8.0,
     'b_q_norm_2': 8.0,
     'ffn2_norm_2': 8.0}
    for name, (base, spread) in spreads.items():
        noise = np.random.default_rng([zlib.crc32(name.encode()), seed]).standard_normal(out[name].shape)
        drawn = base * np.exp(spread * noise) if base else spread * noise
        out[name] = __import__('jax').numpy.asarray(drawn.astype(out[name].dtype))
    for name, factor in factors.items():
        out[name] = (out[name] * factor).astype(out[name].dtype)
    return out
```

```python
from contextlib import ExitStack

import numpy as np

import concourse.bass as bass
from concourse import mybir

F32 = mybir.dt.float32
F32R = mybir.dt.float32r
ALU = mybir.AluOpType
ACT = mybir.ActivationFunctionType
AX = mybir.AxisListType

P = 128
BIG = 1.0e30

SEQ = 512
META = 16
LEN = META + SEQ
TOK = slice(META, LEN)
MET = slice(0, META)
D = 1024
KT = D // P
DEPTH = 2
D_FF = 2816
FT = D_FF // P
HD = 64
NB = SEQ // P
ALPHA = (2 * DEPTH) ** 0.25
LN_EPS = 1e-5
GN_EPS = 1e-6
RMS_EPS = 1e-6
HEADS = 8
IN_TILES_1 = 22
IN_TILES_2 = 24
A_HEADS = 4
B_HEADS = 4
B_DC = 256
IDX_HEADS = 8
TOPK = 128
BUCKETS = 32
LAM_INIT = 0.2

RAW_SLOTS = 3
SPLIT_SLOTS = 4
AHEAD = 3
PIECE = 8


class Done:

    def __init__(self, sem, value):
        self.sem, self.value = sem, value


class Engine:

    def __init__(self, eng, sem):
        self.eng, self.sem, self.count, self.seen = eng, sem, 0, {}

    def wait(self, after):
        for d in after:
            if d is None or self.seen.get(id(d.sem), 0) >= d.value:
                continue
            self.seen[id(d.sem)] = d.value
            self.eng.wait_ge(d.sem, d.value)

    def do(self, issue, after=(), mark=True):
        self.wait(after)
        instruction = issue()
        if not mark:
            return None
        self.count += 1
        instruction.then_inc(self.sem, 1)
        return Done(self.sem, self.count)

    def dma(self, sem, total, issue, after=()):
        self.wait(after)
        issue().then_inc(sem, 16)
        return Done(sem, total)


class Slots:

    def __init__(self, bufs):
        self.bufs, self.free, self.next = bufs, [[] for _ in bufs], 0

    def take(self):
        n = len(self.bufs)
        i = next(j % n for j in range(self.next, self.next + n) if self.free[j % n] is not None)
        self.next = (i + 1) % n
        free, self.free[i] = self.free[i], None
        return i, self.bufs[i], free


def pieces(matrix, col_tile, tiles):
    return [(matrix, col_tile, k, min(PIECE, tiles - k)) for k in range(0, tiles, PIECE)]


def build(nc, t):
    ctx = ExitStack()
    with ctx:
        sem = lambda name: ctx.enter_context(nc.semaphore(name))
        sb = lambda name, shape, dt=F32: ctx.enter_context(nc.sbuf_tensor(name, shape, dt))

        pe = Engine(nc.tensor, sem("pe_done"))
        act = Engine(nc.scalar, sem("act_done"))
        dve = Engine(nc.vector, sem("dve_done"))
        pool = Engine(nc.gpsimd, sem("pool_done"))
        sp = Engine(nc.sync, sem("sp_done"))

        x = sb("x", [P, KT, LEN])
        x_hi = sb("x_hi", [P, KT, LEN], F32R)
        x_lo = sb("x_lo", [P, KT, LEN], F32R)
        w_raw = [sb(f"w_raw{i}", [P, PIECE * P]) for i in range(RAW_SLOTS)]
        w_hi = [sb(f"w_hi{i}", [P, PIECE * P], F32R) for i in range(SPLIT_SLOTS)]
        w_lo = [sb(f"w_lo{i}", [P, PIECE * P], F32R) for i in range(SPLIT_SLOTS)]
        scratch = Slots([sb(f"scratch{i}", [P, LEN]) for i in range(4)])
        squares = Slots([sb(f"square{i}", [P, LEN]) for i in range(2)])
        ident = sb("ident", [P, P])
        ones = sb("ones", [P, P])
        half = sb("half", [P, P])
        pairs = sb("pairs", [P, 2])
        eps = sb("eps", [P, 4])
        gains = sb("gains", [P, t["gains"].shape[1]])
        small = Slots([sb(f"small{i}", [P, 16]) for i in range(8)])
        psum = ctx.enter_context(nc.psum_tensor("psum", [P, 8, 512], F32))

        bank = lambda i: psum[:, i, :]
        proj_banks = Slots([0, 1, 2])
        work_free = {i: [] for i in range(3, 8)}
        work_at = [3]

        def work_banks(n=1):
            for at in [*range(work_at[0], 9 - n), *range(3, 9 - n)]:
                taken_banks = range(at, at + n)
                if all(work_free[b] is not None for b in taken_banks):
                    break
            else:
                raise AssertionError("all work banks are held")
            free = [d for b in taken_banks for d in work_free[b]]
            for b in taken_banks:
                work_free[b] = None
            work_at[0] = at + n
            return at, free

        def work_release(at, n, readers):
            for b in range(at, at + n):
                work_free[b] = list(readers)

        load_sem = {}

        def load(eng, name, dst, src, after=()):
            load_sem[name] = sem("load_" + name)
            return eng.dma(load_sem[name], 16, lambda: eng.eng.dma_start(dst, src), after)

        x_loaded = load(sp, "x", x[:, :, TOK], t["x"].rearrange("(k p) n -> p k n", p=P))
        meta_loaded = load(sp, "meta", x[:, :, MET], t["meta"].rearrange("(k p) n -> p k n", p=P))
        ident_loaded = load(act, "ident", ident[:], t["ident"])
        half_loaded = load(act, "half", half[:], t["half"])
        gains_loaded = load(act, "gains", gains[:], t["gains"])
        ones_set = dve.do(lambda: nc.vector.memset(ones[:], 1.0))
        consts_set = dve.do(lambda: nc.vector.memset(pairs[:], 0.0))
        for to, value in ((pairs[0:HD, 0:1], 1.0), (pairs[HD:P, 1:2], 1.0),
                          (eps[:, 0:1], LN_EPS), (eps[:, 1:2], RMS_EPS),
                          (eps[:, 2:3], 4.0 * LN_EPS)):
            consts_set = dve.do(lambda to=to, value=value: nc.vector.memset(to, value),
                                after=[consts_set])
        gain_at = t["gain_at"]

        def gain(name, k=0, rows=slice(0, P)):
            c = gain_at[name] + k
            return gains[rows, c:c + 1]

        plan = weight_plan()
        raw_sem = [sem(f"raw{i}") for i in range(RAW_SLOTS)]
        split = []
        piece_read = []
        taken = [0]

        def split_piece(u):
            matrix, m, k0, n = plan[u]
            r, s = u % RAW_SLOTS, u % SPLIT_SLOTS
            src = t[matrix][m, :, k0 * P:(k0 + n) * P]
            loaded = sp.dma(raw_sem[r], 16 * (u // RAW_SLOTS + 1),
                            lambda: nc.sync.dma_start(w_raw[r][:, 0:n * P], src),
                            after=[split[u - RAW_SLOTS][1]] if u >= RAW_SLOTS else [])
            unread = [piece_read[u - SPLIT_SLOTS]] if u >= SPLIT_SLOTS else []
            high = act.do(lambda: nc.scalar.copy(w_hi[s][:, 0:n * P], w_raw[r][:, 0:n * P]),
                          after=[loaded] + unread)
            low = dve.do(lambda: nc.vector.tensor_tensor(
                w_lo[s][:, 0:n * P], w_raw[r][:, 0:n * P], w_hi[s][:, 0:n * P].bitcast(F32),
                ALU.subtract), after=[high])
            split.append((high, low))

        def project(matrix, m, tiles, operand, meta_operand=None, columns=SEQ):
            b, _, free = proj_banks.take()
            done = meta = None
            if meta_operand:
                mb, mfree = work_banks()
            for key in pieces(matrix, m, tiles):
                u = taken[0]
                taken[0] += 1
                assert plan[u] == key, (plan[u], key)
                while len(split) <= min(u + AHEAD, len(plan) - 1):
                    split_piece(len(split))
                _, _, k0, n = key
                s = u % SPLIT_SLOTS
                for k in range(k0, k0 + n):
                    hi, lo, ready = operand(k)
                    w_h = w_hi[s][:, (k - k0) * P:(k - k0 + 1) * P]
                    w_l = w_lo[s][:, (k - k0) * P:(k - k0 + 1) * P]
                    first, last = k == 0, k == tiles - 1
                    need = [split[u][1], *ready] + (free if first else [])
                    out = bank(b)
                    pe.do(lambda o=out, a=w_h, c=hi, f=first: nc.tensor.matmul(
                        o, a, c, start=f, stop=False), after=need, mark=False)
                    pe.do(lambda o=out, a=w_h, c=lo: nc.tensor.matmul(
                        o, a, c, start=False, stop=False), mark=False)
                    end = k == k0 + n - 1 and not meta_operand
                    done = pe.do(lambda o=out, a=w_l, c=hi, e=last: nc.tensor.matmul(
                        o, a, c, start=False, stop=e), mark=end) or done
                    if meta_operand:
                        hi, lo, ready = meta_operand(k)
                        out = psum[:, mb, 0:META]
                        pe.do(lambda o=out, a=w_h, c=hi, f=first: nc.tensor.matmul(
                            o, a, c, start=f, stop=False),
                            after=[*ready] + (mfree if first else []), mark=False)
                        pe.do(lambda o=out, a=w_h, c=lo: nc.tensor.matmul(
                            o, a, c, start=False, stop=False), mark=False)
                        done = pe.do(lambda o=out, a=w_l, c=hi, e=last: nc.tensor.matmul(
                            o, a, c, start=False, stop=e), mark=k == k0 + n - 1) or done
                piece_read.append(done)
            if meta_operand:
                return b, done, mb
            return b, done

        def proj_release(b, readers):
            proj_banks.free[b] = list(readers)

        def split_into(hi, lo, value, after=()):
            h = act.do(lambda: nc.scalar.copy(hi, value), after=after)
            l = dve.do(lambda: nc.vector.tensor_tensor(lo, value, hi.bitcast(F32), ALU.subtract),
                       after=[h])
            return h, l

        ready = [[] for _ in range(KT)]
        x_ready = [[] for _ in range(KT)]

        def tokens_operand(k):
            return x_hi[:, k, TOK], x_lo[:, k, TOK], ready[k]

        def meta_operand_x(k):
            return x_hi[:, k, MET], x_lo[:, k, MET], ready[k]

        class Stats:

            def __init__(self, groups, meta):
                self.groups = groups
                self.blocks = [(META + P * j, P) for j in range(NB)] + ([(0, META)] if meta else [])
                self.sums, self.sums_free = work_banks()
                self.first = True

            def add(self, tile, after, last):
                g = self.groups
                for j, (c, w) in enumerate(self.blocks):
                    done = pe.do(lambda o=psum[0:w, self.sums, j * g:(j + 1) * g],
                                 a=tile[:, c:c + w], r=ones[:, 0:1] if g == 1 else pairs[:],
                                 f=self.first: nc.tensor.matmul(
                                     o, a, r, start=f, stop=last, skip_group_check=True),
                                 after=[*after, ones_set, consts_set] +
                                 (self.sums_free if self.first else []),
                                 mark=(j == len(self.blocks) - 1))
                    self.first = False
                self.summed = done
                return done

            def finish(self, scale, eps_col, factor=1.0):
                g = self.groups
                slot, root, root_free = small.take()
                parts = [(P, 0, NB * g)]
                if len(self.blocks) > NB:
                    parts.append((META, NB * g, (NB + 1) * g))
                for w, a, b in parts:
                    rooted = act.do(lambda w=w, a=a, b=b: nc.scalar.activation(
                        root[0:w, a:b], psum[0:w, self.sums, a:b], ACT.Sqrt,
                        bias=eps[0:w, eps_col:eps_col + 1], scale=scale),
                        after=[self.summed, consts_set] + root_free)
                for w, a, b in parts:
                    inverse = dve.do(lambda w=w, a=a, b=b: nc.vector.reciprocal(
                        root[0:w, a:b], root[0:w, a:b]), after=[rooted])
                if factor != 1.0:
                    w, a, b = parts[0]
                    inverse = dve.do(lambda: nc.vector.tensor_scalar(
                        root[0:w, a:b], root[0:w, a:b], factor, None, ALU.mult), after=[inverse])
                self.out, out_free = work_banks()
                for j, (c, w) in enumerate(self.blocks):
                    for s in range(g):
                        rows = slice(P // g * s, P // g * (s + 1))
                        lhs = root[0:w, j * g + s:j * g + s + 1].to_broadcast([w, P // g])
                        to = psum[rows, self.out, c - META:c - META + P] if w == P else \
                            psum[rows, self.sums, 64:64 + META]
                        spread = pe.do(lambda o=to, a=lhs, w=w: nc.tensor.matmul(
                            o, a, ident[0:w, 0:w], start=True, stop=True),
                            after=[inverse, ident_loaded, rooted] + out_free)
                small.free[slot] = [spread]
                self.spread = spread
                return psum[:, self.out, :], psum[:, self.sums, 64:64 + META], spread

            def release(self, readers):
                work_release(self.sums, 1, list(readers) + [self.spread])
                work_release(self.out, 1, list(readers) + [self.spread])

        def square_into(stats, tile, cols, after, last, source=None):
            slot, sq, free = squares.take()
            done = act.do(lambda: nc.scalar.activation(
                sq[:, cols], tile if source is None else source, ACT.Square),
                after=list(after) + free)
            squares.free[slot] = [stats.add(sq, [done], last)]
            return done

        def layer_norm_x(g, b, eps_col, z_ready):
            mb, mfree = work_banks()
            for k in range(KT):
                summed = pe.do(lambda k=k: nc.tensor.matmul(
                    bank(mb), ones[:], x[:, k, TOK], start=(k == 0), stop=(k == KT - 1)),
                    after=[z_ready[k], ones_set] + (mfree if k == 0 else []))
            slot, negmean, nfree = scratch.take()
            meaned = act.do(lambda: nc.scalar.mul(negmean[:, TOK], bank(mb), -1.0 / D),
                            after=[summed] + nfree)
            work_release(mb, 1, [meaned])
            stats = Stats(1, False)
            squared = []
            for k in range(KT):
                c = dve.do(lambda k=k: nc.vector.tensor_tensor(
                    x[:, k, TOK], x[:, k, TOK], negmean[:, TOK], ALU.add), after=[meaned])
                squared.append(square_into(stats, x[:, k, TOK], TOK, [c], k == KT - 1))
            scratch.free[slot] = [c]
            main, _, spread = stats.finish(1.0 / D, eps_col)
            for k in range(KT):
                y = dve.do(lambda k=k: nc.vector.scalar_tensor_tensor(
                    x[:, k, TOK], x[:, k, TOK], gain(g, k), main, ALU.mult, ALU.mult),
                    after=[spread, squared[k], gains_loaded])
                shifted = act.do(lambda k=k: nc.scalar.activation(
                    x[:, k, TOK], x[:, k, TOK], ACT.Identity, bias=gain(b, k)), after=[y])
                x_ready[k] = [shifted]
                ready[k] = list(split_into(x_hi[:, k, TOK], x_lo[:, k, TOK], x[:, k, TOK],
                                           after=[shifted, piece_read[-1]]))
            stats.release([y])

        def rms_norm_x(g, x_done):
            stats = Stats(1, True)
            for k in range(KT):
                square_into(stats, x[:, k, :], slice(0, LEN), x_done[k], k == KT - 1)
            main, meta, spread = stats.finish(1.0 / D, 1)
            for k in range(KT):
                slot, y, free = scratch.take()
                dve.do(lambda k=k, y=y: nc.vector.scalar_tensor_tensor(
                    y[:, TOK], x[:, k, TOK], gain(g, k), main, ALU.mult, ALU.mult),
                    after=[spread, *x_done[k]] + free)
                normed = dve.do(lambda k=k, y=y: nc.vector.scalar_tensor_tensor(
                    y[:, MET], x[:, k, MET], gain(g, k), meta, ALU.mult, ALU.mult))
                ready[k] = list(split_into(x_hi[:, k, :], x_lo[:, k, :], y[:],
                                           after=[normed, piece_read[-1]]))
                scratch.free[slot] = ready[k]
            stats.release([normed])

        def ffn(gate, up, down, with_meta, residual):
            with ExitStack() as own:
                tensor = lambda name, shape, dt: own.enter_context(nc.sbuf_tensor(name, shape, dt))
                tag = f"{gate[0]}{gate[1]}"
                lead = META if with_meta else 0
                cols = lead + SEQ
                h_hi = tensor("h_hi_" + tag, [P, FT, cols], F32R)
                h_lo = tensor("h_lo_" + tag, [P, FT, cols], F32R)
                h_ready = [None] * FT
                meta_op = meta_operand_x if with_meta else None
                pending = []
                for f in range(FT):
                    a = project(gate[0], gate[1] + f, KT, tokens_operand, meta_op)
                    u = project(up[0], up[1] + f, KT, tokens_operand, meta_op)
                    slot, hid, hfree = scratch.take()
                    parts = [(slice(lead, cols), psum[:, a[0], :], psum[:, u[0], :])]
                    if with_meta:
                        parts.append((slice(0, META), psum[:, a[2], 0:META],
                                      psum[:, u[2], 0:META]))
                    for c, ga, _ in parts:
                        silu = act.do(lambda h=hid, c=c, ga=ga: nc.scalar.activation(
                            h[:, c], ga, ACT.Silu), after=[a[1]] + hfree)
                    proj_release(a[0], [silu])
                    if with_meta:
                        work_release(a[2], 1, [silu])
                    for c, _, up_ in parts:
                        gated = dve.do(lambda h=hid, c=c, up_=up_: nc.vector.tensor_tensor(
                            h[:, c], h[:, c], up_, ALU.mult), after=[silu, u[1]])
                    proj_release(u[0], [gated])
                    if with_meta:
                        work_release(u[2], 1, [gated])

                    def finish(f=f, slot=slot, hid=hid, gated=gated):
                        h_ready[f] = list(split_into(
                            h_hi[:, f, :], h_lo[:, f, :], hid[:, 0:cols],
                            after=[gated] + region_free))
                        scratch.free[slot] = h_ready[f]
                    for later in pending:
                        later()
                    pending = [finish]
                pending[0]()
                hidden = lambda k: (h_hi[:, k, lead:cols], h_lo[:, k, lead:cols], h_ready[k])
                hidden_meta = (lambda k: (h_hi[:, k, 0:META], h_lo[:, k, 0:META], h_ready[k])) \
                    if with_meta else None
                for m in range(KT):
                    out = project(down[0], down[1] + m, FT, hidden, hidden_meta)
                    residual(m, *out)
            region_ends()

        region_free = []

        def region_ends():
            region_free[:] = [Done(e.sem, e.count) for e in (pe, act, dve, pool) if e.count]

        def residual_tokens(scale):
            z_ready = [None] * KT

            def residual(m, b, done):
                z = dve.do(lambda: nc.vector.scalar_tensor_tensor(
                    x[:, m, TOK], x[:, m, TOK], scale, bank(b), ALU.mult, ALU.add),
                    after=[done, *x_ready[m]])
                proj_release(b, [z])
                z_ready[m] = z
            return residual, z_ready

        def copy_psum(dst, src, after):
            return act.do(lambda: nc.scalar.copy(dst, src), after=after)

        def drive(steps, n):
            for _ in range(n):
                if next(steps, "end") == "end":
                    return

        def transposed(sources, copy_to, after, free):
            b, bfree = work_banks()
            for i, (tile, rows, cols) in enumerate(sources):
                done = pe.do(lambda i=i, a=tile, r=rows, c=cols: nc.tensor.transpose(
                    psum[0:c, b, i * P:i * P + r], a, ident[0:r, 0:r]),
                    after=[*after, ident_loaded] + bfree, mark=i == len(sources) - 1)
            for dst, parts, cols in copy_to:
                copied = copy_psum(dst, psum[parts, b, cols], [done, *free])
            work_release(b, 1, [copied])
            return copied, done

        def mixer_1(layer):
            own = ExitStack()
            tensor = lambda name, shape, dt=F32: own.enter_context(
                nc.sbuf_tensor(f"{name}_{layer}", shape, dt))
            entry = list(region_free)
            tab = tensor("tables", [P, t["tables"].shape[1]])
            tab_loaded = load(pool, f"tables{layer}", tab[:], t["tables"], after=entry)
            table = lambda n: tab[:, t["table_at"][n][0]:t["table_at"][n][1]]
            q_a = tensor("q_a", [P, 4, SEQ])
            k_a = tensor("k_a", [P, SEQ])
            v_a = tensor("v_a", [P, NB, P])
            y_a = tensor("y_a", [P, 4, SEQ])
            y_r = tensor("y_r", [P, 4, SEQ])
            q_r = [tensor(f"q_r{i}", [P, SEQ]) for i in range(2)]
            q_w = [tensor(f"q_w{i}", [P, SEQ]) for i in range(2)]
            k_r = [tensor(f"k_r{i}", [P, SEQ]) for i in range(2)]
            k_w = [tensor(f"k_w{i}", [P, NB, P]) for i in range(2)]
            v_r = [tensor(f"v_r{i}", [P, NB, P]) for i in range(2)]
            gate = [tensor(f"gate{i}", [P, SEQ]) for i in range(2)]
            prob = Slots([tensor(f"prob{i}", [P, 4, 2 * P]) for i in range(3)])
            prob_t = tensor("prob_t", [P, 2, 4 * P])
            state = tensor("state", [P, NB - 1, HD])

            def rotated(b, done, out, rot, cos, sin, scale, free=()):
                slot, raw, rfree = scratch.take()
                copied = copy_psum(raw[:, TOK], bank(b), [done] + rfree)
                proj_release(b, [copied])
                wb, wfree = work_banks()
                turned = pe.do(lambda: nc.tensor.matmul(
                    bank(wb), table(rot), raw[:, TOK], start=True, stop=True),
                    after=[copied, tab_loaded] + wfree)
                slot2, part, pfree = scratch.take()
                times_cos = dve.do(lambda: nc.vector.scalar_tensor_tensor(
                    part[:, TOK], raw[:, TOK], scale, table(cos), ALU.mult, ALU.mult),
                    after=[copied, tab_loaded] + pfree)
                times_sin = dve.do(lambda: nc.vector.scalar_tensor_tensor(
                    out, bank(wb), scale, table(sin), ALU.mult, ALU.mult),
                    after=[turned, *entry, *free])
                work_release(wb, 1, [times_sin])
                scratch.free[slot] = [times_cos, turned]
                rot_done = dve.do(lambda: nc.vector.tensor_tensor(
                    out, out, part[:, TOK], ALU.add), after=[times_cos, times_sin])
                scratch.free[slot2] = [rot_done]
                return rot_done

            def token_major(b, done, out, free=()):
                slot, raw, rfree = scratch.take()
                copied = copy_psum(raw[:, TOK], bank(b), [done] + rfree)
                proj_release(b, [copied])
                turned, read = transposed(
                    [(raw[:, META + n * P:META + (n + 1) * P], P, P) for n in range(NB)],
                    [(out[:].rearrange("p n f -> p (n f)"), slice(0, P), slice(0, SEQ))],
                    [copied], [*entry, *free])
                scratch.free[slot] = [read]
                return turned

            att = {}

            def attention_scores(n, g):
                rows = slice(HD * g, HD * (g + 1))
                k0 = max(n - 1, 0) * P
                width = (n + 1) * P - k0
                band = table("band")[:, 2 * P - width:].unsqueeze(1).to_broadcast([P, 4, width])
                b, bfree = work_banks(2)
                for j in range(4):
                    out = psum[:, b + j // 2, (j % 2) * 256:(j % 2) * 256 + width]
                    done = pe.do(lambda o=out, j=j: nc.tensor.matmul(
                        o, q_a[rows, j, n * P:(n + 1) * P], k_a[rows, k0:k0 + width],
                        start=True, stop=True), after=[*att["q"], att["k"]] + bfree)
                scores = psum[:, b:b + 2, :].rearrange("p b (j k) -> p (b j) k", j=2)[:, :, 0:width]
                slot, s, sfree = prob.take()
                s = s[:, :, 0:width]
                masked = dve.do(lambda: nc.vector.scalar_tensor_tensor(
                    s, scores, HD ** -0.5, band, ALU.mult, ALU.add),
                    after=[done, tab_loaded, *entry] + sfree)
                work_release(b, 2, [masked])
                st_slot, st, st_free = small.take()
                top = dve.do(lambda: nc.vector.tensor_reduce(st[:, 0:4], s, AX.X, ALU.max),
                             after=[masked] + st_free)
                sink = gains[:, gain_at[f"sinks{layer}"] + 4 * g:][:, 0:4]
                top = dve.do(lambda: nc.vector.tensor_tensor(
                    st[:, 0:4], st[:, 0:4], sink, ALU.max), after=[top])
                neg = dve.do(lambda: nc.vector.tensor_scalar(
                    st[:, 0:4], st[:, 0:4], -1.0, None, ALU.mult), after=[top])
                sink_in = dve.do(lambda: nc.vector.tensor_tensor(
                    st[:, 4:8], sink, st[:, 0:4], ALU.add), after=[neg])
                for j in range(4):
                    act.do(lambda j=j: nc.scalar.activation(
                        s[:, j, :], s[:, j, :], ACT.Exp, bias=st[:, j:j + 1],
                        accum_out=st[:, 8 + j:9 + j]), after=[neg])
                exps = act.do(lambda: nc.scalar.activation(
                    st[:, 4:8], st[:, 4:8], ACT.Exp), after=[sink_in])
                total = dve.do(lambda: nc.vector.tensor_tensor(
                    st[:, 8:12], st[:, 8:12], st[:, 4:8], ALU.add), after=[exps])
                inverse = dve.do(lambda: nc.vector.reciprocal(st[:, 8:12], st[:, 8:12]),
                                 after=[total])
                normed = dve.do(lambda: nc.vector.tensor_tensor(
                    s, s, st[:, 8:12].unsqueeze(2).to_broadcast([P, 4, width]), ALU.mult),
                    after=[inverse])
                small.free[st_slot] = [normed]
                return n, g, slot, s, width, normed

            def attention_values(n, g, slot, s, width, normed):
                rows = slice(HD * g, HD * (g + 1))
                for kb in range(width // P):
                    copied, read = transposed(
                        [(s[:, j, kb * P:(kb + 1) * P], P, P) for j in range(4)],
                        [(prob_t[:, kb, :], slice(0, P), slice(0, SEQ))],
                        [normed], [*entry, *att["prob_t_free"]])
                prob.free[slot] = [read]
                b, bfree = work_banks()
                for kb in range(width // P):
                    token_block = n + 1 - width // P + kb
                    done = pe.do(lambda kb=kb, tb=token_block: nc.tensor.matmul(
                        psum[rows, b, :], v_a[:, tb, rows], prob_t[:, kb, :],
                        start=kb == 0, stop=kb == width // P - 1),
                        after=[copied, att["v"]] + bfree)
                att["prob_t_free"] = [done]
                out = act.do(lambda: nc.scalar.copy(
                    y_a[rows, :, n * P:(n + 1) * P],
                    psum[rows, b, :].rearrange("p (j q) -> p j q", j=4)), after=[done, *entry])
                work_release(b, 1, [out])
                att["out"] = out

            def attention():
                att["prob_t_free"] = []
                waiting = None
                for n in range(NB):
                    for g in range(2):
                        this = attention_scores(n, g)
                        yield
                        if waiting:
                            attention_values(*waiting)
                            yield
                        waiting = this
                attention_values(*waiting)
                yield

            ret_out = [None] * 4
            ret_free = [[], []]

            def retention(j, i, q_done, kw_done, k_done, v_done, gate_done):
                b, bfree = work_banks(2)
                for n in range(NB):
                    for s in range(2):
                        rows, cols = slice(HD * s, HD * (s + 1)), slice(n * P, (n + 1) * P)
                        scored = pe.do(lambda n=n, s=s, rows=rows, cols=cols: nc.tensor.matmul(
                            psum[:, b + s, cols],
                            k_r[i][rows, cols], q_r[i][rows, cols], start=True, stop=True),
                            after=[q_done, k_done] + bfree, mark=(n, s) == (NB - 1, 1))
                slot, sc, sfree = prob.take()
                decay = table("decay")[:, 2 * j * P:2 * (j + 1) * P].rearrange(
                    "p (s i) -> p s i", s=2).unsqueeze(2).to_broadcast([P, 2, NB, P])
                sc = sc[:].rearrange("p a b -> p (a b)").rearrange(
                    "p (s n i) -> p s n i", s=2, n=NB)
                decayed = dve.do(lambda: nc.vector.tensor_tensor(
                    sc, psum[:, b:b + 2, :].rearrange("p s (n i) -> p s n i", n=NB), decay,
                    ALU.mult), after=[scored, tab_loaded, *entry] + sfree)
                work_release(b, 2, [decayed])
                yield
                b2, b2free = work_banks()
                for n in range(NB - 1):
                    for s in range(2):
                        rows = slice(HD * s, HD * (s + 1))
                        added = pe.do(lambda n=n, rows=rows: nc.tensor.matmul(
                            psum[rows, b2, n * HD:(n + 1) * HD], k_w[i][:, n, rows],
                            v_r[i][:, n, rows], start=True, stop=True),
                            after=[kw_done, v_done] + b2free, mark=(n, s) == (NB - 2, 1))
                before = dve.do(lambda: nc.vector.tensor_copy(
                    state[:, 0, :], psum[:, b2, 0:HD]), after=[added, *ret_state_free, *entry])
                g_col = table("g_chunk")[:, j:j + 1]
                for n in range(1, NB - 1):
                    before = dve.do(lambda n=n: nc.vector.scalar_tensor_tensor(
                        state[:, n, :], state[:, n - 1, :], g_col,
                        psum[:, b2, n * HD:(n + 1) * HD], ALU.mult, ALU.add), after=[before])
                work_release(b2, 1, [before])
                yield
                b3, b3free = work_banks()
                for n in range(NB):
                    cols = slice(n * P, (n + 1) * P)
                    for s in range(2):
                        rows = slice(HD * s, HD * (s + 1))
                        out = pe.do(lambda n=n, s=s, rows=rows, cols=cols: nc.tensor.matmul(
                            psum[rows, b3, cols], v_r[i][:, n, rows],
                            sc[:, s, n, :], start=True, stop=n == 0,
                            skip_group_check=True),
                            after=[decayed, v_done] + b3free, mark=n == 0)
                        if n:
                            out = pe.do(lambda n=n, rows=rows, cols=cols: nc.tensor.matmul(
                                psum[rows, b3, cols], state[rows, n - 1, :],
                                q_w[i][rows, cols], start=False, stop=True,
                                skip_group_check=True), after=[before])
                prob.free[slot] = [out]
                ret_state_free[:] = [out]
                yield
                oslot, o, ofree = scratch.take()
                copied = copy_psum(o[:, TOK], bank(b3), [out] + ofree)
                work_release(b3, 1, [copied])
                b4, b4free = work_banks()
                summed = pe.do(lambda: nc.tensor.matmul(
                    bank(b4), half[:], o[:, TOK], start=True, stop=True),
                    after=[copied, half_loaded] + b4free)
                centred = dve.do(lambda: nc.vector.scalar_tensor_tensor(
                    o[:, TOK], bank(b4), -1.0 / HD, o[:, TOK], ALU.mult, ALU.add),
                    after=[summed])
                work_release(b4, 1, [centred])
                stats = Stats(2, False)
                square_into(stats, o[:, TOK], TOK, [centred], True)
                yield
                main, _, spread = stats.finish(1.0 / HD, 1)
                normed = dve.do(lambda: nc.vector.tensor_tensor(
                    o[:, TOK], o[:, TOK], main, ALU.mult), after=[spread])
                stats.release([normed])
                ret_out[j] = dve.do(lambda: nc.vector.tensor_tensor(
                    y_r[:, j, :], o[:, TOK], gate[i][:], ALU.mult),
                    after=[normed, gate_done, *entry])
                scratch.free[oslot] = [ret_out[j]]
                ret_free[i] = [ret_out[j]]
                yield

            ret_state_free = []
            first = layer * IN_TILES_1
            at = [first]

            def next_tile():
                out = project("w_in", at[0], KT, tokens_operand)
                at[0] += 1
                return out

            att["q"] = []
            for j in range(4):
                b, done = next_tile()
                att["q"].append(rotated(b, done, q_a[:, j, :], "rot_a", "cos_a", "sin_a", 1.0))
            b, done = next_tile()
            att["k"] = rotated(b, done, k_a[:], "rot_a", "cos_a", "sin_a", 1.0)
            b, done = next_tile()
            att["v"] = token_major(b, done, v_a)
            steps = attention()
            ret_steps = iter(())
            for j in range(4):
                i = j % 2
                free = ret_free[i]
                drive(steps, 1)
                b, done = next_tile()
                q_done = rotated(b, done, q_r[i][:], "rot_r", "cos_r", "sin_r", 1.0, free)
                weighted = dve.do(lambda i=i, j=j: nc.vector.tensor_tensor(
                    q_w[i][:].rearrange("p (n c) -> p n c", n=NB),
                    q_r[i][:].rearrange("p (n c) -> p n c", n=NB),
                    table("w_q")[:, j * P:(j + 1) * P].unsqueeze(1).to_broadcast([P, NB, P]),
                    ALU.mult), after=[q_done])
                drive(ret_steps, 2)
                drive(steps, 1)
                b, done = next_tile()
                k_done = rotated(b, done, k_r[i][:], "rot_r", "cos_r", "sin_r", HD ** -0.5, free)
                drive(ret_steps, 2)
                drive(steps, 1)
                b, done = next_tile()
                v_done = token_major(b, done, v_r[i], free)
                wb, wfree = work_banks()
                for n in range(NB):
                    turned = pe.do(lambda n=n, i=i: nc.tensor.transpose(
                        psum[:, wb, n * P:(n + 1) * P], k_r[i][:, n * P:(n + 1) * P], ident[:]),
                        after=[k_done] + wfree)
                kw_done = dve.do(lambda i=i, j=j, wb=wb: nc.vector.tensor_tensor(
                    k_w[i][:], bank(wb).rearrange("p (n d) -> p n d", n=NB),
                    table("w_k")[:, j * P:(j + 1) * P].unsqueeze(1).to_broadcast([P, NB, P]),
                    ALU.mult), after=[turned, *entry, *free])
                work_release(wb, 1, [kw_done])
                drive(ret_steps, 2)
                drive(steps, 1)
                b, done = next_tile()
                gate_done = act.do(lambda i=i, b=b: nc.scalar.activation(
                    gate[i][:], bank(b), ACT.Silu), after=[done, *entry, *free])
                proj_release(b, [gate_done])
                drive(ret_steps, 9)
                ret_steps = retention(j, i, weighted, kw_done, k_done, v_done, gate_done)
            drive(steps, 99)
            read = piece_read[-1]
            y_ready = [None] * KT
            for j in range(4):
                y_ready[j] = list(split_into(x_hi[:, j, TOK], x_lo[:, j, TOK], y_a[:, j, :],
                                             after=[att["out"], read]))
            drive(ret_steps, 9)
            for j in range(4):
                y_ready[4 + j] = list(split_into(
                    x_hi[:, 4 + j, TOK], x_lo[:, 4 + j, TOK], y_r[:, j, :],
                    after=[ret_out[j], read]))
            operand = lambda k: (x_hi[:, k, TOK], x_lo[:, k, TOK], y_ready[k])
            residual, z_ready = residual_tokens(ALPHA)
            for m in range(KT):
                residual(m, *project("w_out", layer * KT + m, KT, operand))
            own.close()
            region_ends()
            layer_norm_x(f"ln2_g{layer}", f"ln2_b{layer}", 0, z_ready)

        def both(f, after):
            return [f(TOK, after), f(MET, after)]

        def residual_both(x_done):
            def residual(m, b, done, meta_b):
                z = dve.do(lambda: nc.vector.scalar_tensor_tensor(
                    x[:, m, TOK], bank(b), 0.5, x[:, m, TOK], ALU.mult, ALU.add),
                    after=[done, *x_done[m]])
                zm = dve.do(lambda: nc.vector.scalar_tensor_tensor(
                    x[:, m, MET], psum[:, meta_b, 0:META], 0.5, x[:, m, MET],
                    ALU.mult, ALU.add))
                proj_release(b, [z])
                work_release(meta_b, 1, [zm])
                x_done[m] = [zm]
            return residual

        def mixer_2(x_done):
            own = ExitStack()
            tensor = lambda name, shape, dt=F32: own.enter_context(
                nc.sbuf_tensor("b2_" + name, shape, dt))
            entry = list(region_free)
            q_a = tensor("q_a", [P, A_HEADS, SEQ])
            k_a = tensor("k_a", [P, A_HEADS, LEN])
            v_a = tensor("v_a", [P, NB, A_HEADS, P])
            v_a_meta = tensor("v_a_meta", [META, A_HEADS, P])
            q_lat = tensor("q_lat", [P, B_HEADS, 2, SEQ])
            c_fm = tensor("c_fm", [P, 2, LEN])
            c_tm = tensor("c_tm", [P, NB, B_DC])
            c_tm_meta = tensor("c_tm_meta", [META, B_DC])
            q_i = tensor("q_i", [P, 4, SEQ])
            k_i = tensor("k_i", [P, LEN])
            w_i = tensor("w_i", [P, NB, IDX_HEADS])
            w_uk = tensor("w_uk", [P, B_HEADS * B_DC])
            w_uv = tensor("w_uv", [P, B_HEADS, 2, P])
            window = tensor("window", [P, A_HEADS + B_HEADS, WINDOW_2])
            rank = tensor("rank", [P, LEN])
            keep_at = [sum(META + P * (i + 1) for i in range(b)) for b in range(NB + 1)]
            keep = tensor("keep", [P, keep_at[NB]])
            attn_t = Slots([tensor(f"attn_t{i}", [P, NB + 1, P]) for i in range(2)])
            lat = tensor("lat", [P, 2, P])
            lam = tensor("lam", [P, 8])
            exps = Slots([tensor(f"exp{i}", [P, LEN]) for i in range(3)])

            hot = exps.bufs[0][0:BUCKETS, 0:REL_N]
            table = exps.bufs[1][0:BUCKETS, 0:8]
            cut = exps.bufs[2][0:8, 0:REL_N]
            rows = rank[0:8, 0:REL_N]
            hot_loaded = load(pool, "hot", hot, t["distance_hot"], after=entry)
            bias_loaded = load(pool, "rel_bias", table, t["rel_bias"])
            cut_loaded = load(pool, "cut", cut, t["distance_mask"])
            uk_loaded = load(pool, "w_uk", w_uk[:], t["w_uk"])
            uv_loaded = load(pool, "w_uv", w_uv[:].rearrange("p h k d -> p (h k d)"), t["w_uv"])
            b, free = work_banks()
            looked = pe.do(lambda: nc.tensor.matmul(
                psum[0:8, b, 0:REL_N], table, hot, start=True, stop=True),
                after=[hot_loaded, bias_loaded] + free)
            far = dve.do(lambda: nc.vector.tensor_copy(lam[0:8, 0:1], psum[0:8, b, 0:1]),
                         after=[looked, *entry])
            relative = dve.do(lambda: nc.vector.tensor_scalar(
                rows, psum[0:8, b, 0:REL_N], lam[0:8, 0:1], None, ALU.subtract), after=[far])
            work_release(b, 1, [relative])
            causal = dve.do(lambda: nc.vector.tensor_tensor(rows, rows, cut, ALU.add),
                            after=[relative, cut_loaded])
            rows_stored = load(pool, "rows_stored", t["bias_rows"], rows, after=[causal])
            heads = A_HEADS + B_HEADS
            mirrored = q_lat[:].rearrange("p h k n -> p (h k n)")[:, 0:heads * WINDOW_2]
            mirrored_in = [load(pool, f"mirrored{h}", mirrored[:, h * WINDOW_2:(h + 1) * WINDOW_2],
                                bass.AP(t["bias_rows"].tensor, h * REL_N,
                                        [[1, P], [1, WINDOW_2]]),
                                after=[rows_stored]) for h in range(heads)]
            flip_loaded = load(pool, "flip", lat[:, 0, :], t["flip"])
            for h in range(0, heads, 2):
                b, free = work_banks()
                turned = pe.do(lambda: nc.tensor.matmul(
                    bank(b), lat[:, 0, :], mirrored[:, h * WINDOW_2:(h + 2) * WINDOW_2],
                    start=True, stop=True), after=[*mirrored_in[h:h + 2], flip_loaded] + free)
                window_done = copy_psum(window[:, h:h + 2, :].rearrange("p h j -> p (h j)"),
                                        bank(b), [turned, *entry])
                work_release(b, 1, [window_done])
            window_turned = turned

            g0 = gain_at["lambda_q1"]
            multiplied = dve.do(lambda: nc.vector.tensor_tensor(
                lam[0:HD, 2:4], gains[0:HD, g0:g0 + 3:2], gains[0:HD, g0 + 1:g0 + 4:2],
                ALU.mult), after=[relative])
            b, free = work_banks()
            dotted = pe.do(lambda: nc.tensor.matmul(
                psum[:, b, 0:2], ones[0:HD, :], lam[0:HD, 2:4], start=True, stop=True),
                after=[multiplied] + free)
            exped = act.do(lambda: nc.scalar.activation(lam[:, 4:6], psum[:, b, 0:2], ACT.Exp),
                           after=[dotted])
            work_release(b, 1, [exped])
            lam_done = dve.do(lambda: nc.vector.tensor_tensor(
                lam[:, 6:7], lam[:, 5:6], lam[:, 4:5], ALU.subtract), after=[exped])
            lam_done = dve.do(lambda: nc.vector.tensor_scalar(
                lam[:, 6:7], lam[:, 6:7], LAM_INIT, None, ALU.subtract), after=[lam_done])
            exps_free = [looked, causal]
            for i in range(3):
                exps.free[i] = exps_free

            at = [0]

            def next_tile(meta):
                out = project("b2_in", at[0], KT, tokens_operand,
                              meta_operand_x if meta else None)
                at[0] += 1
                return out

            def evacuate(dst, out, free=()):
                after = [out[1], *entry, *free]
                main = copy_psum(dst[:, TOK] if len(out) == 3 else dst, bank(out[0]), after)
                proj_release(out[0], [main])
                if len(out) == 3:
                    main = copy_psum(dst[:, MET], psum[:, out[2], 0:META], after)
                    work_release(out[2], 1, [main])
                return main

            def normalise(dst, stats_main, stats_meta, g, spread):
                meta = stats_meta is not None
                cols = TOK if meta else slice(0, SEQ)
                done = dve.do(lambda: nc.vector.scalar_tensor_tensor(
                    dst[:, cols], dst[:, cols], g, stats_main, ALU.mult, ALU.mult),
                    after=[spread])
                if meta:
                    done = dve.do(lambda: nc.vector.scalar_tensor_tensor(
                        dst[:, MET], dst[:, MET], g, stats_meta, ALU.mult, ALU.mult))
                return done

            q_i_done, kept = [None] * 4, [None] * NB

            def keys(b):
                return META + P * (b + 1)

            def bank_parts(n):
                return [(0, min(n, 512))] + ([(512, n)] if n > 512 else [])

            def two_banks(b, n):
                return psum[:, b:b + 2, :].rearrange("p b n -> p (b n)")[:, 0:n] if n > 512 \
                    else psum[:, b, 0:n]

            def indexer(b):
                n = keys(b)
                width = 2 if n > 512 else 1
                own_cols = slice(n - P, n)
                acc = None
                for h in range(IDX_HEADS):
                    rows = slice(HD * (h % 2), HD * (h % 2 + 1))
                    wb, free = work_banks(width)
                    for c0, c1 in bank_parts(n):
                        dots = pe.do(lambda: nc.tensor.matmul(
                            psum[:, wb + c0 // 512, 0:c1 - c0],
                            q_i[rows, h // 2, b * P:(b + 1) * P], k_i[rows, c0:c1],
                            start=True, stop=True), after=[q_i_done[h // 2], k_i_done[0]] + free)
                    slot, pos, pfree = scratch.take()
                    positive = act.do(lambda: nc.scalar.activation(
                        pos[:, 0:n], two_banks(wb, n), ACT.Relu, scale=HD ** -0.5),
                        after=[dots] + pfree)
                    work_release(wb, width, [positive])
                    weight = w_i[:, b, h:h + 1]
                    if h == 0:
                        acc = dve.do(lambda: nc.vector.tensor_scalar(
                            rank[:, 0:n], pos[:, 0:n], weight, None, ALU.mult),
                            after=[positive, w_i_done[0], rows_stored, kept[b - 1][1] if b else None])
                    else:
                        acc = dve.do(lambda: nc.vector.scalar_tensor_tensor(
                            rank[:, 0:n], pos[:, 0:n], weight, rank[:, 0:n],
                            ALU.mult, ALU.add), after=[positive, acc])
                    scratch.free[slot] = [acc]
                    yield
                acc = dve.do(lambda: nc.vector.tensor_tensor(
                    rank[:, own_cols], rank[:, own_cols], edge[:], ALU.add),
                    after=[acc, edge_done])
                slot, best, bfree = small.take()
                for _ in range(TOPK // 8):
                    found = dve.do(lambda: nc.vector.max(best[:, 0:8], rank[:, 0:n]),
                                   after=[acc] + bfree)
                    acc = dve.do(lambda: nc.vector.match_replace(
                        rank[:, 0:n], best[:, 0:8], rank[:, 0:n], -2.0 * BIG), after=[found])
                    yield
                small.free[slot] = [acc]
                kp = keep[:, keep_at[b]:keep_at[b + 1]]
                done = dve.do(lambda: nc.vector.tensor_scalar(
                    kp, rank[:, 0:n], -2.0 * BIG, -BIG, ALU.not_equal, ALU.mult),
                    after=[acc, *entry])
                kept[b] = (kp, done)
                yield

            def weights_t(tile, n, after):
                slot, out, free = attn_t.take()
                blocks = (n - META) // P
                sources = [(tile[:, META + P * j:META + P * (j + 1)], P, P)
                           for j in range(blocks)]
                meta_in = (tile[:, MET], P, META)
                if blocks < 4:
                    copied, read = transposed(
                        sources + [meta_in],
                        [(out[:, 0:blocks, :].rearrange("p n q -> p (n q)"), slice(0, P),
                          slice(0, blocks * P)),
                         (out[0:META, NB, :], slice(0, META),
                          slice(blocks * P, (blocks + 1) * P))], after, [*entry, *free])
                else:
                    transposed(sources, [(out[:, 0:blocks, :].rearrange("p n q -> p (n q)"),
                                          slice(0, P), slice(0, blocks * P))],
                               after, [*entry, *free])
                    copied, read = transposed([meta_in], [(out[0:META, NB, :], slice(0, META),
                                                           slice(0, P))], after, [])
                return slot, out, copied, read

            def softmax(s, n, ready_):
                slot, st, free = small.take()
                top = dve.do(lambda: nc.vector.tensor_reduce(
                    st[:, 0:1], s[:, 0:n], AX.X, ALU.max), after=[ready_] + free)
                neg = dve.do(lambda: nc.vector.tensor_scalar(
                    st[:, 0:1], st[:, 0:1], -1.0, None, ALU.mult), after=[top])
                exped = act.do(lambda: nc.scalar.activation(
                    s[:, 0:n], s[:, 0:n], ACT.Exp, bias=st[:, 0:1], accum_out=st[:, 1:2]),
                    after=[neg])
                inverse = dve.do(lambda: nc.vector.reciprocal(st[:, 1:2], st[:, 1:2]),
                                 after=[exped])
                return slot, st, inverse

            def latent_attention_scores(b, h):
                n = keys(b)
                width = 2 if n > 512 else 1
                w0 = max(n - WINDOW_2, 0)
                kp, kdone = kept[b]
                wb, free = work_banks(width)
                for c0, c1 in bank_parts(n):
                    for k in range(2):
                        done = pe.do(lambda: nc.tensor.matmul(
                            psum[:, wb + c0 // 512, 0:c1 - c0],
                            q_lat[:, h, k, b * P:(b + 1) * P], c_fm[:, k, c0:c1],
                            start=k == 0, stop=k == 1), after=[q_lat_done[h], c_done[0]] + free)
                slot, s, sfree = exps.take()
                masked = dve.do(lambda: nc.vector.scalar_tensor_tensor(
                    s[:, 0:n], two_banks(wb, n), B_DC ** -0.5, kp, ALU.mult, ALU.add),
                    after=[done, kdone] + sfree)
                work_release(wb, width, [masked])
                biased = dve.do(lambda: nc.vector.tensor_tensor(
                    s[:, w0:n], s[:, w0:n], window[:, A_HEADS + h, WINDOW_2 - (n - w0):],
                    ALU.add), after=[masked, window_done])
                st_slot, st, inverse = softmax(s, n, biased)
                normed = dve.do(lambda: nc.vector.tensor_scalar(
                    s[:, 0:n], s[:, 0:n], st[:, 1:2], None, ALU.mult), after=[inverse])
                small.free[st_slot] = [normed]
                return b, h, slot, s, normed

            def latent_attention_values(b, h, slot, s, normed):
                n = keys(b)
                blocks = (n - META) // P
                aslot, a_t, copied, read = weights_t(s, n, [normed])
                exps.free[slot] = [read]
                wb, free = work_banks()
                for k in range(2):
                    cols = slice(k * P, (k + 1) * P)
                    for j in range(blocks):
                        pe.do(lambda: nc.tensor.matmul(
                            psum[:, wb, cols], c_tm[:, j, cols], a_t[:, j, :],
                            start=j == 0, stop=False), after=[copied, c_tm_done[0]] + free,
                            mark=False)
                    done = pe.do(lambda: nc.tensor.matmul(
                        psum[:, wb, cols], c_tm_meta[:, cols], a_t[0:META, NB, :],
                        start=False, stop=True))
                attn_t.free[aslot] = [done]
                latent = copy_psum(lat[:].rearrange("p k q -> p (k q)"), psum[:, wb, 0:2 * P],
                                   [done, *entry, *lat_free])
                for k in range(2):
                    done = pe.do(lambda: nc.tensor.matmul(
                        psum[:, wb, 2 * P:3 * P], w_uv[:, h, k, :], lat[:, k, :],
                        start=k == 0, stop=k == 1), after=[latent, uv_loaded])
                lat_free[:] = [done]
                out = copy_psum(q_i[:, h, b * P:(b + 1) * P], psum[:, wb, 2 * P:3 * P],
                                [done, kept[b][1]])
                work_release(wb, 1, [out])
                y_b_done[h] = out

            def differential_scores(b, h):
                n = keys(b)
                width = 2 if n > 512 else 1
                w0 = max(n - WINDOW_2, 0)
                maps = []
                for m in range(2):
                    rows = slice(HD * m, HD * (m + 1))
                    wb, free = work_banks(width)
                    for c0, c1 in bank_parts(n):
                        done = pe.do(lambda: nc.tensor.matmul(
                            psum[:, wb + c0 // 512, 0:c1 - c0],
                            q_a[rows, h, b * P:(b + 1) * P], k_a[rows, h, c0:c1],
                            start=True, stop=True), after=[q_a_done[h], k_a_done[h]] + free)
                    slot, s, sfree = exps.take()
                    view = two_banks(wb, n)
                    if w0:
                        act.do(lambda: nc.scalar.mul(s[:, 0:w0], view[:, 0:w0], HD ** -0.5),
                               after=[done] + sfree)
                    far_ = Done(act.sem, act.count) if w0 else None
                    biased = dve.do(lambda: nc.vector.scalar_tensor_tensor(
                        s[:, w0:n], view[:, w0:n], HD ** -0.5,
                        window[:, h, WINDOW_2 - (n - w0):], ALU.mult, ALU.add),
                        after=[done, far_, window_done] + sfree)
                    work_release(wb, width, [biased])
                    st_slot, st, inverse = softmax(s, n, biased)
                    maps.append((slot, s, st_slot, st, inverse))
                (slot0, s0, stslot0, st0, inv0), (slot1, s1, stslot1, st1, inv1) = maps
                factor = dve.do(lambda: nc.vector.tensor_tensor(
                    st1[:, 1:2], st1[:, 1:2], lam[:, 6:7], ALU.mult), after=[inv1, lam_done])
                second = dve.do(lambda: nc.vector.tensor_scalar(
                    s1[:, 0:n], s1[:, 0:n], st1[:, 1:2], None, ALU.mult), after=[factor])
                both_ = dve.do(lambda: nc.vector.scalar_tensor_tensor(
                    s0[:, 0:n], s0[:, 0:n], st0[:, 1:2], s1[:, 0:n], ALU.mult, ALU.add),
                    after=[inv0, second])
                small.free[stslot0] = small.free[stslot1] = [both_]
                exps.free[slot1] = [both_]
                return b, h, slot0, s0, both_

            def differential_values(b, h, slot, s, normed):
                n = keys(b)
                blocks = (n - META) // P
                aslot, a_t, copied, read = weights_t(s, n, [normed])
                exps.free[slot] = [read]
                wb, free = work_banks()
                for j in range(blocks):
                    pe.do(lambda: nc.tensor.matmul(
                        psum[:, wb, 0:P], v_a[:, j, h, :], a_t[:, j, :],
                        start=j == 0, stop=False), after=[copied, v_a_done[h]] + free,
                        mark=False)
                done = pe.do(lambda: nc.tensor.matmul(
                    psum[:, wb, 0:P], v_a_meta[:, h, :], a_t[0:META, NB, :],
                    start=False, stop=True))
                attn_t.free[aslot] = [done]
                out = copy_psum(q_a[:, h, b * P:(b + 1) * P], psum[:, wb, 0:P], [done])
                work_release(wb, 1, [out])
                y_a_done[h] = out

            def attention_steps(scores, values, order):
                waiting = None
                for b, h in order:
                    this = scores(b, h)
                    yield
                    if waiting:
                        values(*waiting)
                        yield
                    waiting = this
                values(*waiting)
                yield

            edge = tensor("edge", [P, P])
            edge_done = load(pool, "edge", edge[:], t["tables"][:, t["table_at"]["band"][0] + P:
                                                               t["table_at"]["band"][1]])
            k_i_done, w_i_done, c_done, c_tm_done = [None], [None], [None], [None]
            q_lat_done, q_a_done, k_a_done, v_a_done = ([None] * 4 for _ in range(4))
            y_a_done, y_b_done, lat_free = [None] * 4, [None] * 4, [window_turned]

            for j in range(4):
                q_i_done[j] = evacuate(q_i[:, j, :], next_tile(False))
            k_i_done[0] = evacuate(k_i[:], next_tile(True))
            out = next_tile(False)
            slot, raw, free = scratch.take()
            copied = evacuate(raw[:, 0:SEQ], out, free)
            wb, wfree = work_banks()
            for j in range(NB):
                turned = pe.do(lambda: nc.tensor.transpose(
                    psum[:, wb, j * IDX_HEADS:(j + 1) * IDX_HEADS],
                    raw[0:IDX_HEADS, j * P:(j + 1) * P], ident[0:IDX_HEADS, 0:IDX_HEADS]),
                    after=[copied] + wfree)
            scratch.free[slot] = [turned]
            w_i_done[0] = act.do(lambda: nc.scalar.mul(
                w_i[:].rearrange("p n h -> p (n h)"), psum[:, wb, 0:NB * IDX_HEADS],
                IDX_HEADS ** -0.5), after=[turned, *entry])
            work_release(wb, 1, [w_i_done[0]])

            def selection():
                for b in range(NB):
                    yield from indexer(b)

            steps = selection()
            stats = Stats(1, True)
            for k in range(2):
                copied = evacuate(c_fm[:, k, :], next_tile(True))
                square_into(stats, c_fm[:, k, :], slice(0, LEN), [copied], k == 1)
                drive(steps, 3)
            main, meta, spread = stats.finish(1.0 / B_DC, 1)
            for k in range(2):
                done = normalise(c_fm[:, k, :], main, meta, gain("b_kv_norm", k), spread)
            stats.release([done])
            c_done[0] = done
            for k in range(2):
                cols = slice(k * P, (k + 1) * P)
                transposed([(c_fm[:, k, META + P * j:META + P * (j + 1)], P, P)
                            for j in range(NB)],
                           [(c_tm[:, :, cols], slice(0, P), slice(0, SEQ))],
                           [done], entry)
                c_tm_done[0], _ = transposed([(c_fm[:, k, MET], P, META)],
                                             [(c_tm_meta[:, cols], slice(0, META),
                                               slice(0, P))], [done], entry)
            for h in range(B_HEADS):
                out = next_tile(False)
                slot, raw, free = scratch.take()
                copied = evacuate(raw[:, 0:SEQ], out, free)
                stats = Stats(1, False)
                for k in range(2):
                    wb, wfree = work_banks()
                    made = pe.do(lambda: nc.tensor.matmul(
                        bank(wb), w_uk[:, h * B_DC + k * P:h * B_DC + (k + 1) * P],
                        raw[:, 0:SEQ], start=True, stop=True), after=[copied, uk_loaded] + wfree)
                    moved = copy_psum(q_lat[:, h, k, :], bank(wb), [made, window_turned, *entry])
                    work_release(wb, 1, [moved])
                    square_into(stats, q_lat[:, h, k, :], TOK, [moved], k == 1)
                scratch.free[slot] = [made]
                drive(steps, 3)
                main, _, spread = stats.finish(1.0 / B_DC, 1)
                for k in range(2):
                    done = normalise(q_lat[:, h, k, :], main, None, gain("b_q_norm", k), spread)
                stats.release([done])
                q_lat_done[h] = done
                drive(steps, 2)
            for h in range(A_HEADS):
                out = next_tile(False)
                copied = evacuate(q_a[:, h, :], out)
                stats = Stats(2, False)
                square_into(stats, q_a[:, h, :], TOK, [copied], True)
                main, _, spread = stats.finish(1.0 / HD, 1)
                q_a_done[h] = normalise(q_a[:, h, :], main, None, gain("a_q_norm"), spread)
                stats.release([q_a_done[h]])
                drive(steps, 6)
            for h in range(A_HEADS):
                out = next_tile(True)
                copied = evacuate(k_a[:, h, :], out)
                stats = Stats(2, True)
                square_into(stats, k_a[:, h, :], slice(0, LEN), [copied], True)
                main, meta, spread = stats.finish(1.0 / HD, 1)
                k_a_done[h] = normalise(k_a[:, h, :], main, meta, gain("a_k_norm"), spread)
                stats.release([k_a_done[h]])
                drive(steps, 6)
            for h in range(A_HEADS):
                out = next_tile(True)
                slot, raw, free = scratch.take()
                copied = evacuate(raw, out, free)
                transposed([(raw[:, META + P * j:META + P * (j + 1)], P, P) for j in range(NB)],
                           [(v_a[:, :, h, :], slice(0, P), slice(0, SEQ))],
                           [copied], entry)
                v_a_done[h], read = transposed([(raw[:, MET], P, META)],
                                               [(v_a_meta[:, h, :], slice(0, META),
                                                 slice(0, P))], [copied], entry)
                scratch.free[slot] = [read]
                drive(steps, 6)

            order = [(b, h) for b in range(NB) for h in range(4)]
            diff = attention_steps(differential_scores, differential_values, order)
            for _ in diff:
                drive(steps, 3)
            drive(steps, 999)
            drive(attention_steps(latent_attention_scores, latent_attention_values, order), 999)

            read = piece_read[-1]
            y_ready = [None] * KT
            for h in range(A_HEADS):
                stats = Stats(1, False)
                square_into(stats, q_a[:, h, :], TOK, [y_a_done[h]], True)
                main, _, spread = stats.finish(1.0 / P, 1, factor=1.0 - LAM_INIT)
                done = normalise(q_a[:, h, :], main, None, gain("a_subln"), spread)
                stats.release([done])
                y_ready[h] = list(split_into(x_hi[:, h, TOK], x_lo[:, h, TOK], q_a[:, h, :],
                                             after=[done, read]))
            for h in range(B_HEADS):
                y_ready[4 + h] = list(split_into(
                    x_hi[:, 4 + h, TOK], x_lo[:, 4 + h, TOK], q_i[:, h, :],
                    after=[y_b_done[h], read]))
            operand = lambda k: (x_hi[:, k, TOK], x_lo[:, k, TOK], y_ready[k])
            for m in range(KT):
                b, done = project("b2_out", m, KT, operand)
                z = dve.do(lambda: nc.vector.tensor_tensor(
                    x[:, m, TOK], x[:, m, TOK], bank(b), ALU.add), after=[done, *x_done[m]])
                proj_release(b, [z])
                x_done[m] = [z]
            own.close()
            region_ends()

        def block_2():
            x_done = [list(x_ready[k]) + [meta_loaded] for k in range(KT)]
            rms_norm_x("ffn1_norm", x_done)
            ffn(("b2_gate1", 0), ("b2_up1", 0), ("b2_down1", 0), True, residual_both(x_done))
            rms_norm_x("mix_norm", x_done)
            mixer_2(x_done)
            rms_norm_x("ffn2_norm", x_done)

            def residual(m, b, done):
                z = dve.do(lambda: nc.vector.scalar_tensor_tensor(
                    x[:, m, TOK], bank(b), 0.5, x[:, m, TOK], ALU.mult, ALU.add),
                    after=[done, *x_done[m]])
                proj_release(b, [z])
                x_done[m] = [z]
            ffn(("b2_gate2", 0), ("b2_up2", 0), ("b2_down2", 0), False, residual)
            for k in range(KT):
                x_ready[k] = x_done[k]

        for k in range(KT):
            x_ready[k] = [x_loaded]
            ready[k] = list(split_into(x_hi[:, k, TOK], x_lo[:, k, TOK], x[:, k, TOK],
                                       after=[x_loaded]))
        for layer in range(DEPTH):
            residual, z_ready = residual_tokens(2.0 * ALPHA)
            ffn(("ffn1_gu", layer * 2 * FT), ("ffn1_gu", layer * 2 * FT + FT),
                ("ffn1_down", layer * KT), False, residual)
            layer_norm_x(f"ln1_g{layer}", f"ln1_b{layer}", 2, z_ready)
            mixer_1(layer)
            residual, z_ready = residual_tokens(2.0 * ALPHA)
            ffn(("ffn2_gu", layer * 2 * FT), ("ffn2_gu", layer * 2 * FT + FT),
                ("ffn2_down", layer * KT), False, residual)
            layer_norm_x(f"ln3_g{layer}", f"ln3_b{layer}", 2, z_ready)
        block_2()
        out_sem = sem("out_stored")
        for k in range(KT):
            stored = sp.dma(out_sem, 16 * (k + 1), lambda k=k: nc.sync.dma_start(
                t["out"][k * P:(k + 1) * P, :], x[:, k, TOK]), after=x_ready[k])
        sp.wait([stored])



def weight_plan():
    plan = []

    def ffn(gate, up, down):
        for f in range(FT):
            plan.extend(pieces(gate[0], gate[1] + f, KT))
            plan.extend(pieces(up[0], up[1] + f, KT))
        for m in range(KT):
            plan.extend(pieces(down[0], down[1] + m, FT))

    def matrix(name, first, n):
        for m in range(n):
            plan.extend(pieces(name, first + m, KT))

    for layer in range(DEPTH):
        ffn(("ffn1_gu", layer * 2 * FT), ("ffn1_gu", layer * 2 * FT + FT),
            ("ffn1_down", layer * KT))
        matrix("w_in", layer * IN_TILES_1, IN_TILES_1)
        matrix("w_out", layer * KT, KT)
        ffn(("ffn2_gu", layer * 2 * FT), ("ffn2_gu", layer * 2 * FT + FT),
            ("ffn2_down", layer * KT))
    ffn(("b2_gate1", 0), ("b2_up1", 0), ("b2_down1", 0))
    matrix("b2_in", 0, IN_TILES_2)
    matrix("b2_out", 0, KT)
    ffn(("b2_gate2", 0), ("b2_up2", 0), ("b2_down2", 0))
    return plan


def column_tiles(w):
    k, n = w.shape
    return np.ascontiguousarray(
        w.reshape(k // P, P, n // P, P).transpose(2, 1, 0, 3).reshape(n // P, P, k))


def head_pairs(w, axis):
    order = [h for j in range(HEADS // 2) for h in (j, HEADS // 2 + j)]
    shape = w.shape
    w = w.reshape(shape[:axis] + (HEADS, HD) + shape[axis + 1:])
    return np.take(w, order, axis=axis).reshape(shape)


def shape_tables():
    f = np.float32
    pos = np.arange(SEQ, dtype=f)
    freq_a = f(10000.0) ** (-np.arange(0, HD, 2, dtype=f) / f(HD))
    freq_r = f(1.0) / (f(10000.0) ** np.linspace(0.0, 1.0, HD // 2, dtype=f))
    ang_a, ang_r = pos[:, None] * freq_a[None], pos[:, None] * freq_r[None]
    row = np.arange(P) % HD
    at_a, at_r = row % (HD // 2), row // 2
    log_gamma = np.log1p(-np.exp2(f(-5.0) - np.arange(HEADS, dtype=f))).astype(f)
    idx = np.arange(P, dtype=f)
    diff = idx[:, None] - idx[None, :]
    decay = np.where(diff[None] >= 0,
                     np.exp(np.maximum(diff, 0)[None] * log_gamma[:, None, None]), 0).astype(f)
    w_k = np.exp((f(P) - 1 - idx)[None] * log_gamma[:, None]).astype(f)
    w_q = np.exp((idx + 1)[None] * log_gamma[:, None]).astype(f)
    g_chunk = np.exp(f(P) * log_gamma).astype(f)
    rot_a, rot_r = np.zeros((P, P), f), np.zeros((P, P), f)
    for m in range(P):
        rot_a[m + 32 if m % HD < 32 else m - 32, m] = -1 if m % HD < 32 else 1
        rot_r[m ^ 1, m] = -1 if m % 2 == 0 else 1
    q = np.arange(P)[:, None]
    rel = q - (np.arange(2 * P)[None] - P)
    parts = {
        "cos_a": np.cos(ang_a)[:, at_a].T, "sin_a": np.sin(ang_a)[:, at_a].T,
        "cos_r": np.cos(ang_r)[:, at_r].T, "sin_r": np.sin(ang_r)[:, at_r].T,
        "decay": decay.transpose(2, 0, 1).reshape(P, HEADS * P),
        "w_q": np.stack([np.repeat(w_q[2 * j:2 * j + 2], HD, axis=0) for j in range(4)], 1)
        .reshape(P, 4 * P),
        "w_k": np.repeat(w_k.T, HD, axis=1),
        "g_chunk": np.stack([np.repeat(g_chunk[2 * j:2 * j + 2], HD) for j in range(4)], 1),
        "band": np.where((rel >= 0) & (rel < P), 0.0, -BIG),
        "rot_a": rot_a, "rot_r": rot_r,
    }
    at, cols, n = {}, [], 0
    for name, v in parts.items():
        at[name] = (n, n + v.shape[1])
        n += v.shape[1]
        cols.append(v.astype(f))
    return np.ascontiguousarray(np.concatenate(cols, 1)), at


WINDOW_2 = 2 * P
REL_N = 3 * P - 1


def distance_buckets():
    f = np.float32
    n = 255 - np.arange(REL_N)
    nf = np.maximum(n, 1).astype(f)
    large = 16 + (np.log(nf / f(16)) / f(np.log(8.0)) * f(16)).astype(np.int32)
    bucket = np.where(n < 16, n, np.minimum(large, BUCKETS - 1))
    assert bucket[0] == BUCKETS - 1 and bucket[255 - (P + 1)] == BUCKETS - 1
    hot = np.zeros((BUCKETS, REL_N), f)
    for i in range(REL_N):
        if n[i] >= 0:
            hot[bucket[i], i] = 1
    return hot, np.broadcast_to(np.where(n >= 0, 0.0, -BIG).astype(f), (8, REL_N)).copy()


def kernel(**inputs):
    from concourse import bacc
    from concourse.bass_utils import run_bass_kernel_spmd

    v = {k: np.asarray(a) for k, a in inputs.items()}
    arrays = {}

    arrays["x"] = np.ascontiguousarray(v["x"][0].T)
    arrays["meta"] = np.ascontiguousarray(v["meta_tokens_2"].T)

    def stacked(name, per_layer):
        return np.concatenate([column_tiles(per_layer(w)) for w in v[name]], 0)

    aw, kw = HEADS * HD, 2 * HD
    cuts = np.cumsum([aw, kw, kw, 512, 512, 512])

    def in_1(w):
        qa, ka, va, qr, kr, vr, gr = np.split(w, cuts, axis=1)
        tiles = [head_pairs(qa, 1), ka, va]
        for j in range(4):
            tiles += [a[:, j * P:(j + 1) * P] for a in (qr, kr, vr, gr)]
        return np.concatenate(tiles, 1)

    def in_2(w):
        qa, ka, va, qb, ckv, iq, ik, iw = np.split(
            w, np.cumsum([512, 512, 512, 512, 256, 512, 64]), axis=1)
        return np.concatenate([iq, ik, ik, np.tile(iw, (1, P // IDX_HEADS)), ckv, qb,
                               qa, ka, va], 1)

    same = lambda w: w
    arrays["w_in"] = stacked("w_in", in_1)
    arrays["w_out"] = stacked("w_out", lambda w: np.concatenate(
        [head_pairs(w[:aw], 0), w[aw:]], 0))
    for name in ("ffn1", "ffn2"):
        arrays[name + "_gu"] = stacked(name + "_w_gu", same)
        arrays[name + "_down"] = stacked(name + "_w_down", same)
    arrays["b2_in"] = stacked("w_in_2", in_2)
    arrays["b2_out"] = stacked("w_out_2", same)
    for i in "12":
        arrays["b2_gate" + i] = stacked(f"ffn{i}_w_gate_2", same)
        arrays["b2_up" + i] = stacked(f"ffn{i}_w_up_2", same)
        arrays["b2_down" + i] = stacked(f"ffn{i}_w_down_2", same)
    arrays["w_uk"] = np.ascontiguousarray(
        v["b_w_uk_2"][0].transpose(1, 0, 2).reshape(P, B_HEADS * B_DC))
    arrays["w_uv"] = np.ascontiguousarray(
        v["b_w_uv_2"][0].reshape(B_HEADS, 2, P, P).transpose(2, 0, 1, 3).reshape(P, -1))
    arrays["rel_bias"] = np.ascontiguousarray(v["rel_bias_2"])

    gain_at, cols = {}, []

    def column(name, a):
        gain_at[name] = sum(c.shape[1] for c in cols)
        cols.append(np.ascontiguousarray(a))

    for layer in range(DEPTH):
        for n in "123":
            column(f"ln{n}_g{layer}", v[f"ln{n}_g"][layer].reshape(KT, P).T)
            column(f"ln{n}_b{layer}", v[f"ln{n}_b"][layer].reshape(KT, P).T)
        column(f"sinks{layer}", np.broadcast_to(
            v["attn_sinks"][layer][None], (P, HEADS)))
    for n in ("ffn1_norm", "mix_norm", "ffn2_norm"):
        column(n, v[n + "_2"][0].reshape(KT, P).T)
    for n in ("a_q_norm", "a_k_norm"):
        column(n, np.tile(v[n + "_2"][0], 2)[:, None])
    column("a_subln", v["a_subln_2"][0][:, None])
    for n in ("b_kv_norm", "b_q_norm"):
        column(n, v[n + "_2"][0].reshape(2, P).T)
    for n in ("q1", "k1", "q2", "k2"):
        column("lambda_" + n, np.tile(v[f"a_lambda_{n}_2"][0], 2)[:, None])
    arrays["gains"] = np.ascontiguousarray(np.concatenate(cols, 1))

    arrays["ident"] = np.eye(P, dtype=np.float32)
    arrays["flip"] = np.eye(P, dtype=np.float32)[::-1].copy()
    arrays["half"] = np.kron(np.eye(2, dtype=np.float32), np.ones((HD, HD), np.float32))
    arrays["tables"], table_at = shape_tables()
    arrays["distance_hot"], arrays["distance_mask"] = distance_buckets()

    nc = bacc.Bacc("TRN2", target_bir_lowering=False, num_devices=1)
    t = {"gain_at": gain_at, "table_at": table_at}
    feed = {}
    for name, a in arrays.items():
        feed["in_" + name] = a
        t[name] = nc.dram_tensor("in_" + name, a.shape, F32, kind="ExternalInput").ap()
    t["out"] = nc.dram_tensor("out", (D, SEQ), F32, kind="ExternalOutput").ap()
    t["bias_rows"] = nc.dram_tensor("bias_rows", (8, REL_N), F32, kind="Internal").ap()
    build(nc, t)
    result = run_bass_kernel_spmd(nc, [feed], core_ids=[0]).results[0]["out"]
    return np.ascontiguousarray(np.asarray(result).T)[None]
```

```python
from contextlib import ExitStack

import numpy as np

import concourse.bass as bass
from concourse import mybir

F32 = mybir.dt.float32
F32R = mybir.dt.float32r
ALU = mybir.AluOpType
ACT = mybir.ActivationFunctionType
AX = mybir.AxisListType

P = 128
BIG = 1.0e30

SEQ = 512
META = 16
LEN = META + SEQ
TOK = slice(META, LEN)
MET = slice(0, META)
HALF = LEN // 2
D = 1024
KT = D // P
DEPTH = 2
D_FF = 2816
FT = D_FF // P
HD = 64
NB = SEQ // P
ALPHA = (2 * DEPTH) ** 0.25
LN_EPS = 1e-5
GN_EPS = 1e-6
RMS_EPS = 1e-6
HEADS = 8
IN_TILES_1 = 22
IN_TILES_2 = 24
A_HEADS = 4
B_HEADS = 4
B_DC = 256
IDX_HEADS = 8
TOPK = 128
BUCKETS = 32
LAM_INIT = 0.2

RAW_SLOTS = 3
SPLIT_SLOTS = 4
AHEAD = 3
GROUP = 3
PIECE = 8


class Done:

    def __init__(self, sem, value):
        self.sem, self.value = sem, value


class Engine:

    def __init__(self, eng, sem):
        self.eng, self.sem, self.count, self.seen = eng, sem, 0, {}

    def wait(self, after):
        for d in after:
            if d is None or self.seen.get(id(d.sem), 0) >= d.value:
                continue
            self.seen[id(d.sem)] = d.value
            self.eng.wait_ge(d.sem, d.value)

    def do(self, issue, after=(), mark=True):
        self.wait(after)
        instruction = issue()
        if not mark:
            return None
        self.count += 1
        instruction.then_inc(self.sem, 1)
        return Done(self.sem, self.count)

    def dma(self, sem, total, issue, after=()):
        self.wait(after)
        issue().then_inc(sem, 16)
        return Done(sem, total)


class Slots:

    def __init__(self, bufs):
        self.bufs, self.free, self.next = bufs, [[] for _ in bufs], 0

    def take(self):
        n = len(self.bufs)
        i = next(j % n for j in range(self.next, self.next + n) if self.free[j % n] is not None)
        self.next = (i + 1) % n
        free, self.free[i] = self.free[i], None
        return i, self.bufs[i], free


def pieces(matrix, col_tile, tiles, first=0):
    end = first + tiles
    return [(matrix, col_tile, k, min(PIECE, end - k)) for k in range(first, end, PIECE)]


def build(nc, t):
    ctx = ExitStack()
    with ctx:
        sem = lambda name: ctx.enter_context(nc.semaphore(name))
        sb = lambda name, shape, dt=F32: ctx.enter_context(nc.sbuf_tensor(name, shape, dt))

        pe = Engine(nc.tensor, sem("pe_done"))
        act = Engine(nc.scalar, sem("act_done"))
        dve = Engine(nc.vector, sem("dve_done"))
        pool = Engine(nc.gpsimd, sem("pool_done"))
        sp = Engine(nc.sync, sem("sp_done"))

        x = sb("x", [P, KT, LEN])
        x_hi = sb("x_hi", [P, KT, LEN], F32R)
        x_lo = sb("x_lo", [P, KT, LEN], F32R)
        w_raw = [sb(f"w_raw{i}", [P, PIECE * P]) for i in range(RAW_SLOTS)]
        w_hi = [sb(f"w_hi{i}", [P, PIECE * P], F32R) for i in range(SPLIT_SLOTS)]
        w_lo = [sb(f"w_lo{i}", [P, PIECE * P], F32R) for i in range(SPLIT_SLOTS)]
        scratch = Slots([sb(f"scratch{i}", [P, LEN]) for i in range(4)])
        squares = Slots([sb(f"square{i}", [P, LEN]) for i in range(2)])
        ident = sb("ident", [P, P])
        ones = sb("ones", [P, P])
        half = sb("half", [P, P])
        pairs = sb("pairs", [P, 2])
        eps = sb("eps", [P, 4])
        gains = sb("gains", [P, t["gains"].shape[1]])
        lam = sb("lam", [P, 8])
        small = Slots([sb(f"small{i}", [P, 16]) for i in range(10)])
        psum = ctx.enter_context(nc.psum_tensor("psum", [P, 8, 512], F32))

        bank = lambda i: psum[:, i, :]
        bank_free = [[] for _ in range(8)]
        bank_age = [0] * 8
        halves = lambda tile: tile.rearrange("p (a n) -> p a n", a=2)
        two_halves = lambda b: psum[:, b:b + 2, 0:HALF]

        def free_banks(n):
            found = [at for at in range(9 - n)
                     if all(bank_free[b] is not None for b in range(at, at + n))]
            return min(found, key=lambda at: max(bank_age[at:at + n]), default=None)

        def take_banks(n=1):
            at = free_banks(n)
            assert at is not None, "all banks are held"
            free = [d for b in range(at, at + n) for d in bank_free[b]]
            for b in range(at, at + n):
                bank_free[b] = None
            return at, free

        def release_banks(at, n, readers):
            for b in range(at, at + n):
                bank_free[b] = list(readers)
                bank_age[b] = max(bank_age) + 1

        tasks = []

        def step_tasks():
            for task in list(tasks):
                if next(task, "end") == "end":
                    tasks.remove(task)

        def run_tasks(until=None):
            rounds = 0
            while (not until()) if until else tasks:
                step_tasks()
                rounds += 1
                assert rounds < 5000, "tasks wait for each other"

        def banks_for(n=1):
            while free_banks(n) is None:
                yield
            return take_banks(n)

        def slots_for(slots, n=1):
            while sum(f is not None for f in slots.free) < n:
                yield
            return [slots.take() for _ in range(n)]

        def made(table, *keys):
            while any(table.get(k) is None for k in keys):
                yield
            return [table[k] for k in keys]

        load_sem = {}

        def load(eng, name, dst, src, after=()):
            load_sem[name] = sem("load_" + name)
            return eng.dma(load_sem[name], 16, lambda: eng.eng.dma_start(dst, src), after)

        meta_loaded = load(pool, "meta", x[:, :, MET], t["meta"].rearrange("(k p) n -> p k n", p=P))
        ident_loaded = load(pool, "ident", ident[:], t["ident"])
        half_loaded = load(pool, "half", half[:], t["half"])
        gains_loaded = load(pool, "gains", gains[:], t["gains"])
        ones_set = dve.do(lambda: nc.vector.memset(ones[:], 1.0))
        consts_set = dve.do(lambda: nc.vector.memset(pairs[:], 0.0))
        for to, value in ((pairs[0:HD, 0:1], 1.0), (pairs[HD:P, 1:2], 1.0),
                          (eps[:, 0:1], LN_EPS), (eps[:, 1:2], RMS_EPS),
                          (eps[:, 2:3], 4.0 * LN_EPS)):
            consts_set = dve.do(lambda to=to, value=value: nc.vector.memset(to, value),
                                after=[consts_set])
        gain_at = t["gain_at"]

        def gain(name, k=0, rows=slice(0, P)):
            c = gain_at[name] + k
            return gains[rows, c:c + 1]

        plan = weight_plan()
        raw_sem = [sem(f"raw{i}") for i in range(RAW_SLOTS)]
        split = []
        piece_read = []
        taken = [0]

        def split_piece(u):
            matrix, m, k0, n = plan[u]
            r, s = u % RAW_SLOTS, u % SPLIT_SLOTS
            src = t[matrix][m, :, k0 * P:(k0 + n) * P]
            loaded = sp.dma(raw_sem[r], 16 * (u // RAW_SLOTS + 1),
                            lambda: nc.sync.dma_start(w_raw[r][:, 0:n * P], src),
                            after=[split[u - RAW_SLOTS][1]] if u >= RAW_SLOTS else [])
            unread = [piece_read[u - SPLIT_SLOTS]] if u >= SPLIT_SLOTS else []
            high = act.do(lambda: nc.scalar.copy(w_hi[s][:, 0:n * P], w_raw[r][:, 0:n * P]),
                          after=[loaded] + unread)
            sub = pool if matrix in ("b2_in", "b2_out") else dve
            low = sub.do(lambda: sub.eng.tensor_tensor(
                w_lo[s][:, 0:n * P], w_raw[r][:, 0:n * P], w_hi[s][:, 0:n * P].bitcast(F32),
                ALU.subtract), after=[high])
            split.append((high, low))

        def stream_until(u):
            while len(split) <= min(u, len(plan) - 1):
                split_piece(len(split))

        def multiply(u, k, outs, operand, first, last, free, mark):
            _, _, k0, _ = plan[u]
            s = u % SPLIT_SLOTS
            hi, lo, ready = operand(k)
            w_h = w_hi[s][:, (k - k0) * P:(k - k0 + 1) * P]
            w_l = w_lo[s][:, (k - k0) * P:(k - k0 + 1) * P]
            pe.wait([*split[u], *ready, *(free if first else [])])
            done = None
            for w, v, begin, end in ((w_h, hi, first, False), (w_h, lo, False, False),
                                     (w_l, hi, False, last)):
                for i, (o, c) in enumerate(outs):
                    done = pe.do(lambda: nc.tensor.matmul(o, w, v[:, c], start=begin, stop=end),
                                 mark=mark and w is w_l and i == len(outs) - 1)
            return done

        def out_ranges(b, wide):
            if wide:
                return [(psum[:, b + i, 0:HALF], slice(i * HALF, (i + 1) * HALF))
                        for i in range(2)]
            return [(bank(b), slice(0, SEQ))]

        def next_piece(key):
            u = taken[0]
            taken[0] += 1
            assert plan[u] == key, (plan[u], key)
            return u

        def project(matrix, m, tiles, operand, wide=False, k_range=None):
            begin, end = k_range or (0, tiles)
            n = 2 if wide else 1
            while free_banks(n) is None:
                step_tasks()
            b, free = take_banks(n)
            outs = out_ranges(b, wide)
            for key in pieces(matrix, m, end - begin, begin):
                u = next_piece(key)
                stream_until(u + AHEAD)
                for k in range(key[2], key[2] + key[3]):
                    done = multiply(u, k, outs, operand, k == begin, k == end - 1, free,
                                    k == key[2] + key[3] - 1)
                piece_read.append(done)
                step_tasks()
            return b, done

        def project_group(columns, operand, wide=False):
            group = []
            for matrix, m in columns:
                b, free = take_banks(2 if wide else 1)
                (key,) = pieces(matrix, m, KT)
                group.append((next_piece(key), b, free, out_ranges(b, wide)))
            stream_until(group[-1][0])
            for k in range(KT):
                done = [multiply(u, k, outs, operand, k == 0, k == KT - 1, free, k == KT - 1)
                        for u, b, free, outs in group]
            piece_read.extend(done)
            return [(g[1], d) for g, d in zip(group, done)]

        def split_into(hi, lo, value, after=()):
            h = act.do(lambda: nc.scalar.copy(hi, value), after=after)
            l = dve.do(lambda: nc.vector.tensor_tensor(lo, value, hi.bitcast(F32), ALU.subtract),
                       after=[h])
            return h, l

        ready = [[] for _ in range(KT)]
        x_ready = [[] for _ in range(KT)]

        def tokens_operand(k):
            return x_hi[:, k, TOK], x_lo[:, k, TOK], ready[k]

        def all_operand(k):
            return x_hi[:, k, :], x_lo[:, k, :], ready[k]

        class Stats:

            def __init__(self, groups, wide, banks):
                self.groups, self.wide = groups, wide
                self.blocks = [(a * HALF + c, w) for c, w in ((0, P), (P, P), (2 * P, HALF - 2 * P))
                               for a in range(2)] if wide else \
                    [(META + P * j, P) for j in range(NB)]
                self.sums, self.sums_free = banks
                self.first = True
                self.square_slot = None

            def add(self, tile, after, last):
                g = self.groups
                for j, (c, w) in enumerate(self.blocks):
                    done = pe.do(lambda o=psum[0:w, self.sums, j * g:(j + 1) * g],
                                 a=tile[:, c:c + w], r=ones[:, 0:1] if g == 1 else pairs[:],
                                 f=self.first: nc.tensor.matmul(
                                     o, a, r, start=f, stop=last, skip_group_check=True),
                                 after=[*after, ones_set, consts_set] +
                                 (self.sums_free if self.first else []),
                                 mark=(j == len(self.blocks) - 1))
                    self.first = False
                self.summed = done
                if self.square_slot is not None:
                    squares.free[self.square_slot] = [done]
                return done

            def root(self, scale, eps_col, factor=1.0):
                g = self.groups
                self.slot, root, root_free = small.take()
                parts = [(P, 0, NB * g)]
                if self.wide:
                    parts.append((HALF - 2 * P, NB * g, (NB + 2) * g))
                for w, a, b in parts:
                    rooted = act.do(lambda w=w, a=a, b=b: nc.scalar.activation(
                        root[0:w, a:b], psum[0:w, self.sums, a:b], ACT.Sqrt,
                        bias=eps[0:w, eps_col:eps_col + 1], scale=scale),
                        after=[self.summed, consts_set] + root_free)
                release_banks(self.sums, 1, [rooted])
                for w, a, b in parts:
                    inverse = dve.do(lambda w=w, a=a, b=b: nc.vector.reciprocal(
                        root[0:w, a:b], root[0:w, a:b]), after=[rooted])
                if factor != 1.0:
                    w, a, b = parts[0]
                    inverse = dve.do(lambda: nc.vector.tensor_scalar(
                        root[0:w, a:b], root[0:w, a:b], factor, None, ALU.mult), after=[inverse])
                self.rooted, self.inverse, self.roots = rooted, inverse, root

            def spread(self, banks):
                g = self.groups
                self.out, out_free = banks
                for j, (c, w) in enumerate(self.blocks):
                    for s in range(g):
                        rows = slice(P // g * s, P // g * (s + 1))
                        lhs = self.roots[0:w, j * g + s:j * g + s + 1].to_broadcast([w, P // g])
                        to = psum[rows, self.out + c // HALF, c % HALF:c % HALF + w] \
                            if self.wide else psum[rows, self.out, c - META:c - META + P]
                        spread = pe.do(lambda o=to, a=lhs, w=w: nc.tensor.matmul(
                            o, a, ident[0:w, 0:w], start=True, stop=True),
                            after=[self.inverse, ident_loaded, self.rooted] + out_free)
                small.free[self.slot] = [spread]
                return two_halves(self.out) if self.wide else bank(self.out), spread

            def release(self, readers):
                release_banks(self.out, 2 if self.wide else 1, readers)

        def square_into(stats, tile, cols, after, last):
            slot, sq, free = squares.take()
            done = act.do(lambda: nc.scalar.activation(sq[:, cols], tile, ACT.Square),
                          after=list(after) + free)
            squares.free[slot] = [stats.add(sq, [done], last)]
            return done

        def squared(groups, wide, tile, cols, after):
            banks = yield from banks_for()
            stats = Stats(groups, wide, banks)
            ((slot, sq, free),) = yield from slots_for(squares)
            done = act.do(lambda: nc.scalar.activation(sq[:, cols], tile, ACT.Square),
                          after=[after] + free)
            stats.square_slot = slot
            return stats, (sq, [done])

        class MeanSum:

            def __init__(self):
                self.bank, self.free = take_banks()
                self.tiles = 0

            def add(self, k, done):
                yield
                self.summed = pe.do(lambda: nc.tensor.matmul(
                    bank(self.bank), ones[:], x[:, k, TOK], start=self.tiles == 0,
                    stop=self.tiles == KT - 1), after=[done, ones_set] +
                    (self.free if self.tiles == 0 else []))
                self.tiles += 1

        def layer_norm_x(g, b, eps_col, mean):
            run_tasks()
            slot, negmean, nfree = scratch.take()
            meaned = act.do(lambda: nc.scalar.mul(negmean[:, TOK], bank(mean.bank), -1.0 / D),
                            after=[mean.summed] + nfree)
            release_banks(mean.bank, 1, [meaned])
            stats = Stats(1, False, take_banks())
            squared = []
            for k in range(KT):
                c = dve.do(lambda k=k: nc.vector.tensor_tensor(
                    x[:, k, TOK], x[:, k, TOK], negmean[:, TOK], ALU.add), after=[meaned])
                squared.append(square_into(stats, x[:, k, TOK], TOK, [c], k == KT - 1))
            scratch.free[slot] = [c]
            stats.root(1.0 / D, eps_col)
            main, spread = stats.spread(take_banks())

            def finish(k, shifted):
                ready[k] = list(split_into(x_hi[:, k, TOK], x_lo[:, k, TOK], x[:, k, TOK],
                                           after=[shifted, piece_read[-1]]))
            waiting = None
            for k in range(KT):
                y = dve.do(lambda k=k: nc.vector.scalar_tensor_tensor(
                    x[:, k, TOK], x[:, k, TOK], gain(g, k), main, ALU.mult, ALU.mult),
                    after=[spread, squared[k], gains_loaded])
                shifted = act.do(lambda k=k: nc.scalar.activation(
                    x[:, k, TOK], x[:, k, TOK], ACT.Identity, bias=gain(b, k)), after=[y])
                x_ready[k] = [shifted]
                if waiting:
                    finish(*waiting)
                waiting = (k, shifted)
            finish(*waiting)
            stats.release([y])

        def rms_norm_x(g, x_done, stats):
            run_tasks()
            stats.root(1.0 / D, 1)
            main, spread = stats.spread(take_banks(2))
            waiting = None

            def finish(k, slot, y, normed):
                ready[k] = list(split_into(x_hi[:, k, :], x_lo[:, k, :], y[:],
                                           after=[normed, piece_read[-1]]))
                scratch.free[slot] = ready[k]
            for k in range(KT):
                slot, y, free = scratch.take()
                normed = dve.do(lambda k=k, y=y: nc.vector.scalar_tensor_tensor(
                    halves(y[:]), halves(x[:, k, :]), gain(g, k), main, ALU.mult, ALU.mult),
                    after=[spread, *x_done[k]] + free)
                if waiting:
                    finish(*waiting)
                waiting = (k, slot, y, normed)
            finish(*waiting)
            stats.release([normed])

        def ffn(gate, up, down, wide, residual, group=GROUP):
            with ExitStack() as own:
                tensor = lambda name, shape, dt: own.enter_context(nc.sbuf_tensor(name, shape, dt))
                tag = f"{gate[0]}{gate[1]}"
                cols, n = (LEN, 2) if wide else (SEQ, 1)
                h_hi = tensor("h_hi_" + tag, [P, FT, cols], F32R)
                h_lo = tensor("h_lo_" + tag, [P, FT, cols], F32R)
                h_ready = [None] * FT
                operand = all_operand if wide else tokens_operand
                view = (lambda tile: halves(tile)) if wide else (lambda tile: tile)
                product = two_halves if wide else bank
                order = [(w[0], w[1] + f) for f in range(FT) for w in (gate, up)]
                first = project_group(order[0:group], operand, wide)
                order = iter(order[group:])
                pending = []
                for f in range(FT):
                    a, u = (first.pop(0) if first else project(*next(order), KT, operand, wide)
                            for _ in range(2))
                    slot, hid, hfree = scratch.take()
                    silu = act.do(lambda: nc.scalar.activation(
                        view(hid[:, 0:cols]), product(a[0]), ACT.Silu), after=[a[1]] + hfree)
                    release_banks(a[0], n, [silu])
                    gated = dve.do(lambda: nc.vector.tensor_tensor(
                        view(hid[:, 0:cols]), view(hid[:, 0:cols]), product(u[0]), ALU.mult),
                        after=[silu, u[1]])
                    release_banks(u[0], n, [gated])

                    def finish(f=f, slot=slot, hid=hid, gated=gated):
                        h_ready[f] = list(split_into(
                            h_hi[:, f, :], h_lo[:, f, :], hid[:, 0:cols],
                            after=[gated] + region_free))
                        scratch.free[slot] = h_ready[f]
                    for later in pending:
                        later()
                    pending = [finish]
                pending[0]()
                hidden = lambda k: (h_hi[:, k, :], h_lo[:, k, :], h_ready[k])
                for m in range(KT):
                    residual(m, *project(down[0], down[1] + m, FT, hidden, wide))
            region_ends()

        region_free = []

        def region_ends():
            region_free[:] = [Done(e.sem, e.count) for e in (pe, act, dve, pool) if e.count]

        def residual_tokens(scale):
            mean = MeanSum()

            def residual(m, b, done):
                z = dve.do(lambda: nc.vector.scalar_tensor_tensor(
                    x[:, m, TOK], x[:, m, TOK], scale, bank(b), ALU.mult, ALU.add),
                    after=[done, *x_ready[m]])
                release_banks(b, 1, [z])
                tasks.append(mean.add(m, z))
            return residual, mean

        def copy_psum(dst, src, after):
            return act.do(lambda: nc.scalar.copy(dst, src), after=after)

        def transposed(banks, sources, copy_to, after, free):
            b, bfree = banks
            for i, (tile, rows, cols) in enumerate(sources):
                done = pe.do(lambda i=i, a=tile, r=rows, c=cols: nc.tensor.transpose(
                    psum[0:c, b, i * P:i * P + r], a, ident[0:r, 0:r]),
                    after=[*after, ident_loaded] + bfree, mark=i == len(sources) - 1)
            for dst, parts, cols in copy_to:
                copied = copy_psum(dst, psum[parts, b, cols], [done, *free])
            release_banks(b, 1, [copied])
            return copied, done

        def mixer_1(layer):
            own = ExitStack()
            tensor = lambda name, shape, dt=F32: own.enter_context(
                nc.sbuf_tensor(f"{name}_{layer}", shape, dt))
            entry = list(region_free)
            tab = tensor("tables", [P, t["tables"].shape[1]])
            tab_loaded = load(pool, f"tables{layer}", tab[:], t["tables"], after=entry)
            table = lambda n: tab[:, t["table_at"][n][0]:t["table_at"][n][1]]
            q_a = tensor("q_a", [P, 4, SEQ])
            k_a = tensor("k_a", [P, SEQ])
            v_a = tensor("v_a", [P, NB, P])
            y_a = tensor("y_a", [P, 4, SEQ])
            y_r = tensor("y_r", [P, 4, SEQ])
            q_r = [tensor(f"q_r{i}", [P, SEQ]) for i in range(2)]
            q_w = [tensor(f"q_w{i}", [P, SEQ]) for i in range(2)]
            k_r = [tensor(f"k_r{i}", [P, SEQ]) for i in range(2)]
            k_w = [tensor(f"k_w{i}", [P, NB, P]) for i in range(2)]
            v_r = [tensor(f"v_r{i}", [P, NB, P]) for i in range(2)]
            gate = tensor("gate", [P, 4, SEQ])
            prob = Slots([tensor(f"prob{i}", [P, 4, 2 * P]) for i in range(3)])
            prob_t = Slots([tensor(f"prob_t{i}", [P, 4 * P]) for i in range(3)])
            state = tensor("state", [P, NB - 1, HD])

            done_ = {}

            def rotated(b, done, out, key, rot, cos, sin, scale, free=lambda: ()):
                ((slot, raw, rfree),) = yield from slots_for(scratch)
                copied = copy_psum(raw[:, TOK], bank(b), [done] + rfree)
                release_banks(b, 1, [copied])
                ((slot2, part, pfree),) = yield from slots_for(scratch)
                times_cos = dve.do(lambda: nc.vector.scalar_tensor_tensor(
                    part[:, TOK], raw[:, TOK], scale, table(cos), ALU.mult, ALU.mult),
                    after=[copied, tab_loaded] + pfree)
                yield
                while free() is None:
                    yield
                wb, wfree = yield from banks_for()
                turned = pe.do(lambda: nc.tensor.matmul(
                    bank(wb), table(rot), raw[:, TOK], start=True, stop=True),
                    after=[copied, tab_loaded] + wfree)
                times_sin = dve.do(lambda: nc.vector.scalar_tensor_tensor(
                    out, bank(wb), scale, table(sin), ALU.mult, ALU.mult),
                    after=[turned, *entry, *free()])
                release_banks(wb, 1, [times_sin])
                scratch.free[slot] = [times_cos, turned]
                done_[key] = dve.do(lambda: nc.vector.tensor_tensor(
                    out, out, part[:, TOK], ALU.add), after=[times_cos, times_sin])
                scratch.free[slot2] = [done_[key]]

            def token_major(b, done, out, key, free=lambda: ()):
                ((slot, raw, rfree),) = yield from slots_for(scratch)
                copied = copy_psum(raw[:, TOK], bank(b), [done] + rfree)
                release_banks(b, 1, [copied])
                yield
                while free() is None:
                    yield
                banks = yield from banks_for()
                done_[key], read = transposed(banks,
                    [(raw[:, META + n * P:META + (n + 1) * P], P, P) for n in range(NB)],
                    [(out[:].rearrange("p n f -> p (n f)"), slice(0, P), slice(0, SEQ))],
                    [copied], [*entry, *free()])
                scratch.free[slot] = [read]

            def attention(items):
                yield from made(done_, *(("q", j) for j in range(4)), "k", "v")
                for n, g in items:
                    rows = slice(HD * g, HD * (g + 1))
                    k0 = max(n - 1, 0) * P
                    width = (n + 1) * P - k0
                    band = table("band")[:, 2 * P - width:].unsqueeze(1).to_broadcast(
                        [P, 4, width])
                    ((slot, s, sfree),) = yield from slots_for(prob)
                    ((st_slot, st, st_free),) = yield from slots_for(small)
                    b, bfree = yield from banks_for(2)
                    for j in range(4):
                        out = psum[:, b + j // 2, (j % 2) * 256:(j % 2) * 256 + width]
                        done = pe.do(lambda: nc.tensor.matmul(
                            out, q_a[rows, j, n * P:(n + 1) * P], k_a[rows, k0:k0 + width],
                            start=True, stop=True),
                            after=[*(done_["q", i] for i in range(4)), done_["k"]] + bfree)
                    scores = psum[:, b:b + 2, :].rearrange(
                        "p b (j k) -> p (b j) k", j=2)[:, :, 0:width]
                    s = s[:, :, 0:width]
                    masked = dve.do(lambda: nc.vector.scalar_tensor_tensor(
                        s, scores, HD ** -0.5, band, ALU.mult, ALU.add),
                        after=[done, tab_loaded, *entry] + sfree)
                    release_banks(b, 2, [masked])
                    top = dve.do(lambda: nc.vector.tensor_reduce(
                        st[:, 0:4], s, AX.X, ALU.max), after=[masked] + st_free)
                    sink = gains[:, gain_at[f"sinks{layer}"] + 4 * g:][:, 0:4]
                    top = dve.do(lambda: nc.vector.tensor_tensor(
                        st[:, 0:4], st[:, 0:4], sink, ALU.max), after=[top])
                    neg = dve.do(lambda: nc.vector.tensor_scalar(
                        st[:, 0:4], st[:, 0:4], -1.0, None, ALU.mult), after=[top])
                    sink_in = dve.do(lambda: nc.vector.tensor_tensor(
                        st[:, 4:8], sink, st[:, 0:4], ALU.add), after=[neg])
                    for j in range(4):
                        act.do(lambda: nc.scalar.activation(
                            s[:, j, :], s[:, j, :], ACT.Exp, bias=st[:, j:j + 1],
                            accum_out=st[:, 8 + j:9 + j]), after=[neg])
                    exps = act.do(lambda: nc.scalar.activation(
                        st[:, 4:8], st[:, 4:8], ACT.Exp), after=[sink_in])
                    yield
                    total = dve.do(lambda: nc.vector.tensor_tensor(
                        st[:, 8:12], st[:, 8:12], st[:, 4:8], ALU.add), after=[exps])
                    inverse = dve.do(lambda: nc.vector.reciprocal(st[:, 8:12], st[:, 8:12]),
                                     after=[total])
                    normed = dve.do(lambda: nc.vector.tensor_tensor(
                        s, s, st[:, 8:12].unsqueeze(2).to_broadcast([P, 4, width]), ALU.mult),
                        after=[inverse])
                    small.free[st_slot] = [normed]
                    yield
                    blocks = width // P
                    turned = yield from slots_for(prob_t, blocks)
                    copied = [None] * blocks
                    for kb, (_, w_t, wfree) in enumerate(turned):
                        banks = yield from banks_for()
                        copied[kb], read = transposed(
                            banks, [(s[:, j, kb * P:(kb + 1) * P], P, P) for j in range(4)],
                            [(w_t[:], slice(0, P), slice(0, SEQ))], [normed], [*entry, *wfree])
                    prob.free[slot] = [read]
                    yield
                    b, bfree = yield from banks_for()
                    for kb, (_, w_t, _) in enumerate(turned):
                        done = pe.do(lambda: nc.tensor.matmul(
                            psum[rows, b, :], v_a[:, n + 1 - blocks + kb, rows], w_t[:],
                            start=kb == 0, stop=kb == blocks - 1),
                            after=[copied[kb], done_["v"]] + bfree)
                    for i, _, _ in turned:
                        prob_t.free[i] = [done]
                    done_["y_a", n, g] = act.do(lambda: nc.scalar.copy(
                        y_a[rows, :, n * P:(n + 1) * P],
                        psum[rows, b, :].rearrange("p (j q) -> p j q", j=4)),
                        after=[done, *entry])
                    release_banks(b, 1, [done_["y_a", n, g]])

            y_ready = [None] * KT

            def keys_weighted(j):
                i = j % 2
                yield from made(done_, ("k_r", j))
                yield
                wb, wfree = yield from banks_for()
                for n in range(NB):
                    turned = pe.do(lambda: nc.tensor.transpose(
                        psum[:, wb, n * P:(n + 1) * P], k_r[i][:, n * P:(n + 1) * P], ident[:]),
                        after=[done_["k_r", j]] + wfree)
                done_["k_w", j] = dve.do(lambda: nc.vector.tensor_tensor(
                    k_w[i][:], bank(wb).rearrange("p (n d) -> p n d", n=NB),
                    table("w_k")[:, j * P:(j + 1) * P].unsqueeze(1).to_broadcast([P, NB, P]),
                    ALU.mult), after=[turned, *entry, *set_free(j)()])
                release_banks(wb, 1, [done_["k_w", j]])

            def set_free(j):
                return lambda: () if j < 2 else \
                    [done_["set_read", j - 2]] if ("set_read", j - 2) in done_ else None

            def retention(j):
                i = j % 2
                yield from made(done_, ("q_r", j))
                done_["q_w", j] = dve.do(lambda: nc.vector.tensor_tensor(
                    q_w[i][:].rearrange("p (n c) -> p n c", n=NB),
                    q_r[i][:].rearrange("p (n c) -> p n c", n=NB),
                    table("w_q")[:, j * P:(j + 1) * P].unsqueeze(1).to_broadcast([P, NB, P]),
                    ALU.mult), after=[done_["q_r", j]])
                yield from made(done_, ("k_w", j), ("v_r", j))
                ((slot, sc, sfree),) = yield from slots_for(prob)
                b, bfree = yield from banks_for(2)
                for n in range(NB):
                    for s in range(2):
                        rows, cols = slice(HD * s, HD * (s + 1)), slice(n * P, (n + 1) * P)
                        scored = pe.do(lambda: nc.tensor.matmul(
                            psum[:, b + s, cols],
                            k_r[i][rows, cols], q_r[i][rows, cols], start=True, stop=True),
                            after=[done_["q_r", j], done_["k_r", j]] + bfree,
                            mark=(n, s) == (NB - 1, 1))
                decay = table("decay")[:, 2 * j * P:2 * (j + 1) * P].rearrange(
                    "p (s i) -> p s i", s=2).unsqueeze(2).to_broadcast([P, 2, NB, P])
                sc = sc[:].rearrange("p a b -> p (a b)").rearrange(
                    "p (s n i) -> p s n i", s=2, n=NB)
                decayed = dve.do(lambda: nc.vector.tensor_tensor(
                    sc, psum[:, b:b + 2, :].rearrange("p s (n i) -> p s n i", n=NB), decay,
                    ALU.mult), after=[scored, tab_loaded, *entry] + sfree)
                release_banks(b, 2, [decayed])
                b2, b2free = yield from banks_for()
                for n in range(NB - 1):
                    for s in range(2):
                        rows = slice(HD * s, HD * (s + 1))
                        added = pe.do(lambda: nc.tensor.matmul(
                            psum[rows, b2, n * HD:(n + 1) * HD], k_w[i][:, n, rows],
                            v_r[i][:, n, rows], start=True, stop=True),
                            after=[done_["k_w", j], done_["v_r", j]] + b2free,
                            mark=(n, s) == (NB - 2, 1))
                st_read = [done_["set_read", j - 1]] if j else []
                before = dve.do(lambda: nc.vector.tensor_copy(
                    state[:, 0, :], psum[:, b2, 0:HD]), after=[added, *st_read, *entry])
                g_col = table("g_chunk")[:, j:j + 1]
                for n in range(1, NB - 1):
                    before = dve.do(lambda: nc.vector.scalar_tensor_tensor(
                        state[:, n, :], state[:, n - 1, :], g_col,
                        psum[:, b2, n * HD:(n + 1) * HD], ALU.mult, ALU.add), after=[before])
                release_banks(b2, 1, [before])
                yield
                b3, b3free = yield from banks_for()
                for n in range(NB):
                    cols = slice(n * P, (n + 1) * P)
                    for s in range(2):
                        rows = slice(HD * s, HD * (s + 1))
                        out = pe.do(lambda: nc.tensor.matmul(
                            psum[rows, b3, cols], v_r[i][:, n, rows],
                            sc[:, s, n, :], start=True, stop=n == 0,
                            skip_group_check=True),
                            after=[decayed, done_["v_r", j]] + b3free, mark=n == 0)
                        if n:
                            out = pe.do(lambda: nc.tensor.matmul(
                                psum[rows, b3, cols], state[rows, n - 1, :],
                                q_w[i][rows, cols], start=False, stop=True,
                                skip_group_check=True), after=[before, done_["q_w", j]])
                prob.free[slot] = [out]
                done_["set_read", j] = out
                ((oslot, o, ofree),) = yield from slots_for(scratch)
                copied = copy_psum(o[:, TOK], bank(b3), [out] + ofree)
                release_banks(b3, 1, [copied])
                yield
                b4, b4free = yield from banks_for()
                summed = pe.do(lambda: nc.tensor.matmul(
                    bank(b4), half[:], o[:, TOK], start=True, stop=True),
                    after=[copied, half_loaded] + b4free)
                centred = dve.do(lambda: nc.vector.scalar_tensor_tensor(
                    o[:, TOK], bank(b4), -1.0 / HD, o[:, TOK], ALU.mult, ALU.add),
                    after=[summed])
                release_banks(b4, 1, [centred])
                stats, square = yield from squared(2, False, o[:, TOK], TOK, centred)
                yield
                stats.add(*square, True)
                stats.root(1.0 / HD, 1)
                yield
                banks = yield from banks_for()
                main, spread = stats.spread(banks)
                normed = dve.do(lambda: nc.vector.tensor_tensor(
                    o[:, TOK], o[:, TOK], main, ALU.mult), after=[spread])
                stats.release([normed])
                yield from made(done_, ("gate", j))
                done_["y_r", j] = dve.do(lambda: nc.vector.tensor_tensor(
                    y_r[:, j, :], o[:, TOK], gate[:, j, :], ALU.mult),
                    after=[normed, done_["gate", j], *entry])
                scratch.free[oslot] = [done_["y_r", j]]

            first = layer * IN_TILES_1
            at = [first]

            def next_tile():
                out = project("w_in", at[0], KT, tokens_operand)
                at[0] += 1
                return out

            group = project_group([("w_in", first + i) for i in range(GROUP)], tokens_operand)
            at[0] += GROUP
            for j in range(4):
                out = group[j] if j < GROUP else next_tile()
                tasks.append(rotated(*out, q_a[:, j, :], ("q", j), "rot_a", "cos_a", "sin_a",
                                     1.0))
            tasks.append(rotated(*next_tile(), k_a[:], "k", "rot_a", "cos_a", "sin_a", 1.0))
            tasks.append(token_major(*next_tile(), v_a, "v"))
            items = iter([(n, g) for n in range(NB) for g in range(2)])
            tasks.extend(attention(items) for _ in range(2))
            for j in range(4):
                i = j % 2
                tasks.append(rotated(*next_tile(), q_r[i][:], ("q_r", j), "rot_r", "cos_r",
                                     "sin_r", 1.0, set_free(j)))
                tasks.append(rotated(*next_tile(), k_r[i][:], ("k_r", j), "rot_r", "cos_r",
                                     "sin_r", HD ** -0.5, set_free(j)))
                tasks.append(keys_weighted(j))
                tasks.append(token_major(*next_tile(), v_r[i], ("v_r", j), set_free(j)))
                tasks.append(retention(j))
            for j in range(4):
                b, done = next_tile()
                done_["gate", j] = act.do(lambda: nc.scalar.activation(
                    gate[:, j, :], bank(b), ACT.Silu), after=[done, *entry])
                release_banks(b, 1, [done_["gate", j]])
            read = piece_read[-1]
            items = [("y_a", n, g) for n in range(NB) for g in range(2)]
            run_tasks(lambda: all(k in done_ for k in items))
            for j in range(4):
                y_ready[j] = list(split_into(x_hi[:, j, TOK], x_lo[:, j, TOK], y_a[:, j, :],
                                             after=[*(done_[k] for k in items), read]))

            def split_retained():
                for j in range(4):
                    yield from made(done_, ("y_r", j))
                    y_ready[4 + j] = list(split_into(
                        x_hi[:, 4 + j, TOK], x_lo[:, 4 + j, TOK], y_r[:, j, :],
                        after=[done_["y_r", j], read]))
            tasks.append(split_retained())
            operand = lambda k: (x_hi[:, k, TOK], x_lo[:, k, TOK], y_ready[k])
            for m in range(KT):
                b, done = project("w_out", layer * KT + m, KT, operand, k_range=(0, KT // 2))
                z = dve.do(lambda: nc.vector.scalar_tensor_tensor(
                    x[:, m, TOK], x[:, m, TOK], ALPHA, bank(b), ALU.mult, ALU.add),
                    after=[done, *x_ready[m]])
                release_banks(b, 1, [z])
                x_ready[m] = [z]
            run_tasks()
            residual, mean = residual_tokens(1.0)
            for m in range(KT):
                residual(m, *project("w_out", layer * KT + m, KT, operand,
                                     k_range=(KT // 2, KT)))
            own.close()
            region_ends()
            layer_norm_x(f"ln2_g{layer}", f"ln2_b{layer}", 0, mean)

        def squares_task(stats, m, z, x_done):
            x_done[m] = [z]
            yield
            ((slot, sq, free),) = yield from slots_for(squares)
            done = act.do(lambda: nc.scalar.activation(sq[:], x[:, m, :], ACT.Square),
                          after=[z] + free)
            x_done[m] = [z, done]
            yield
            squares.free[slot] = [stats.add(sq, [done], m == KT - 1)]

        def residual_both(x_done):
            stats = Stats(1, True, take_banks())

            def residual(m, b, done):
                z = dve.do(lambda: nc.vector.scalar_tensor_tensor(
                    halves(x[:, m, :]), two_halves(b), 0.5, halves(x[:, m, :]),
                    ALU.mult, ALU.add), after=[done, *x_done[m]])
                release_banks(b, 2, [z])
                tasks.append(squares_task(stats, m, z, x_done))
            return residual, stats

        prepared = {}

        def bias_setup():
            ((hot_slot, hot, _), (rows_slot, rows, _)) = yield from slots_for(squares, 2)
            ((cut_slot, cut, cut_free),) = yield from slots_for(scratch)
            hot, rows = hot[0:BUCKETS, 0:REL_N], rows[0:8, 0:REL_N]
            table, cut = cut[0:BUCKETS, REL_N:REL_N + 8], cut[0:8, 0:REL_N]
            hot_loaded = load(pool, "hot", hot, t["distance_hot"])
            bias_loaded = load(pool, "rel_bias", table, t["rel_bias"], after=cut_free)
            cut_loaded = load(pool, "cut", cut, t["distance_mask"])
            yield
            yield
            b, free = yield from banks_for()
            looked = pe.do(lambda: nc.tensor.matmul(
                psum[0:8, b, 0:REL_N], table, hot, start=True, stop=True),
                after=[hot_loaded, bias_loaded] + free)
            far = dve.do(lambda: nc.vector.tensor_copy(lam[0:8, 0:1], psum[0:8, b, 0:1]),
                         after=[looked])
            relative = dve.do(lambda: nc.vector.tensor_scalar(
                rows, psum[0:8, b, 0:REL_N], lam[0:8, 0:1], None, ALU.subtract), after=[far])
            release_banks(b, 1, [relative])
            causal = dve.do(lambda: nc.vector.tensor_tensor(rows, rows, cut, ALU.add),
                            after=[relative, cut_loaded])
            rows_stored = load(pool, "rows_stored", t["bias_rows"], rows, after=[causal])
            prepared["rows_stored"] = rows_stored
            squares.free[hot_slot] = [looked]
            squares.free[rows_slot] = [rows_stored]
            scratch.free[cut_slot] = [causal, looked]

            g0 = gain_at["lambda_q1"]
            multiplied = dve.do(lambda: nc.vector.tensor_tensor(
                lam[0:HD, 2:4], gains[0:HD, g0:g0 + 3:2], gains[0:HD, g0 + 1:g0 + 4:2],
                ALU.mult), after=[relative, gains_loaded])
            yield
            b, free = yield from banks_for()
            dotted = pe.do(lambda: nc.tensor.matmul(
                psum[:, b, 0:2], ones[0:HD, :], lam[0:HD, 2:4], start=True, stop=True),
                after=[multiplied, ones_set] + free)
            exped = act.do(lambda: nc.scalar.activation(lam[:, 4:6], psum[:, b, 0:2], ACT.Exp),
                           after=[dotted])
            release_banks(b, 1, [exped])
            lam_done = dve.do(lambda: nc.vector.tensor_tensor(
                lam[:, 6:7], lam[:, 5:6], lam[:, 4:5], ALU.subtract), after=[exped])
            prepared["lambda"] = dve.do(lambda: nc.vector.tensor_scalar(
                lam[:, 6:7], lam[:, 6:7], LAM_INIT, None, ALU.subtract), after=[lam_done])

        def mixer_2(x_done):
            own = ExitStack()
            tensor = lambda name, shape, dt=F32: own.enter_context(
                nc.sbuf_tensor("b2_" + name, shape, dt))
            entry = list(region_free)
            q_a = tensor("q_a", [P, A_HEADS, SEQ])
            k_a = tensor("k_a", [P, A_HEADS, LEN])
            v_a = tensor("v_a", [P, NB, A_HEADS, P])
            v_a_meta = tensor("v_a_meta", [META, A_HEADS, P])
            q_lat = tensor("q_lat", [P, B_HEADS, 2, SEQ])
            c_fm = tensor("c_fm", [P, 2, LEN])
            c_tm = tensor("c_tm", [P, NB, B_DC])
            c_tm_meta = tensor("c_tm_meta", [META, B_DC])
            q_i = tensor("q_i", [P, 4, SEQ])
            k_i = tensor("k_i", [P, LEN])
            w_i = tensor("w_i", [P, NB, IDX_HEADS])
            w_uk = tensor("w_uk", [P, B_HEADS * B_DC])
            w_uv = tensor("w_uv", [P, B_HEADS, 2, P])
            window = tensor("window", [P, A_HEADS + B_HEADS, WINDOW_2])
            rank = tensor("rank", [P, LEN])
            keep_at = [sum(META + P * (i + 1) for i in range(b)) for b in range(NB + 1)]
            keep = tensor("keep", [P, keep_at[NB]])
            attn_t = Slots([tensor(f"attn_t{i}", [P, NB + 1, P]) for i in range(2)])
            flip = tensor("flip", [P, P])
            edge = tensor("edge", [P, P])
            spare = [tensor(f"spare{i}", [P, LEN]) for i in range(2)]
            work = Slots([*scratch.bufs, *spare])
            work.free = [*scratch.free, list(entry), list(entry)]

            uk_loaded = load(act, "w_uk", w_uk[:], t["w_uk"], after=entry)
            uv_loaded = load(act, "w_uv", w_uv[:].rearrange("p h k d -> p (h k d)"), t["w_uv"])
            edge_loaded = load(act, "edge", edge[:], t["tables"][:, t["table_at"]["band"][0] + P:
                                                                 t["table_at"]["band"][1]])
            flip_loaded = load(act, "flip", flip[:], t["flip"])
            heads = A_HEADS + B_HEADS
            mirrored = q_lat[:].rearrange("p h k n -> p (h k n)")[:, 0:heads * WINDOW_2]
            mirrored_in = [load(act, f"mirrored{h}", mirrored[:, h * WINDOW_2:(h + 1) * WINDOW_2],
                                bass.AP(t["bias_rows"].tensor, h * REL_N,
                                        [[1, P], [1, WINDOW_2]]),
                                after=[prepared["rows_stored"]]) for h in range(heads)]
            done_ = {}

            def windows():
                for _ in range(2):
                    yield
                for h in range(0, heads, 2):
                    b, free = yield from banks_for()
                    done_["turned"] = pe.do(lambda: nc.tensor.matmul(
                        bank(b), flip[:], mirrored[:, h * WINDOW_2:(h + 2) * WINDOW_2],
                        start=True, stop=True), after=[*mirrored_in[h:h + 2], flip_loaded] + free)
                    copied = copy_psum(window[:, h:h + 2, :].rearrange("p h j -> p (h j)"),
                                       bank(b), [done_["turned"], *entry])
                    release_banks(b, 1, [copied])
                done_["window"] = copied

            at = [0]

            def next_tile(wide):
                out = project("b2_in", at[0], KT, all_operand if wide else tokens_operand, wide)
                at[0] += 1
                return out

            def evacuate(dst, out, free=()):
                wide = dst.shape[-1] == LEN
                copied = copy_psum(halves(dst) if wide else dst,
                                   two_halves(out[0]) if wide else bank(out[0]),
                                   [out[1], *entry, *free])
                release_banks(out[0], 2 if wide else 1, [copied])
                return copied

            def normalise(dst, roots, wide, g, spread):
                view = halves if wide else (lambda tile: tile)
                return dve.do(lambda: nc.vector.scalar_tensor_tensor(
                    view(dst), view(dst), g, roots, ALU.mult, ALU.mult),
                    after=[spread, gains_loaded])

            def normed(dst, groups, wide, scale, g, key, after, factor=1.0):
                cols = slice(0, LEN if wide else SEQ)
                offset = 0 if wide else META
                stats, square = yield from squared(groups, wide, dst,
                                                   slice(offset, LEN), after)
                yield
                stats.add(*square, True)
                stats.root(scale, 1, factor)
                yield
                banks = yield from banks_for(2 if wide else 1)
                roots, spread = stats.spread(banks)
                done_[key] = normalise(dst[:, cols], roots, wide, g, spread)
                stats.release([done_[key]])

            def keys(b):
                return META + P * (b + 1)

            def bank_parts(n):
                return [(0, min(n, 512))] + ([(512, n)] if n > 512 else [])

            def two_banks(b, n):
                return psum[:, b:b + 2, :].rearrange("p b n -> p (b n)")[:, 0:n] if n > 512 \
                    else psum[:, b, 0:n]

            def indexer(b):
                n = keys(b)
                width = 2 if n > 512 else 1
                own_cols = slice(n - P, n)
                acc = None
                yield from made(done_, *(("q_i", j) for j in range(4)), "k_i", "w_i")
                for h in range(IDX_HEADS):
                    rows = slice(HD * (h % 2), HD * (h % 2 + 1))
                    ((slot, pos, pfree),) = yield from slots_for(work)
                    wb, free = yield from banks_for(width)
                    for c0, c1 in bank_parts(n):
                        dots = pe.do(lambda: nc.tensor.matmul(
                            psum[:, wb + c0 // 512, 0:c1 - c0],
                            q_i[rows, h // 2, b * P:(b + 1) * P], k_i[rows, c0:c1],
                            start=True, stop=True),
                            after=[done_["q_i", h // 2], done_["k_i"]] + free)
                    positive = act.do(lambda: nc.scalar.activation(
                        pos[:, 0:n], two_banks(wb, n), ACT.Relu, scale=HD ** -0.5),
                        after=[dots] + pfree)
                    release_banks(wb, width, [positive])
                    weight = w_i[:, b, h:h + 1]
                    if h == 0:
                        acc = dve.do(lambda: nc.vector.tensor_scalar(
                            rank[:, 0:n], pos[:, 0:n], weight, None, ALU.mult),
                            after=[positive, done_["w_i"],
                                   *([done_["kept", b - 1]] if b else entry)])
                    else:
                        acc = dve.do(lambda: nc.vector.scalar_tensor_tensor(
                            rank[:, 0:n], pos[:, 0:n], weight, rank[:, 0:n],
                            ALU.mult, ALU.add), after=[positive, acc])
                    work.free[slot] = [acc]
                    if h % 2:
                        yield
                done_["scored", b] = dots
                acc = dve.do(lambda: nc.vector.tensor_tensor(
                    rank[:, own_cols], rank[:, own_cols], edge[:], ALU.add),
                    after=[acc, edge_loaded])
                ((slot, best, bfree),) = yield from slots_for(small)
                for i in range(TOPK // 8):
                    found = dve.do(lambda: nc.vector.max(best[:, 0:8], rank[:, 0:n]),
                                   after=[acc] + bfree)
                    acc = dve.do(lambda: nc.vector.match_replace(
                        rank[:, 0:n], best[:, 0:8], rank[:, 0:n], -2.0 * BIG), after=[found])
                    if i % 3 == 2:
                        yield
                small.free[slot] = [acc]
                done_["kept", b] = dve.do(lambda: nc.vector.tensor_scalar(
                    keep[:, keep_at[b]:keep_at[b + 1]], rank[:, 0:n], -2.0 * BIG, -BIG,
                    ALU.not_equal, ALU.mult), after=[acc, *entry])
                yield

            def weights_t(tile, n, after):
                ((slot, out, free),) = yield from slots_for(attn_t)
                blocks = (n - META) // P
                sources = [(tile[:, META + P * j:META + P * (j + 1)], P, P)
                           for j in range(blocks)]
                meta_in = (tile[:, MET], P, META)
                banks = yield from banks_for()
                if blocks < 4:
                    copied, read = transposed(
                        banks, sources + [meta_in],
                        [(out[:, 0:blocks, :].rearrange("p n q -> p (n q)"), slice(0, P),
                          slice(0, blocks * P)),
                         (out[0:META, NB, :], slice(0, META),
                          slice(blocks * P, (blocks + 1) * P))], after, [*entry, *free])
                else:
                    transposed(banks, sources,
                               [(out[:, 0:blocks, :].rearrange("p n q -> p (n q)"),
                                 slice(0, P), slice(0, blocks * P))], after, [*entry, *free])
                    banks = yield from banks_for()
                    copied, read = transposed(banks, [meta_in],
                                              [(out[0:META, NB, :], slice(0, META),
                                                slice(0, P))], after, [])
                return slot, out, copied, read

            def top(s, n, st, ready_, free):
                found = dve.do(lambda: nc.vector.tensor_reduce(
                    st[:, 0:1], s[:, 0:n], AX.X, ALU.max), after=[ready_] + free)
                return dve.do(lambda: nc.vector.tensor_scalar(
                    st[:, 0:1], st[:, 0:1], -1.0, None, ALU.mult), after=[found])

            def exponentials(s, n, st, negated):
                return act.do(lambda: nc.scalar.activation(
                    s[:, 0:n], s[:, 0:n], ACT.Exp, bias=st[:, 0:1], accum_out=st[:, 1:2]),
                    after=[negated])

            def inverse_sum(st, exped):
                return dve.do(lambda: nc.vector.reciprocal(st[:, 1:2], st[:, 1:2]),
                              after=[exped])

            def latent_attention(items):
                yield from made(done_, "window", "c", ("c_tm", 0), ("c_tm", 1))
                for b, h in items:
                    yield from made(done_, ("q_lat", h, 0), ("q_lat", h, 1), ("kept", b))
                    n = keys(b)
                    width = 2 if n > 512 else 1
                    w0 = max(n - WINDOW_2, 0)
                    ((slot, s, sfree),) = yield from slots_for(work)
                    ((st_slot, st, st_free),) = yield from slots_for(small)
                    wb, free = yield from banks_for(width)
                    for c0, c1 in bank_parts(n):
                        for k in range(2):
                            done = pe.do(lambda: nc.tensor.matmul(
                                psum[:, wb + c0 // 512, 0:c1 - c0],
                                q_lat[:, h, k, b * P:(b + 1) * P], c_fm[:, k, c0:c1],
                                start=k == 0, stop=k == 1),
                                after=[done_["q_lat", h, k], done_["c", k]] + free)
                    masked = dve.do(lambda: nc.vector.scalar_tensor_tensor(
                        s[:, 0:n], two_banks(wb, n), B_DC ** -0.5,
                        keep[:, keep_at[b]:keep_at[b + 1]], ALU.mult, ALU.add),
                        after=[done, done_["kept", b]] + sfree)
                    release_banks(wb, width, [masked])
                    biased = dve.do(lambda: nc.vector.tensor_tensor(
                        s[:, w0:n], s[:, w0:n], window[:, A_HEADS + h, WINDOW_2 - (n - w0):],
                        ALU.add), after=[masked, done_["window"]])
                    exped = exponentials(s, n, st, top(s, n, st, biased, st_free))
                    yield
                    inverse = inverse_sum(st, exped)
                    ready_ = dve.do(lambda: nc.vector.tensor_scalar(
                        s[:, 0:n], s[:, 0:n], st[:, 1:2], None, ALU.mult), after=[inverse])
                    small.free[st_slot] = [ready_]
                    yield
                    aslot, a_t, copied, read = yield from weights_t(s, n, [ready_])
                    yield
                    blocks = (n - META) // P
                    wb, free = yield from banks_for()
                    for k in range(2):
                        cols = slice(k * P, (k + 1) * P)
                        for j in range(blocks):
                            pe.do(lambda: nc.tensor.matmul(
                                psum[:, wb, cols], c_tm[:, j, cols], a_t[:, j, :],
                                start=j == 0, stop=False),
                                after=[copied, done_["c_tm", k]] + free, mark=False)
                        done = pe.do(lambda: nc.tensor.matmul(
                            psum[:, wb, cols], c_tm_meta[:, cols], a_t[0:META, NB, :],
                            start=False, stop=True))
                    attn_t.free[aslot] = [done]
                    latent = copy_psum(s[:, 0:2 * P], psum[:, wb, 0:2 * P], [done, read])
                    release_banks(wb, 1, [latent])
                    yield
                    wb, free = yield from banks_for()
                    for k in range(2):
                        done = pe.do(lambda: nc.tensor.matmul(
                            psum[:, wb, 0:P], w_uv[:, h, k, :], s[:, k * P:(k + 1) * P],
                            start=k == 0, stop=k == 1), after=[latent, uv_loaded] + free)
                    work.free[slot] = [done]
                    done_["y_b", b, h] = copy_psum(
                        q_i[:, h, b * P:(b + 1) * P], psum[:, wb, 0:P],
                        [done, done_["scored", b]])
                    release_banks(wb, 1, [done_["y_b", b, h]])

            def differential(items):
                yield from made(done_, "window")
                for b, h in items:
                    yield from made(done_, ("q_a", h), ("k_a", h), ("v_a", h))
                    n = keys(b)
                    width = 2 if n > 512 else 1
                    w0 = max(n - WINDOW_2, 0)
                    (slot0, s0, free0), (slot1, s1, free1) = yield from slots_for(work, 2)
                    (st_slot0, st0, st_free0), (st_slot1, st1, st_free1) = \
                        yield from slots_for(small, 2)
                    exped = []
                    for m, s, sfree, st, st_free in ((0, s0, free0, st0, st_free0),
                                                     (1, s1, free1, st1, st_free1)):
                        rows = slice(HD * m, HD * (m + 1))
                        wb, free = yield from banks_for(width)
                        for c0, c1 in bank_parts(n):
                            done = pe.do(lambda: nc.tensor.matmul(
                                psum[:, wb + c0 // 512, 0:c1 - c0],
                                q_a[rows, h, b * P:(b + 1) * P], k_a[rows, h, c0:c1],
                                start=True, stop=True),
                                after=[done_["q_a", h], done_["k_a", h]] + free)
                        view = two_banks(wb, n)
                        after = [done, done_["window"]] + sfree
                        if w0:
                            after.append(act.do(lambda: nc.scalar.mul(
                                s[:, 0:w0], view[:, 0:w0], HD ** -0.5), after=[done] + sfree))
                        biased = dve.do(lambda: nc.vector.scalar_tensor_tensor(
                            s[:, w0:n], view[:, w0:n], HD ** -0.5,
                            window[:, h, WINDOW_2 - (n - w0):], ALU.mult, ALU.add),
                            after=after)
                        release_banks(wb, width, [biased])
                        exped.append(exponentials(s, n, st, top(s, n, st, biased, st_free)))
                        yield
                    inv0, inv1 = inverse_sum(st0, exped[0]), inverse_sum(st1, exped[1])
                    factor = dve.do(lambda: nc.vector.tensor_tensor(
                        st1[:, 1:2], st1[:, 1:2], lam[:, 6:7], ALU.mult),
                        after=[inv1, prepared["lambda"]])
                    second = dve.do(lambda: nc.vector.tensor_scalar(
                        s1[:, 0:n], s1[:, 0:n], st1[:, 1:2], None, ALU.mult), after=[factor])
                    ready_ = dve.do(lambda: nc.vector.scalar_tensor_tensor(
                        s0[:, 0:n], s0[:, 0:n], st0[:, 1:2], s1[:, 0:n], ALU.mult, ALU.add),
                        after=[inv0, second])
                    small.free[st_slot0] = small.free[st_slot1] = [ready_]
                    work.free[slot1] = [ready_]
                    yield
                    aslot, a_t, copied, read = yield from weights_t(s0, n, [ready_])
                    work.free[slot0] = [read]
                    yield
                    blocks = (n - META) // P
                    wb, free = yield from banks_for()
                    for j in range(blocks):
                        pe.do(lambda: nc.tensor.matmul(
                            psum[:, wb, 0:P], v_a[:, j, h, :], a_t[:, j, :],
                            start=j == 0, stop=False), after=[copied, done_["v_a", h]] + free,
                            mark=False)
                    done = pe.do(lambda: nc.tensor.matmul(
                        psum[:, wb, 0:P], v_a_meta[:, h, :], a_t[0:META, NB, :],
                        start=False, stop=True))
                    attn_t.free[aslot] = [done]
                    done_["y_a", b, h] = copy_psum(q_a[:, h, b * P:(b + 1) * P],
                                                   psum[:, wb, 0:P], [done])
                    release_banks(wb, 1, [done_["y_a", b, h]])

            def head_weights(b, done):
                ((slot, raw, free),) = yield from slots_for(work)
                copied = evacuate(raw[:, 0:SEQ], (b, done), free)
                yield
                wb, wfree = yield from banks_for()
                for j in range(NB):
                    turned = pe.do(lambda: nc.tensor.transpose(
                        psum[:, wb, j * IDX_HEADS:(j + 1) * IDX_HEADS],
                        raw[0:IDX_HEADS, j * P:(j + 1) * P], ident[0:IDX_HEADS, 0:IDX_HEADS]),
                        after=[copied] + wfree)
                work.free[slot] = [turned]
                done_["w_i"] = act.do(lambda: nc.scalar.mul(
                    w_i[:].rearrange("p n h -> p (n h)"), psum[:, wb, 0:NB * IDX_HEADS],
                    IDX_HEADS ** -0.5), after=[turned, *entry])
                release_banks(wb, 1, [done_["w_i"]])

            def selection():
                for b in range(NB):
                    yield from indexer(b)

            def latent_c(copied):
                banks = yield from banks_for()
                stats = Stats(1, True, banks)
                for k in range(2):
                    ((slot, sq, free),) = yield from slots_for(squares)
                    done = act.do(lambda: nc.scalar.activation(sq[:], c_fm[:, k, :], ACT.Square),
                                  after=[copied[k]] + free)
                    yield
                    squares.free[slot] = [stats.add(sq, [done], k == 1)]
                stats.root(1.0 / B_DC, 1)
                yield
                banks = yield from banks_for(2)
                roots, spread = stats.spread(banks)
                for k in range(2):
                    done_["c", k] = normalise(c_fm[:, k, :], roots, True, gain("b_kv_norm", k),
                                              spread)
                stats.release([done_["c", 0], done_["c", 1]])
                done_["c"] = done_["c", 1]
                for k in range(2):
                    yield
                    cols = slice(k * P, (k + 1) * P)
                    banks = yield from banks_for()
                    transposed(banks, [(c_fm[:, k, META + P * j:META + P * (j + 1)], P, P)
                                       for j in range(NB)],
                               [(c_tm[:, :, cols], slice(0, P), slice(0, SEQ))],
                               [done_["c", k]], entry)
                    banks = yield from banks_for()
                    done_["c_tm", k], _ = transposed(
                        banks, [(c_fm[:, k, MET], P, META)],
                        [(c_tm_meta[:, cols], slice(0, META), slice(0, P))],
                        [done_["c", k]], entry)

            def latent_query(h, b, done):
                ((slot, raw, free),) = yield from slots_for(work)
                copied = evacuate(raw[:, 0:SEQ], (b, done), free)
                yield from made(done_, "turned")
                yield
                banks = yield from banks_for()
                stats = Stats(1, False, banks)
                square = []
                for k in range(2):
                    wb, wfree = yield from banks_for()
                    multiplied = pe.do(lambda: nc.tensor.matmul(
                        bank(wb), w_uk[:, h * B_DC + k * P:h * B_DC + (k + 1) * P],
                        raw[:, 0:SEQ], start=True, stop=True), after=[copied, uk_loaded] + wfree)
                    moved = copy_psum(q_lat[:, h, k, :], bank(wb),
                                      [multiplied, done_["turned"], *entry])
                    release_banks(wb, 1, [moved])
                    ((sq_slot, sq, free),) = yield from slots_for(squares)
                    squared_ = act.do(lambda: nc.scalar.activation(
                        sq[:, TOK], q_lat[:, h, k, :], ACT.Square), after=[moved] + free)
                    yield
                    squares.free[sq_slot] = [stats.add(sq, [squared_], k == 1)]
                work.free[slot] = [multiplied]
                stats.root(1.0 / B_DC, 1)
                yield
                banks = yield from banks_for()
                roots, spread = stats.spread(banks)
                for k in range(2):
                    done_["q_lat", h, k] = normalise(q_lat[:, h, k, :], roots, False,
                                                     gain("b_q_norm", k), spread)
                stats.release([done_["q_lat", h, 0], done_["q_lat", h, 1]])

            def values_token_major(h, b, done):
                ((slot, raw, free),) = yield from slots_for(work)
                copied = evacuate(raw, (b, done), free)
                yield
                banks = yield from banks_for()
                transposed(banks, [(raw[:, META + P * j:META + P * (j + 1)], P, P)
                                   for j in range(NB)],
                           [(v_a[:, :, h, :], slice(0, P), slice(0, SEQ))], [copied], entry)
                banks = yield from banks_for()
                done_["v_a", h], read = transposed(
                    banks, [(raw[:, MET], P, META)],
                    [(v_a_meta[:, h, :], slice(0, META), slice(0, P))], [copied], entry)
                work.free[slot] = [read]

            tasks.append(windows())
            group = project_group([("b2_in", i) for i in range(GROUP)], tokens_operand)
            at[0] = GROUP
            for j in range(4):
                done_["q_i", j] = evacuate(q_i[:, j, :],
                                           group[j] if j < GROUP else next_tile(False))
            done_["k_i"] = evacuate(k_i[:], next_tile(True))
            tasks.append(head_weights(*next_tile(False)))
            tasks.append(selection())
            order = iter([(b, h) for h in range(A_HEADS) for b in range(NB)])
            tasks.extend(differential(order) for _ in range(2))
            for h in range(A_HEADS):
                copied = evacuate(q_a[:, h, :], next_tile(False))
                tasks.append(normed(q_a[:, h, :], 2, False, 1.0 / HD, gain("a_q_norm"),
                                    ("q_a", h), copied))
                copied = evacuate(k_a[:, h, :], next_tile(True))
                tasks.append(normed(k_a[:, h, :], 2, True, 1.0 / HD, gain("a_k_norm"),
                                    ("k_a", h), copied))
                tasks.append(values_token_major(h, *next_tile(True)))
            tasks.append(latent_c([evacuate(c_fm[:, k, :], next_tile(True)) for k in range(2)]))
            order = iter([(b, h) for b in range(NB) for h in range(B_HEADS)])
            tasks.extend(latent_attention(order) for _ in range(3))
            for h in range(B_HEADS):
                tasks.append(latent_query(h, *next_tile(False)))

            read = piece_read[-1]
            y_ready = [None] * KT

            def differential_output(h):
                yield from made(done_, *(("y_a", b, h) for b in range(NB)))
                yield from normed(q_a[:, h, :], 1, False, 1.0 / P, gain("a_subln"),
                                  ("o_a", h), done_["y_a", NB - 1, h], 1.0 - LAM_INIT)
                y_ready[h] = list(split_into(x_hi[:, h, TOK], x_lo[:, h, TOK], q_a[:, h, :],
                                             after=[done_["o_a", h], read]))

            tasks.extend(differential_output(h) for h in range(A_HEADS))
            run_tasks(lambda: all(y_ready[h] for h in range(A_HEADS)))
            operand = lambda k: (x_hi[:, k, TOK], x_lo[:, k, TOK], y_ready[k])

            def add_to_x(m, b, done):
                z = dve.do(lambda: nc.vector.tensor_tensor(
                    x[:, m, TOK], x[:, m, TOK], bank(b), ALU.add), after=[done, *x_done[m]])
                release_banks(b, 1, [z])
                x_done[m] = [z]
                return z
            for m in range(KT):
                add_to_x(m, *project("b2_out", m, KT, operand, k_range=(0, KT // 2)))
            run_tasks()
            for h in range(B_HEADS):
                y_ready[4 + h] = list(split_into(
                    x_hi[:, 4 + h, TOK], x_lo[:, 4 + h, TOK], q_i[:, h, :],
                    after=[*(done_["y_b", b, h] for b in range(NB)), read]))
            stats = Stats(1, True, take_banks())
            for m in range(KT):
                z = add_to_x(m, *project("b2_out", m, KT, operand, k_range=(KT // 2, KT)))
                tasks.append(squares_task(stats, m, z, x_done))
            run_tasks()
            for i in range(4):
                scratch.free[i] = work.free[i]
            own.close()
            region_ends()
            return stats

        def block_2():
            x_done = [list(x_ready[k]) + [meta_loaded] for k in range(KT)]
            stats = Stats(1, True, take_banks())
            for k in range(KT):
                square_into(stats, x[:, k, :], slice(0, LEN), x_done[k], k == KT - 1)
            rms_norm_x("ffn1_norm", x_done, stats)
            residual, stats = residual_both(x_done)
            ffn(("b2_gate1", 0), ("b2_up1", 0), ("b2_down1", 0), True, residual)
            rms_norm_x("mix_norm", x_done, stats)
            stats = mixer_2(x_done)
            rms_norm_x("ffn2_norm", x_done, stats)

            def residual(m, b, done):
                z = dve.do(lambda: nc.vector.scalar_tensor_tensor(
                    x[:, m, TOK], bank(b), 0.5, x[:, m, TOK], ALU.mult, ALU.add),
                    after=[done, *x_done[m]])
                release_banks(b, 1, [z])
                x_done[m] = [z]
            ffn(("b2_gate2", 0), ("b2_up2", 0), ("b2_down2", 0), False, residual)
            for k in range(KT):
                x_ready[k] = x_done[k]
        stream_until(0)
        x_rows = t["x"].rearrange("(k p) n -> p k n", p=P)
        x_loaded = [load(sp, f"x{k}", x[:, k, TOK], x_rows[:, k, :]) for k in range(KT)]
        for k in range(KT):
            x_ready[k] = [x_loaded[k]]
            ready[k] = list(split_into(x_hi[:, k, TOK], x_lo[:, k, TOK], x[:, k, TOK],
                                       after=[x_loaded[k]]))
        tasks.append(bias_setup())
        for layer in range(DEPTH):
            residual, mean = residual_tokens(2.0 * ALPHA)
            ffn(("ffn1_gu", layer * 2 * FT), ("ffn1_gu", layer * 2 * FT + FT),
                ("ffn1_down", layer * KT), False, residual,
                group=GROUP if layer else 1)
            layer_norm_x(f"ln1_g{layer}", f"ln1_b{layer}", 2, mean)
            mixer_1(layer)
            residual, mean = residual_tokens(2.0 * ALPHA)
            ffn(("ffn2_gu", layer * 2 * FT), ("ffn2_gu", layer * 2 * FT + FT),
                ("ffn2_down", layer * KT), False, residual)
            layer_norm_x(f"ln3_g{layer}", f"ln3_b{layer}", 2, mean)
        block_2()
        out_sem = sem("out_stored")
        for k in range(KT):
            stored = sp.dma(out_sem, 16 * (k + 1), lambda k=k: nc.sync.dma_start(
                t["out"][k * P:(k + 1) * P, :], x[:, k, TOK]), after=x_ready[k])
        sp.wait([stored])



def weight_plan():
    plan = []

    def ffn(gate, up, down):
        for f in range(FT):
            plan.extend(pieces(gate[0], gate[1] + f, KT))
            plan.extend(pieces(up[0], up[1] + f, KT))
        for m in range(KT):
            plan.extend(pieces(down[0], down[1] + m, FT))

    def matrix(name, first, n):
        for m in range(n):
            plan.extend(pieces(name, first + m, KT))

    def halves(name, first):
        for k in (0, KT // 2):
            for m in range(KT):
                plan.extend(pieces(name, first + m, KT // 2, k))

    for layer in range(DEPTH):
        ffn(("ffn1_gu", layer * 2 * FT), ("ffn1_gu", layer * 2 * FT + FT),
            ("ffn1_down", layer * KT))
        matrix("w_in", layer * IN_TILES_1, IN_TILES_1)
        halves("w_out", layer * KT)
        ffn(("ffn2_gu", layer * 2 * FT), ("ffn2_gu", layer * 2 * FT + FT),
            ("ffn2_down", layer * KT))
    ffn(("b2_gate1", 0), ("b2_up1", 0), ("b2_down1", 0))
    matrix("b2_in", 0, IN_TILES_2)
    halves("b2_out", 0)
    ffn(("b2_gate2", 0), ("b2_up2", 0), ("b2_down2", 0))
    return plan


def column_tiles(w):
    k, n = w.shape
    return np.ascontiguousarray(
        w.reshape(k // P, P, n // P, P).transpose(2, 1, 0, 3).reshape(n // P, P, k))


def head_pairs(w, axis):
    order = [h for j in range(HEADS // 2) for h in (j, HEADS // 2 + j)]
    shape = w.shape
    w = w.reshape(shape[:axis] + (HEADS, HD) + shape[axis + 1:])
    return np.take(w, order, axis=axis).reshape(shape)


def shape_tables():
    f = np.float32
    pos = np.arange(SEQ, dtype=f)
    freq_a = f(10000.0) ** (-np.arange(0, HD, 2, dtype=f) / f(HD))
    freq_r = f(1.0) / (f(10000.0) ** np.linspace(0.0, 1.0, HD // 2, dtype=f))
    ang_a, ang_r = pos[:, None] * freq_a[None], pos[:, None] * freq_r[None]
    row = np.arange(P) % HD
    at_a, at_r = row % (HD // 2), row // 2
    log_gamma = np.log1p(-np.exp2(f(-5.0) - np.arange(HEADS, dtype=f))).astype(f)
    idx = np.arange(P, dtype=f)
    diff = idx[:, None] - idx[None, :]
    decay = np.where(diff[None] >= 0,
                     np.exp(np.maximum(diff, 0)[None] * log_gamma[:, None, None]), 0).astype(f)
    w_k = np.exp((f(P) - 1 - idx)[None] * log_gamma[:, None]).astype(f)
    w_q = np.exp((idx + 1)[None] * log_gamma[:, None]).astype(f)
    g_chunk = np.exp(f(P) * log_gamma).astype(f)
    rot_a, rot_r = np.zeros((P, P), f), np.zeros((P, P), f)
    for m in range(P):
        rot_a[m + 32 if m % HD < 32 else m - 32, m] = -1 if m % HD < 32 else 1
        rot_r[m ^ 1, m] = -1 if m % 2 == 0 else 1
    q = np.arange(P)[:, None]
    rel = q - (np.arange(2 * P)[None] - P)
    parts = {
        "cos_a": np.cos(ang_a)[:, at_a].T, "sin_a": np.sin(ang_a)[:, at_a].T,
        "cos_r": np.cos(ang_r)[:, at_r].T, "sin_r": np.sin(ang_r)[:, at_r].T,
        "decay": decay.transpose(2, 0, 1).reshape(P, HEADS * P),
        "w_q": np.stack([np.repeat(w_q[2 * j:2 * j + 2], HD, axis=0) for j in range(4)], 1)
        .reshape(P, 4 * P),
        "w_k": np.repeat(w_k.T, HD, axis=1),
        "g_chunk": np.stack([np.repeat(g_chunk[2 * j:2 * j + 2], HD) for j in range(4)], 1),
        "band": np.where((rel >= 0) & (rel < P), 0.0, -BIG),
        "rot_a": rot_a, "rot_r": rot_r,
    }
    at, cols, n = {}, [], 0
    for name, v in parts.items():
        at[name] = (n, n + v.shape[1])
        n += v.shape[1]
        cols.append(v.astype(f))
    return np.ascontiguousarray(np.concatenate(cols, 1)), at


WINDOW_2 = 2 * P
REL_N = 3 * P - 1


def distance_buckets():
    f = np.float32
    n = 255 - np.arange(REL_N)
    nf = np.maximum(n, 1).astype(f)
    large = 16 + (np.log(nf / f(16)) / f(np.log(8.0)) * f(16)).astype(np.int32)
    bucket = np.where(n < 16, n, np.minimum(large, BUCKETS - 1))
    assert bucket[0] == BUCKETS - 1 and bucket[255 - (P + 1)] == BUCKETS - 1
    hot = np.zeros((BUCKETS, REL_N), f)
    for i in range(REL_N):
        if n[i] >= 0:
            hot[bucket[i], i] = 1
    return hot, np.broadcast_to(np.where(n >= 0, 0.0, -BIG).astype(f), (8, REL_N)).copy()


def kernel(**inputs):
    from concourse import bacc
    from concourse.bass_utils import run_bass_kernel_spmd

    v = {k: np.asarray(a) for k, a in inputs.items()}
    arrays = {}

    arrays["x"] = np.ascontiguousarray(v["x"][0].T)
    arrays["meta"] = np.ascontiguousarray(v["meta_tokens_2"].T)

    def stacked(name, per_layer):
        return np.concatenate([column_tiles(per_layer(w)) for w in v[name]], 0)

    aw, kw = HEADS * HD, 2 * HD
    cuts = np.cumsum([aw, kw, kw, 512, 512, 512])

    def in_1(w):
        qa, ka, va, qr, kr, vr, gr = np.split(w, cuts, axis=1)
        tiles = [head_pairs(qa, 1), ka, va]
        for j in range(4):
            tiles += [a[:, j * P:(j + 1) * P] for a in (qr, kr, vr)]
        return np.concatenate(tiles + [gr], 1)

    def in_2(w):
        qa, ka, va, qb, ckv, iq, ik, iw = np.split(
            w, np.cumsum([512, 512, 512, 512, 256, 512, 64]), axis=1)
        heads = [a[:, h * P:(h + 1) * P] for h in range(A_HEADS) for a in (qa, ka, va)]
        return np.concatenate([iq, ik, ik, np.tile(iw, (1, P // IDX_HEADS)), *heads,
                               ckv, qb], 1)

    same = lambda w: w
    arrays["w_in"] = stacked("w_in", in_1)
    arrays["w_out"] = stacked("w_out", lambda w: np.concatenate(
        [head_pairs(w[:aw], 0), w[aw:]], 0))
    for name in ("ffn1", "ffn2"):
        arrays[name + "_gu"] = stacked(name + "_w_gu", same)
        arrays[name + "_down"] = stacked(name + "_w_down", same)
    arrays["b2_in"] = stacked("w_in_2", in_2)
    arrays["b2_out"] = stacked("w_out_2", same)
    for i in "12":
        arrays["b2_gate" + i] = stacked(f"ffn{i}_w_gate_2", same)
        arrays["b2_up" + i] = stacked(f"ffn{i}_w_up_2", same)
        arrays["b2_down" + i] = stacked(f"ffn{i}_w_down_2", same)
    arrays["w_uk"] = np.ascontiguousarray(
        v["b_w_uk_2"][0].transpose(1, 0, 2).reshape(P, B_HEADS * B_DC))
    arrays["w_uv"] = np.ascontiguousarray(
        v["b_w_uv_2"][0].reshape(B_HEADS, 2, P, P).transpose(2, 0, 1, 3).reshape(P, -1))
    arrays["rel_bias"] = np.ascontiguousarray(v["rel_bias_2"])

    gain_at, cols = {}, []

    def column(name, a):
        gain_at[name] = sum(c.shape[1] for c in cols)
        cols.append(np.ascontiguousarray(a))

    for layer in range(DEPTH):
        for n in "123":
            column(f"ln{n}_g{layer}", v[f"ln{n}_g"][layer].reshape(KT, P).T)
            column(f"ln{n}_b{layer}", v[f"ln{n}_b"][layer].reshape(KT, P).T)
        column(f"sinks{layer}", np.broadcast_to(
            v["attn_sinks"][layer][None], (P, HEADS)))
    for n in ("ffn1_norm", "mix_norm", "ffn2_norm"):
        column(n, v[n + "_2"][0].reshape(KT, P).T)
    for n in ("a_q_norm", "a_k_norm"):
        column(n, np.tile(v[n + "_2"][0], 2)[:, None])
    column("a_subln", v["a_subln_2"][0][:, None])
    for n in ("b_kv_norm", "b_q_norm"):
        column(n, v[n + "_2"][0].reshape(2, P).T)
    for n in ("q1", "k1", "q2", "k2"):
        column("lambda_" + n, np.tile(v[f"a_lambda_{n}_2"][0], 2)[:, None])
    arrays["gains"] = np.ascontiguousarray(np.concatenate(cols, 1))

    arrays["ident"] = np.eye(P, dtype=np.float32)
    arrays["flip"] = np.eye(P, dtype=np.float32)[::-1].copy()
    arrays["half"] = np.kron(np.eye(2, dtype=np.float32), np.ones((HD, HD), np.float32))
    arrays["tables"], table_at = shape_tables()
    arrays["distance_hot"], arrays["distance_mask"] = distance_buckets()

    nc = bacc.Bacc("TRN2", target_bir_lowering=False, num_devices=1)
    t = {"gain_at": gain_at, "table_at": table_at}
    feed = {}
    for name, a in arrays.items():
        feed["in_" + name] = a
        t[name] = nc.dram_tensor("in_" + name, a.shape, F32, kind="ExternalInput").ap()
    t["out"] = nc.dram_tensor("out", (D, SEQ), F32, kind="ExternalOutput").ap()
    t["bias_rows"] = nc.dram_tensor("bias_rows", (8, REL_N), F32, kind="Internal").ap()
    build(nc, t)
    result = run_bass_kernel_spmd(nc, [feed], core_ids=[0]).results[0]["out"]
    return np.ascontiguousarray(np.asarray(result).T)[None]
```

```python
from contextlib import ExitStack

import numpy as np

import concourse.bass as bass
from concourse import mybir

F32 = mybir.dt.float32
F32R = mybir.dt.float32r
ALU = mybir.AluOpType
ACT = mybir.ActivationFunctionType
AX = mybir.AxisListType

P = 128
BIG = 1.0e30

SEQ = 512
META = 16
LEN = META + SEQ
TOK = slice(META, LEN)
MET = slice(0, META)
HALF = LEN // 2
D = 1024
KT = D // P
DEPTH = 2
D_FF = 2816
FT = D_FF // P
HD = 64
NB = SEQ // P
ALPHA = (2 * DEPTH) ** 0.25
LN_EPS = 1e-5
GN_EPS = 1e-6
RMS_EPS = 1e-6
HEADS = 8
IN_TILES_1 = 22
IN_TILES_2 = 24
A_HEADS = 4
B_HEADS = 4
B_DC = 256
IDX_HEADS = 8
TOPK = 128
BUCKETS = 32
LAM_INIT = 0.2

RAW_SLOTS = 3
SPLIT_SLOTS = 4
AHEAD = 3
LANES_A = 3
LANES_B = 6
DIRECT_SQUARES = 6
SPARE = 4
TURNED = 2
LEAD = 3
CENTRED = 3
ROUNDS = 4
GROUP = 3
PIECE = 8


class Done:

    def __init__(self, sem, value):
        self.sem, self.value = sem, value


class Engine:

    def __init__(self, eng, sem):
        self.eng, self.sem, self.count, self.seen = eng, sem, 0, {}

    def wait(self, after):
        for d in after:
            if d is None or self.seen.get(id(d.sem), 0) >= d.value:
                continue
            self.seen[id(d.sem)] = d.value
            self.eng.wait_ge(d.sem, d.value)

    def do(self, issue, after=(), mark=True):
        self.wait(after)
        instruction = issue()
        if not mark:
            return None
        self.count += 1
        instruction.then_inc(self.sem, 1)
        return Done(self.sem, self.count)

    def dma(self, sem, total, issue, after=()):
        self.wait(after)
        issue().then_inc(sem, 16)
        return Done(sem, total)


class Slots:

    def __init__(self, bufs):
        self.bufs, self.free, self.next = bufs, [[] for _ in bufs], 0

    def take(self):
        n = len(self.bufs)
        i = next(j % n for j in range(self.next, self.next + n) if self.free[j % n] is not None)
        self.next = (i + 1) % n
        free, self.free[i] = self.free[i], None
        return i, self.bufs[i], free


def pieces(matrix, col_tile, tiles, first=0, lead=0):
    end = first + tiles
    head = [(matrix, col_tile, first, lead)] if lead else []
    return head + [(matrix, col_tile, k, min(PIECE, end - k))
                   for k in range(first + lead, end, PIECE)]


def down_lead(m):
    return LEAD if m == KT - 1 else 0


def build(nc, t):
    ctx = ExitStack()
    with ctx:
        sem = lambda name: ctx.enter_context(nc.semaphore(name))
        sb = lambda name, shape, dt=F32: ctx.enter_context(nc.sbuf_tensor(name, shape, dt))

        pe = Engine(nc.tensor, sem("pe_done"))
        act = Engine(nc.scalar, sem("act_done"))
        dve = Engine(nc.vector, sem("dve_done"))
        pool = Engine(nc.gpsimd, sem("pool_done"))
        sp = Engine(nc.sync, sem("sp_done"))

        x = sb("x", [P, KT, LEN])
        x_hi = sb("x_hi", [P, KT, LEN], F32R)
        x_lo = sb("x_lo", [P, KT, LEN], F32R)
        w_raw = [sb(f"w_raw{i}", [P, PIECE * P]) for i in range(RAW_SLOTS)]
        w_hi = [sb(f"w_hi{i}", [P, PIECE * P], F32R) for i in range(SPLIT_SLOTS)]
        w_lo = [sb(f"w_lo{i}", [P, PIECE * P], F32R) for i in range(SPLIT_SLOTS)]
        scratch = Slots([sb(f"scratch{i}", [P, LEN]) for i in range(4)])
        squares = Slots([sb(f"square{i}", [P, LEN]) for i in range(2)])
        ident = sb("ident", [P, P])
        ones = sb("ones", [P, P])
        half = sb("half", [P, P])
        pairs = sb("pairs", [P, 2])
        eps = sb("eps", [P, 4])
        gains = sb("gains", [P, t["gains"].shape[1]])
        lam = sb("lam", [P, 8])
        small = Slots([sb(f"small{i}", [P, 16]) for i in range(10)])
        psum = ctx.enter_context(nc.psum_tensor("psum", [P, 8, 512], F32))

        bank = lambda i: psum[:, i, :]
        bank_free = [[] for _ in range(8)]
        bank_age = [0] * 8
        halves = lambda tile: tile.rearrange("p (a n) -> p a n", a=2)
        two_halves = lambda b: psum[:, b:b + 2, 0:HALF]

        def free_banks(n):
            found = [at for at in range(9 - n)
                     if all(bank_free[b] is not None for b in range(at, at + n))]
            return min(found, key=lambda at: max(bank_age[at:at + n]), default=None)

        def take_banks(n=1):
            at = free_banks(n)
            assert at is not None, "all banks are held"
            free = [d for b in range(at, at + n) for d in bank_free[b]]
            for b in range(at, at + n):
                bank_free[b] = None
            return at, free

        def release_banks(at, n, readers):
            for b in range(at, at + n):
                bank_free[b] = list(readers)
                bank_age[b] = max(bank_age) + 1

        tasks = []
        HOP = "hop"

        def step_tasks():
            turn = list(tasks)
            while turn:
                said = [(task, next(task, "end")) for task in turn]
                for task, what in said:
                    if what == "end":
                        tasks.remove(task)
                turn = [task for task, what in said if what == HOP]

        def run_tasks(until=None):
            rounds = 0
            while (not until()) if until else tasks:
                step_tasks()
                rounds += 1
                assert rounds < 5000, "tasks wait for each other"

        def banks_for(n=1):
            while free_banks(n) is None:
                yield
            return take_banks(n)

        def slots_for(slots, n=1):
            while sum(f is not None for f in slots.free) < n:
                yield
            return [slots.take() for _ in range(n)]

        def made(table, *keys):
            while any(table.get(k) is None for k in keys):
                yield
            return [table[k] for k in keys]

        load_sem = {}

        def load(eng, name, dst, src, after=()):
            load_sem[name] = sem("load_" + name)
            return eng.dma(load_sem[name], 16, lambda: eng.eng.dma_start(dst, src), after)

        meta_loaded = load(pool, "meta", x[:, :, MET], t["meta"].rearrange("(k p) n -> p k n", p=P))
        ident_loaded = load(pool, "ident", ident[:], t["ident"])
        half_loaded = load(pool, "half", half[:], t["half"])
        gains_loaded = load(pool, "gains", gains[:], t["gains"])
        ones_set = dve.do(lambda: nc.vector.memset(ones[:], 1.0))
        consts_set = dve.do(lambda: nc.vector.memset(pairs[:], 0.0))
        for to, value in ((pairs[0:HD, 0:1], 1.0), (pairs[HD:P, 1:2], 1.0),
                          (eps[:, 0:1], LN_EPS), (eps[:, 1:2], RMS_EPS),
                          (eps[:, 2:3], 4.0 * LN_EPS)):
            consts_set = dve.do(lambda to=to, value=value: nc.vector.memset(to, value),
                                after=[consts_set])
        gain_at = t["gain_at"]

        def gain(name, k=0, rows=slice(0, P)):
            c = gain_at[name] + k
            return gains[rows, c:c + 1]

        plan = weight_plan()
        raw_sem = [sem(f"raw{i}") for i in range(RAW_SLOTS)]
        split = []
        piece_read = []
        taken = [0]

        def split_piece(u):
            matrix, m, k0, n = plan[u]
            r, s = u % RAW_SLOTS, u % SPLIT_SLOTS
            src = t[matrix][m, :, k0 * P:(k0 + n) * P]
            loaded = sp.dma(raw_sem[r], 16 * (u // RAW_SLOTS + 1),
                            lambda: nc.sync.dma_start(w_raw[r][:, 0:n * P], src),
                            after=[split[u - RAW_SLOTS][1]] if u >= RAW_SLOTS else [])
            unread = [piece_read[u - SPLIT_SLOTS]] if u >= SPLIT_SLOTS else []
            high = act.do(lambda: nc.scalar.copy(w_hi[s][:, 0:n * P], w_raw[r][:, 0:n * P]),
                          after=[loaded] + unread)
            sub = pool if matrix in ("b2_in", "b2_out") else dve
            low = sub.do(lambda: sub.eng.tensor_tensor(
                w_lo[s][:, 0:n * P], w_raw[r][:, 0:n * P], w_hi[s][:, 0:n * P].bitcast(F32),
                ALU.subtract), after=[high])
            split.append((high, low))

        def stream_until(u):
            while len(split) <= min(u, len(plan) - 1):
                split_piece(len(split))

        def multiply(u, k, outs, operand, first, last, free, mark):
            _, _, k0, _ = plan[u]
            s = u % SPLIT_SLOTS
            hi, lo, ready = operand(k)
            w_h = w_hi[s][:, (k - k0) * P:(k - k0 + 1) * P]
            w_l = w_lo[s][:, (k - k0) * P:(k - k0 + 1) * P]
            pe.wait(free if first else [])
            done = None
            for w, v, need, begin, end in (
                    (w_h, hi, [split[u][0], ready[0]], first, False),
                    (w_l, hi, [split[u][1]], False, False),
                    (w_h, lo, [ready[1]], False, last)):
                for i, (o, c) in enumerate(outs):
                    done = pe.do(lambda: nc.tensor.matmul(o, w, v[:, c], start=begin, stop=end),
                                 after=need, mark=mark and v is lo and i == len(outs) - 1)
            return done

        def out_ranges(b, wide):
            if wide:
                return [(psum[:, b + i, 0:HALF], slice(i * HALF, (i + 1) * HALF))
                        for i in range(2)]
            return [(bank(b), slice(0, SEQ))]

        def next_piece(key):
            u = taken[0]
            taken[0] += 1
            assert plan[u] == key, (plan[u], key)
            return u

        def project(matrix, m, tiles, operand, wide=False, k_range=None,
                    lead=0):
            begin, end = k_range or (0, tiles)
            n = 2 if wide else 1
            while free_banks(n) is None:
                step_tasks()
            b, free = take_banks(n)
            outs = out_ranges(b, wide)
            for key in pieces(matrix, m, end - begin, begin, lead):
                u = next_piece(key)
                stream_until(u + AHEAD)
                for k in range(key[2], key[2] + key[3]):
                    done = multiply(u, k, outs, operand, k == begin, k == end - 1, free,
                                    k == key[2] + key[3] - 1)
                piece_read.append(done)
                step_tasks()
            return b, done

        def project_group(columns, operand, wide=False):
            group = []
            for matrix, m in columns:
                b, free = take_banks(2 if wide else 1)
                (key,) = pieces(matrix, m, KT)
                group.append((next_piece(key), b, free, out_ranges(b, wide)))
            stream_until(group[-1][0])
            for k in range(KT):
                done = [multiply(u, k, outs, operand, k == 0, k == KT - 1, free, k == KT - 1)
                        for u, b, free, outs in group]
            piece_read.extend(done)
            return [(g[1], d) for g, d in zip(group, done)]

        def split_into(hi, lo, value, after=()):
            h = act.do(lambda: nc.scalar.copy(hi, value), after=after)
            l = dve.do(lambda: nc.vector.tensor_tensor(lo, value, hi.bitcast(F32), ALU.subtract),
                       after=[h])
            return h, l

        def split_high(hi, lo, value, after=()):
            h = act.do(lambda: nc.scalar.copy(hi, value), after=after)
            return h, lambda: dve.do(lambda: nc.vector.tensor_tensor(
                lo, value, hi.bitcast(F32), ALU.subtract), after=[h])

        ready = [[] for _ in range(KT)]
        x_ready = [[] for _ in range(KT)]

        def tokens_operand(k):
            return x_hi[:, k, TOK], x_lo[:, k, TOK], ready[k]

        def all_operand(k):
            return x_hi[:, k, :], x_lo[:, k, :], ready[k]

        class Stats:

            def __init__(self, groups, wide, banks):
                self.groups, self.wide = groups, wide
                self.blocks = [(a * HALF + c, w) for c, w in ((0, P), (P, P), (2 * P, HALF - 2 * P))
                               for a in range(2)] if wide else \
                    [(META + P * j, P) for j in range(NB)]
                self.sums, self.sums_free = banks
                self.first = True
                self.square_slot = None

            def add(self, tile, after, last, column=0):
                g = self.groups
                for j, (c, w) in enumerate(self.blocks):
                    done = pe.do(lambda o=psum[0:w, self.sums, column + j * g:column + (j + 1) * g],
                                 a=tile[:, c:c + w], r=ones[:, 0:1] if g == 1 else pairs[:],
                                 f=self.first: nc.tensor.matmul(
                                     o, a, r, start=f, stop=last, skip_group_check=True),
                                 after=[*after, ones_set, consts_set] +
                                 (self.sums_free if self.first else []),
                                 mark=(j == len(self.blocks) - 1))
                    self.first = False
                self.summed = done
                if self.square_slot is not None:
                    squares.free[self.square_slot] = [done]
                return done

            def root(self, scale, eps_col, factor=1.0):
                for _ in self.root_steps(scale, eps_col, factor):
                    pass

            def root_steps(self, scale, eps_col, factor=1.0):
                g = self.groups
                self.slot, root, root_free = small.take()
                parts = [(P, 0, NB * g)]
                if self.wide:
                    parts.append((HALF - 2 * P, NB * g, (NB + 2) * g))
                for w, a, b in parts:
                    rooted = act.do(lambda w=w, a=a, b=b: nc.scalar.activation(
                        root[0:w, a:b], psum[0:w, self.sums, a:b], ACT.Sqrt,
                        bias=eps[0:w, eps_col:eps_col + 1], scale=scale),
                        after=[self.summed, consts_set] + root_free)
                release_banks(self.sums, 1, [rooted])
                yield HOP
                for w, a, b in parts:
                    inverse = dve.do(lambda w=w, a=a, b=b: nc.vector.reciprocal(
                        root[0:w, a:b], root[0:w, a:b]), after=[rooted])
                if factor != 1.0:
                    w, a, b = parts[0]
                    inverse = dve.do(lambda: nc.vector.tensor_scalar(
                        root[0:w, a:b], root[0:w, a:b], factor, None, ALU.mult), after=[inverse])
                self.rooted, self.inverse, self.roots = rooted, inverse, root

            def spread(self, banks):
                g = self.groups
                self.out, out_free = banks
                for j, (c, w) in enumerate(self.blocks):
                    for s in range(g):
                        rows = slice(P // g * s, P // g * (s + 1))
                        lhs = self.roots[0:w, j * g + s:j * g + s + 1].to_broadcast([w, P // g])
                        to = psum[rows, self.out + c // HALF, c % HALF:c % HALF + w] \
                            if self.wide else psum[rows, self.out, c - META:c - META + P]
                        spread = pe.do(lambda o=to, a=lhs, w=w: nc.tensor.matmul(
                            o, a, ident[0:w, 0:w], start=True, stop=True),
                            after=[self.inverse, ident_loaded, self.rooted] + out_free)
                small.free[self.slot] = [spread]
                return two_halves(self.out) if self.wide else bank(self.out), spread

            def release(self, readers):
                release_banks(self.out, 2 if self.wide else 1, readers)

        def squared(groups, wide, tile, cols, after):
            banks = yield from banks_for()
            stats = Stats(groups, wide, banks)
            ((slot, sq, free),) = yield from slots_for(squares)
            done = act.do(lambda: nc.scalar.activation(sq[:, cols], tile, ACT.Square),
                          after=[after] + free)
            stats.square_slot = slot
            return stats, (sq, [done])

        class LayerNorm:

            def __init__(self, scale, early, last_scale=None):
                self.scale, self.early = scale, early
                self.last_scale = last_scale or scale
                self.z = {}
                self.shifted = {}
                self.d = {}
                self.squared = {}
                tasks.append(self.gather())

            def residual(self, m, b, done):
                if m < self.early:
                    z = dve.do(lambda: nc.vector.scalar_tensor_tensor(
                        x[:, m, TOK], x[:, m, TOK], self.scale, bank(b), ALU.mult, ALU.add),
                        after=[done, *x_ready[m]])
                    self.z[m] = z
                else:
                    run_tasks(lambda: m in self.shifted)
                    z = dve.do(lambda: nc.vector.tensor_tensor(
                        x[:, m, TOK], x[:, m, TOK], bank(b), ALU.add),
                        after=[done, self.shifted[m]])
                    self.d[m] = z
                    if m < KT - 1:
                        tasks.append(self.late(m))
                release_banks(b, 1, [z])

            def square(self, k, out, free):
                self.squared[k] = act.do(lambda: nc.scalar.activation(
                    out[:, TOK], x[:, k, TOK], ACT.Square), after=[self.d[k]] + free)
                return self.squared[k]

            def gather(self):
                early = self.early
                ((zslot, zsum, free),) = yield from slots_for(scratch)
                yield from made(self.z, 0, 1)
                total = pool.do(lambda: nc.gpsimd.tensor_tensor(
                    zsum[:, TOK], x[:, 0, TOK], x[:, 1, TOK], ALU.add),
                    after=[self.z[0], self.z[1]] + free)
                for k in range(2, early):
                    yield from made(self.z, k)
                    total = pool.do(lambda: nc.gpsimd.tensor_tensor(
                        zsum[:, TOK], zsum[:, TOK], x[:, k, TOK], ALU.add),
                        after=[total, self.z[k]])
                b, free = yield from banks_for()
                summed = pe.do(lambda: nc.tensor.matmul(
                    bank(b), ones[:], zsum[:, TOK], start=True, stop=True),
                    after=[total, ones_set] + free)
                ((nslot, neg, nfree),) = yield from slots_for(scratch)
                negated = act.do(lambda: nc.scalar.mul(
                    neg[:, TOK], bank(b), -1.0 / (early * P)), after=[summed] + nfree)
                release_banks(b, 1, [negated])
                scratch.free[zslot] = [summed]
                banks = yield from banks_for()
                self.stats = Stats(1, False, banks)
                self.shift, self.shift_free = yield from banks_for()
                for k in range(early, KT):
                    self.shifted[k] = last = dve.do(lambda: nc.vector.scalar_tensor_tensor(
                        x[:, k, TOK], x[:, k, TOK],
                        self.last_scale if k == KT - 1 else self.scale, neg[:, TOK],
                        ALU.mult, ALU.add),
                        after=[negated, *x_ready[k]])
                ((sslot, total_sq, sfree),) = yield from slots_for(scratch)
                for k in range(early):
                    self.d[k] = last = dve.do(lambda: nc.vector.tensor_tensor(
                        x[:, k, TOK], x[:, k, TOK], neg[:, TOK], ALU.add),
                        after=[negated, total])
                    if k == 0:
                        added = self.square(k, total_sq, sfree)
                        continue
                    ((slot, sq, free),) = yield from slots_for(squares)
                    done = self.square(k, sq, free)
                    adder = pool if k <= early // 2 else dve
                    added = adder.do(lambda: adder.eng.tensor_tensor(
                        total_sq[:, TOK], total_sq[:, TOK], sq[:, TOK], ALU.add),
                        after=[done, added])
                    squares.free[slot] = [added]
                    if k == 3:
                        yield
                scratch.free[nslot] = [last]
                yield
                scratch.free[sslot] = [self.stats.add(total_sq, [added], False)]

            def late(self, k):
                if k < KT - 1:
                    yield
                ((slot, sq, free),) = yield from slots_for(squares)
                self.stats.add(x[:, k, :], [self.d[k]], k == KT - 1, column=NB)
                done = self.square(k, sq, free)
                if k < KT - 1:
                    yield
                squares.free[slot] = [self.stats.add(sq, [done], k == KT - 1)]
                self.moved = pe.do(lambda: nc.tensor.matmul(
                    bank(self.shift), ones[:], x[:, k, TOK], start=k == self.early,
                    stop=k == KT - 1), after=[self.d[k], ones_set] + self.shift_free)

            def finish(self, g, b, eps_col, then, split=True):
                run_tasks()
                for _ in self.late(KT - 1):
                    pass
                stats = self.stats

                def centre(k):
                    self.d[k] = dve.do(lambda: nc.vector.scalar_tensor_tensor(
                        x[:, k, TOK], bank(self.shift), -1.0 / D, x[:, k, TOK],
                        ALU.mult, ALU.add), after=[self.moved, self.squared[k]])
                slot, st, free = small.take()
                mean = dve.do(lambda: nc.vector.tensor_scalar(
                    st[:, 0:NB], psum[:, stats.sums, NB:2 * NB], 1.0 / D, None, ALU.mult),
                    after=[stats.summed] + free)
                mean2 = dve.do(lambda: nc.vector.tensor_tensor(
                    st[:, NB:2 * NB], st[:, 0:NB], st[:, 0:NB], ALU.mult), after=[mean])
                variance = dve.do(lambda: nc.vector.scalar_tensor_tensor(
                    st[:, 2 * NB:3 * NB], psum[:, stats.sums, 0:NB], 1.0 / D,
                    st[:, NB:2 * NB], ALU.mult, ALU.subtract), after=[mean2])
                release_banks(stats.sums, 1, [variance])
                root = st[:, 2 * NB:3 * NB]
                rooted = act.do(lambda: nc.scalar.activation(
                    root, root, ACT.Sqrt, bias=eps[:, eps_col:eps_col + 1]),
                    after=[variance, consts_set])
                stats.inverse = dve.do(lambda: nc.vector.reciprocal(root, root), after=[rooted])
                centre(0)
                stats.rooted, stats.roots, stats.slot = rooted, root, slot
                main, spread = stats.spread(take_banks())
                for k in range(1, CENTRED):
                    centre(k)
                waiting = None
                for k in range(KT):
                    y = dve.do(lambda: nc.vector.scalar_tensor_tensor(
                        x[:, k, TOK], x[:, k, TOK], gain(g, k), main, ALU.mult, ALU.mult),
                        after=[spread, self.d[k], gains_loaded])
                    if k + CENTRED < KT:
                        centre(k + CENTRED)
                    high = split and act.do(lambda: nc.scalar.activation(
                        x_hi[:, k, TOK], x[:, k, TOK], ACT.Identity, bias=gain(b, k)),
                        after=[y, piece_read[-1]])
                    moved = act.do(lambda: nc.scalar.activation(
                        x[:, k, TOK], x[:, k, TOK], ACT.Identity, bias=gain(b, k)), after=[y])
                    x_ready[k] = [moved]
                    if waiting:
                        waiting()
                    waiting = then(k, moved, high)
                release_banks(self.shift, 1, [self.d[KT - 1]])
                stats.release([y])
                waiting()

        def split_x(k, done, high):
            def rest():
                ready[k] = [high, dve.do(lambda: nc.vector.tensor_tensor(
                    x_lo[:, k, TOK], x[:, k, TOK], x_hi[:, k, TOK].bitcast(F32),
                    ALU.subtract), after=[high, done, piece_read[-1]])]
            return rest

        class RmsStats:

            def __init__(self, direct):
                self.direct = direct
                self.stats = Stats(1, True, take_banks())
                self.slot, self.total, self.free = scratch.take()
                self.added = None

            def square(self, k, after):
                slot, sq, free = (None, self.total, self.free) if k == 0 else squares.take()
                done = act.do(lambda: nc.scalar.activation(sq[:], x[:, k, :], ACT.Square),
                              after=[*after, *free])
                if k == 0:
                    self.added = done
                elif k < self.direct:
                    self.added = pool.do(lambda: nc.gpsimd.tensor_tensor(
                        self.total[:], self.total[:], sq[:], ALU.add), after=[done, self.added])
                    squares.free[slot] = [self.added]
                else:
                    if k == KT - 1:
                        scratch.free[self.slot] = [
                            self.stats.add(self.total, [self.added], False)]
                    squares.free[slot] = [self.stats.add(sq, [done], k == KT - 1)]
                return done

        def rms_norm_x(g, x_done, gathered):
            run_tasks()
            stats = gathered.stats
            stats.root(1.0 / D, 1)
            main, spread = stats.spread(take_banks(2))
            waiting = None

            def finish(k, slot, high, low):
                ready[k] = [high, low()]
                scratch.free[slot] = ready[k]
            for k in range(KT):
                slot, y, free = scratch.take()
                normed = dve.do(lambda k=k, y=y: nc.vector.scalar_tensor_tensor(
                    halves(y[:]), halves(x[:, k, :]), gain(g, k), main, ALU.mult, ALU.mult),
                    after=[spread, *x_done[k]] + free)
                if waiting:
                    finish(*waiting)
                waiting = (k, slot, *split_high(x_hi[:, k, :], x_lo[:, k, :], y[:],
                                                after=[normed, piece_read[-1]]))
            finish(*waiting)
            stats.release([normed])

        def ffn(gate, up, down, wide, residual, group=GROUP):
            with ExitStack() as own:
                tensor = lambda name, shape, dt: own.enter_context(nc.sbuf_tensor(name, shape, dt))
                tag = f"{gate[0]}{gate[1]}"
                cols, n = (LEN, 2) if wide else (SEQ, 1)
                h_hi = tensor("h_hi_" + tag, [P, FT, cols], F32R)
                h_lo = tensor("h_lo_" + tag, [P, FT, cols], F32R)
                h_ready = [None] * FT
                operand = all_operand if wide else tokens_operand
                view = (lambda tile: halves(tile)) if wide else (lambda tile: tile)
                product = two_halves if wide else bank
                order = [(w[0], w[1] + f) for f in range(FT) for w in (gate, up)]
                first = project_group(order[0:group], operand, wide)
                order = iter(order[group:])
                pending = []
                for f in range(FT):
                    a, u = (first.pop(0) if first else project(*next(order), KT, operand, wide)
                            for _ in range(2))
                    slot, hid, hfree = scratch.take()
                    silu = act.do(lambda: nc.scalar.activation(
                        view(hid[:, 0:cols]), product(a[0]), ACT.Silu), after=[a[1]] + hfree)
                    release_banks(a[0], n, [silu])
                    gated = dve.do(lambda: nc.vector.tensor_tensor(
                        view(hid[:, 0:cols]), view(hid[:, 0:cols]), product(u[0]), ALU.mult),
                        after=[silu, u[1]])
                    release_banks(u[0], n, [gated])

                    def finish(f=f, slot=slot, hid=hid, gated=gated):
                        h_ready[f] = list(split_into(
                            h_hi[:, f, :], h_lo[:, f, :], hid[:, 0:cols],
                            after=[gated] + region_free))
                        scratch.free[slot] = h_ready[f]
                    for later in pending:
                        later()
                    pending = [finish]
                pending[0]()
                hidden = lambda k: (h_hi[:, k, :], h_lo[:, k, :], h_ready[k])
                for m in range(KT):
                    residual(m, *project(down[0], down[1] + m, FT, hidden, wide,
                                         lead=down_lead(m)))
            region_ends()

        region_free = []

        def region_ends():
            region_free[:] = [Done(e.sem, e.count) for e in (pe, act, dve, pool) if e.count]

        def copy_psum(dst, src, after):
            return act.do(lambda: nc.scalar.copy(dst, src), after=after)

        def transposed(banks, sources, copy_to, after, free):
            b, bfree = banks
            for i, (tile, rows, cols) in enumerate(sources):
                done = pe.do(lambda i=i, a=tile, r=rows, c=cols: nc.tensor.transpose(
                    psum[0:c, b, i * P:i * P + r], a, ident[0:r, 0:r]),
                    after=[*after, ident_loaded] + bfree, mark=i == len(sources) - 1)
            for dst, parts, cols in copy_to:
                copied = copy_psum(dst, psum[parts, b, cols], [done, *free])
            release_banks(b, 1, [copied])
            return copied, done

        def mixer_1(layer):
            own = ExitStack()
            tensor = lambda name, shape, dt=F32: own.enter_context(
                nc.sbuf_tensor(f"{name}_{layer}", shape, dt))
            entry = list(region_free)
            tab = tensor("tables", [P, t["tables"].shape[1]])
            tab_loaded = load(pool, f"tables{layer}", tab[:], t["tables"], after=entry)
            table = lambda n: tab[:, t["table_at"][n][0]:t["table_at"][n][1]]
            q_a = tensor("q_a", [P, 4, SEQ])
            k_a = tensor("k_a", [P, SEQ])
            v_a = tensor("v_a", [P, NB, P])
            y_a = tensor("y_a", [P, 4, SEQ])
            y_r = tensor("y_r", [P, 4, SEQ])
            q_r = [tensor(f"q_r{i}", [P, SEQ]) for i in range(2)]
            q_w = [tensor(f"q_w{i}", [P, SEQ]) for i in range(2)]
            k_r = [tensor(f"k_r{i}", [P, SEQ]) for i in range(2)]
            k_w = [tensor(f"k_w{i}", [P, NB, P]) for i in range(2)]
            v_r = [tensor(f"v_r{i}", [P, NB, P]) for i in range(2)]
            gate = tensor("gate", [P, 4, SEQ])
            prob = Slots([tensor(f"prob{i}", [P, 4, 2 * P]) for i in range(3)])
            prob_t = Slots([tensor(f"prob_t{i}", [P, 4 * P]) for i in range(3)])
            state = tensor("state", [P, NB - 1, HD])

            done_ = {}

            def rotated(b, done, out, key, rot, cos, sin, scale, free=lambda: ()):
                ((slot, raw, rfree),) = yield from slots_for(scratch)
                copied = copy_psum(raw[:, TOK], bank(b), [done] + rfree)
                release_banks(b, 1, [copied])
                yield HOP
                ((slot2, part, pfree),) = yield from slots_for(scratch)
                times_cos = dve.do(lambda: nc.vector.scalar_tensor_tensor(
                    part[:, TOK], raw[:, TOK], scale, table(cos), ALU.mult, ALU.mult),
                    after=[copied, tab_loaded] + pfree)
                yield
                while free() is None:
                    yield
                wb, wfree = yield from banks_for()
                turned = pe.do(lambda: nc.tensor.matmul(
                    bank(wb), table(rot), raw[:, TOK], start=True, stop=True),
                    after=[copied, tab_loaded] + wfree)
                times_sin = dve.do(lambda: nc.vector.scalar_tensor_tensor(
                    out, bank(wb), scale, table(sin), ALU.mult, ALU.mult),
                    after=[turned, *entry, *free()])
                release_banks(wb, 1, [times_sin])
                scratch.free[slot] = [times_cos, turned]
                done_[key] = dve.do(lambda: nc.vector.tensor_tensor(
                    out, out, part[:, TOK], ALU.add), after=[times_cos, times_sin])
                scratch.free[slot2] = [done_[key]]

            def token_major(b, done, out, key, free=lambda: ()):
                ((slot, raw, rfree),) = yield from slots_for(scratch)
                copied = copy_psum(raw[:, TOK], bank(b), [done] + rfree)
                release_banks(b, 1, [copied])
                yield
                while free() is None:
                    yield
                banks = yield from banks_for()
                done_[key], read = transposed(banks,
                    [(raw[:, META + n * P:META + (n + 1) * P], P, P) for n in range(NB)],
                    [(out[:].rearrange("p n f -> p (n f)"), slice(0, P), slice(0, SEQ))],
                    [copied], [*entry, *free()])
                scratch.free[slot] = [read]

            def attention(items):
                yield from made(done_, *(("q", j) for j in range(4)), "k", "v")
                for n, g in items:
                    rows = slice(HD * g, HD * (g + 1))
                    k0 = max(n - 1, 0) * P
                    width = (n + 1) * P - k0
                    band = table("band")[:, 2 * P - width:].unsqueeze(1).to_broadcast(
                        [P, 4, width])
                    ((slot, s, sfree),) = yield from slots_for(prob)
                    ((st_slot, st, st_free),) = yield from slots_for(small)
                    b, bfree = yield from banks_for(2)
                    for j in range(4):
                        out = psum[:, b + j // 2, (j % 2) * 256:(j % 2) * 256 + width]
                        done = pe.do(lambda: nc.tensor.matmul(
                            out, q_a[rows, j, n * P:(n + 1) * P], k_a[rows, k0:k0 + width],
                            start=True, stop=True),
                            after=[*(done_["q", i] for i in range(4)), done_["k"]] + bfree)
                    scores = psum[:, b:b + 2, :].rearrange(
                        "p b (j k) -> p (b j) k", j=2)[:, :, 0:width]
                    s = s[:, :, 0:width]
                    masked = dve.do(lambda: nc.vector.scalar_tensor_tensor(
                        s, scores, HD ** -0.5, band, ALU.mult, ALU.add),
                        after=[done, tab_loaded, *entry] + sfree)
                    release_banks(b, 2, [masked])
                    top = dve.do(lambda: nc.vector.tensor_reduce(
                        st[:, 0:4], s, AX.X, ALU.max), after=[masked] + st_free)
                    sink = gains[:, gain_at[f"sinks{layer}"] + 4 * g:][:, 0:4]
                    top = dve.do(lambda: nc.vector.tensor_tensor(
                        st[:, 0:4], st[:, 0:4], sink, ALU.max), after=[top])
                    neg = dve.do(lambda: nc.vector.tensor_scalar(
                        st[:, 0:4], st[:, 0:4], -1.0, None, ALU.mult), after=[top])
                    sink_in = dve.do(lambda: nc.vector.tensor_tensor(
                        st[:, 4:8], sink, st[:, 0:4], ALU.add), after=[neg])
                    yield HOP
                    for j in range(4):
                        act.do(lambda: nc.scalar.activation(
                            s[:, j, :], s[:, j, :], ACT.Exp, bias=st[:, j:j + 1],
                            accum_out=st[:, 8 + j:9 + j]), after=[neg])
                    exps = act.do(lambda: nc.scalar.activation(
                        st[:, 4:8], st[:, 4:8], ACT.Exp), after=[sink_in])
                    yield HOP
                    total = dve.do(lambda: nc.vector.tensor_tensor(
                        st[:, 8:12], st[:, 8:12], st[:, 4:8], ALU.add), after=[exps])
                    inverse = dve.do(lambda: nc.vector.reciprocal(st[:, 8:12], st[:, 8:12]),
                                     after=[total])
                    normed = dve.do(lambda: nc.vector.tensor_tensor(
                        s, s, st[:, 8:12].unsqueeze(2).to_broadcast([P, 4, width]), ALU.mult),
                        after=[inverse])
                    small.free[st_slot] = [normed]
                    yield
                    blocks = width // P
                    turned = yield from slots_for(prob_t, blocks)
                    copied = [None] * blocks
                    for kb, (_, w_t, wfree) in enumerate(turned):
                        banks = yield from banks_for()
                        copied[kb], read = transposed(
                            banks, [(s[:, j, kb * P:(kb + 1) * P], P, P) for j in range(4)],
                            [(w_t[:], slice(0, P), slice(0, SEQ))], [normed], [*entry, *wfree])
                    prob.free[slot] = [read]
                    yield
                    b, bfree = yield from banks_for()
                    for kb, (_, w_t, _) in enumerate(turned):
                        done = pe.do(lambda: nc.tensor.matmul(
                            psum[rows, b, :], v_a[:, n + 1 - blocks + kb, rows], w_t[:],
                            start=kb == 0, stop=kb == blocks - 1),
                            after=[copied[kb], done_["v"]] + bfree)
                    for i, _, _ in turned:
                        prob_t.free[i] = [done]
                    done_["y_a", n, g] = act.do(lambda: nc.scalar.copy(
                        y_a[rows, :, n * P:(n + 1) * P],
                        psum[rows, b, :].rearrange("p (j q) -> p j q", j=4)),
                        after=[done, *entry])
                    release_banks(b, 1, [done_["y_a", n, g]])

            y_ready = [None] * KT

            def keys_weighted(j):
                i = j % 2
                yield from made(done_, ("k_r", j))
                yield
                wb, wfree = yield from banks_for()
                for n in range(NB):
                    turned = pe.do(lambda: nc.tensor.transpose(
                        psum[:, wb, n * P:(n + 1) * P], k_r[i][:, n * P:(n + 1) * P], ident[:]),
                        after=[done_["k_r", j]] + wfree)
                done_["k_w", j] = dve.do(lambda: nc.vector.tensor_tensor(
                    k_w[i][:], bank(wb).rearrange("p (n d) -> p n d", n=NB),
                    table("w_k")[:, j * P:(j + 1) * P].unsqueeze(1).to_broadcast([P, NB, P]),
                    ALU.mult), after=[turned, *entry, *set_free(j)()])
                release_banks(wb, 1, [done_["k_w", j]])

            def set_free(j):
                return lambda: () if j < 2 else \
                    [done_["set_read", j - 2]] if ("set_read", j - 2) in done_ else None

            def retention(j):
                i = j % 2
                yield from made(done_, ("q_r", j))
                done_["q_w", j] = dve.do(lambda: nc.vector.tensor_tensor(
                    q_w[i][:].rearrange("p (n c) -> p n c", n=NB),
                    q_r[i][:].rearrange("p (n c) -> p n c", n=NB),
                    table("w_q")[:, j * P:(j + 1) * P].unsqueeze(1).to_broadcast([P, NB, P]),
                    ALU.mult), after=[done_["q_r", j]])
                yield from made(done_, ("k_w", j), ("v_r", j))
                ((slot, sc, sfree),) = yield from slots_for(prob)
                b, bfree = yield from banks_for(2)
                for n in range(NB):
                    for s in range(2):
                        rows, cols = slice(HD * s, HD * (s + 1)), slice(n * P, (n + 1) * P)
                        scored = pe.do(lambda: nc.tensor.matmul(
                            psum[:, b + s, cols],
                            k_r[i][rows, cols], q_r[i][rows, cols], start=True, stop=True),
                            after=[done_["q_r", j], done_["k_r", j]] + bfree,
                            mark=(n, s) == (NB - 1, 1))
                decay = table("decay")[:, 2 * j * P:2 * (j + 1) * P].rearrange(
                    "p (s i) -> p s i", s=2).unsqueeze(2).to_broadcast([P, 2, NB, P])
                sc = sc[:].rearrange("p a b -> p (a b)").rearrange(
                    "p (s n i) -> p s n i", s=2, n=NB)
                decayed = dve.do(lambda: nc.vector.tensor_tensor(
                    sc, psum[:, b:b + 2, :].rearrange("p s (n i) -> p s n i", n=NB), decay,
                    ALU.mult), after=[scored, tab_loaded, *entry] + sfree)
                release_banks(b, 2, [decayed])
                b2, b2free = yield from banks_for()
                for n in range(NB - 1):
                    for s in range(2):
                        rows = slice(HD * s, HD * (s + 1))
                        added = pe.do(lambda: nc.tensor.matmul(
                            psum[rows, b2, n * HD:(n + 1) * HD], k_w[i][:, n, rows],
                            v_r[i][:, n, rows], start=True, stop=True),
                            after=[done_["k_w", j], done_["v_r", j]] + b2free,
                            mark=(n, s) == (NB - 2, 1))
                st_read = [done_["set_read", j - 1]] if j else []
                before = dve.do(lambda: nc.vector.tensor_copy(
                    state[:, 0, :], psum[:, b2, 0:HD]), after=[added, *st_read, *entry])
                g_col = table("g_chunk")[:, j:j + 1]
                for n in range(1, NB - 1):
                    before = dve.do(lambda: nc.vector.scalar_tensor_tensor(
                        state[:, n, :], state[:, n - 1, :], g_col,
                        psum[:, b2, n * HD:(n + 1) * HD], ALU.mult, ALU.add), after=[before])
                release_banks(b2, 1, [before])
                yield
                b3, b3free = yield from banks_for()
                for n in range(NB):
                    cols = slice(n * P, (n + 1) * P)
                    for s in range(2):
                        rows = slice(HD * s, HD * (s + 1))
                        out = pe.do(lambda: nc.tensor.matmul(
                            psum[rows, b3, cols], v_r[i][:, n, rows],
                            sc[:, s, n, :], start=True, stop=n == 0,
                            skip_group_check=True),
                            after=[decayed, done_["v_r", j]] + b3free, mark=n == 0)
                        if n:
                            out = pe.do(lambda: nc.tensor.matmul(
                                psum[rows, b3, cols], state[rows, n - 1, :],
                                q_w[i][rows, cols], start=False, stop=True,
                                skip_group_check=True), after=[before, done_["q_w", j]])
                prob.free[slot] = [out]
                done_["set_read", j] = out
                ((oslot, o, ofree),) = yield from slots_for(scratch)
                copied = copy_psum(o[:, TOK], bank(b3), [out] + ofree)
                release_banks(b3, 1, [copied])
                yield
                b4, b4free = yield from banks_for()
                summed = pe.do(lambda: nc.tensor.matmul(
                    bank(b4), half[:], o[:, TOK], start=True, stop=True),
                    after=[copied, half_loaded] + b4free)
                centred = dve.do(lambda: nc.vector.scalar_tensor_tensor(
                    o[:, TOK], bank(b4), -1.0 / HD, o[:, TOK], ALU.mult, ALU.add),
                    after=[summed])
                release_banks(b4, 1, [centred])
                yield HOP
                stats, square = yield from squared(2, False, o[:, TOK], TOK, centred)
                yield
                stats.add(*square, True)
                yield from stats.root_steps(1.0 / HD, 1)
                yield
                banks = yield from banks_for()
                main, spread = stats.spread(banks)
                normed = dve.do(lambda: nc.vector.tensor_tensor(
                    o[:, TOK], o[:, TOK], main, ALU.mult), after=[spread])
                stats.release([normed])
                yield from made(done_, ("gate", j))
                done_["y_r", j] = dve.do(lambda: nc.vector.tensor_tensor(
                    y_r[:, j, :], o[:, TOK], gate[:, j, :], ALU.mult),
                    after=[normed, done_["gate", j], *entry])
                scratch.free[oslot] = [done_["y_r", j]]

            first = layer * IN_TILES_1
            at = [first]

            def next_tile():
                out = project("w_in", at[0], KT, tokens_operand)
                at[0] += 1
                return out

            group = project_group([("w_in", first + i) for i in range(GROUP)], tokens_operand)
            at[0] += GROUP
            for j in range(4):
                out = group[j] if j < GROUP else next_tile()
                tasks.append(rotated(*out, q_a[:, j, :], ("q", j), "rot_a", "cos_a", "sin_a",
                                     1.0))
            tasks.append(rotated(*next_tile(), k_a[:], "k", "rot_a", "cos_a", "sin_a", 1.0))
            tasks.append(token_major(*next_tile(), v_a, "v"))
            items = iter([(n, g) for n in range(NB) for g in range(2)])
            tasks.extend(attention(items) for _ in range(2))
            for j in range(4):
                i = j % 2
                tasks.append(rotated(*next_tile(), q_r[i][:], ("q_r", j), "rot_r", "cos_r",
                                     "sin_r", 1.0, set_free(j)))
                tasks.append(rotated(*next_tile(), k_r[i][:], ("k_r", j), "rot_r", "cos_r",
                                     "sin_r", HD ** -0.5, set_free(j)))
                tasks.append(keys_weighted(j))
                tasks.append(token_major(*next_tile(), v_r[i], ("v_r", j), set_free(j)))
                tasks.append(retention(j))
            for j in range(4):
                b, done = next_tile()
                done_["gate", j] = act.do(lambda: nc.scalar.activation(
                    gate[:, j, :], bank(b), ACT.Silu), after=[done, *entry])
                release_banks(b, 1, [done_["gate", j]])
            read = piece_read[-1]
            items = [("y_a", n, g) for n in range(NB) for g in range(2)]
            run_tasks(lambda: all(k in done_ for k in items))
            for j in range(4):
                y_ready[j] = list(split_into(x_hi[:, j, TOK], x_lo[:, j, TOK], y_a[:, j, :],
                                             after=[*(done_[k] for k in items), read]))

            def split_retained():
                for j in range(4):
                    yield from made(done_, ("y_r", j))
                    y_ready[4 + j] = list(split_into(
                        x_hi[:, 4 + j, TOK], x_lo[:, 4 + j, TOK], y_r[:, j, :],
                        after=[done_["y_r", j], read]))
            tasks.append(split_retained())
            operand = lambda k: (x_hi[:, k, TOK], x_lo[:, k, TOK], y_ready[k])
            for m in range(KT - 1):
                b, done = project("w_out", layer * KT + m, KT, operand, k_range=(0, KT // 2))
                z = dve.do(lambda: nc.vector.scalar_tensor_tensor(
                    x[:, m, TOK], x[:, m, TOK], ALPHA, bank(b), ALU.mult, ALU.add),
                    after=[done, *x_ready[m]])
                release_banks(b, 1, [z])
                x_ready[m] = [z]
            run_tasks()
            norm = LayerNorm(1.0, KT - 3, ALPHA)
            for m in range(KT):
                norm.residual(m, *project("w_out", layer * KT + m, KT, operand,
                                          k_range=(KT // 2, KT) if m < KT - 1 else None))
            own.close()
            region_ends()
            norm.finish(f"ln2_g{layer}", f"ln2_b{layer}", 0, split_x)

        def square_task(gathered, m, z, x_done):
            x_done[m] = [z]
            yield
            while None in squares.free:
                yield
            x_done[m] = [z, gathered.square(m, [z])]

        def residual_both(x_done, gathered):
            def residual(m, b, done):
                z = dve.do(lambda: nc.vector.scalar_tensor_tensor(
                    halves(x[:, m, :]), two_halves(b), 0.5, halves(x[:, m, :]),
                    ALU.mult, ALU.add), after=[done, *x_done[m]])
                release_banks(b, 2, [z])
                tasks.append(square_task(gathered(), m, z, x_done))
            return residual

        prepared = {}

        def bias_setup():
            ((hot_slot, hot, _), (rows_slot, rows, _)) = yield from slots_for(squares, 2)
            ((cut_slot, cut, cut_free),) = yield from slots_for(scratch)
            hot, rows = hot[0:BUCKETS, 0:REL_N], rows[0:8, 0:REL_N]
            table, cut = cut[0:BUCKETS, REL_N:REL_N + 8], cut[0:8, 0:REL_N]
            hot_loaded = load(pool, "hot", hot, t["distance_hot"])
            bias_loaded = load(pool, "rel_bias", table, t["rel_bias"], after=cut_free)
            cut_loaded = load(pool, "cut", cut, t["distance_mask"])
            yield
            yield
            b, free = yield from banks_for()
            looked = pe.do(lambda: nc.tensor.matmul(
                psum[0:8, b, 0:REL_N], table, hot, start=True, stop=True),
                after=[hot_loaded, bias_loaded] + free)
            far = dve.do(lambda: nc.vector.tensor_copy(lam[0:8, 0:1], psum[0:8, b, 0:1]),
                         after=[looked])
            relative = dve.do(lambda: nc.vector.tensor_scalar(
                rows, psum[0:8, b, 0:REL_N], lam[0:8, 0:1], None, ALU.subtract), after=[far])
            release_banks(b, 1, [relative])
            causal = dve.do(lambda: nc.vector.tensor_tensor(rows, rows, cut, ALU.add),
                            after=[relative, cut_loaded])
            rows_stored = load(pool, "rows_stored", t["bias_rows"], rows, after=[causal])
            prepared["rows_stored"] = rows_stored
            squares.free[hot_slot] = [looked]
            squares.free[rows_slot] = [rows_stored]
            scratch.free[cut_slot] = [causal, looked]

            g0 = gain_at["lambda_q1"]
            multiplied = dve.do(lambda: nc.vector.tensor_tensor(
                lam[0:HD, 2:4], gains[0:HD, g0:g0 + 3:2], gains[0:HD, g0 + 1:g0 + 4:2],
                ALU.mult), after=[relative, gains_loaded])
            yield
            b, free = yield from banks_for()
            dotted = pe.do(lambda: nc.tensor.matmul(
                psum[:, b, 0:2], ones[0:HD, :], lam[0:HD, 2:4], start=True, stop=True),
                after=[multiplied, ones_set] + free)
            exped = act.do(lambda: nc.scalar.activation(lam[:, 4:6], psum[:, b, 0:2], ACT.Exp),
                           after=[dotted])
            release_banks(b, 1, [exped])
            lam_done = dve.do(lambda: nc.vector.tensor_tensor(
                lam[:, 6:7], lam[:, 5:6], lam[:, 4:5], ALU.subtract), after=[exped])
            prepared["lambda"] = dve.do(lambda: nc.vector.tensor_scalar(
                lam[:, 6:7], lam[:, 6:7], LAM_INIT, None, ALU.subtract), after=[lam_done])

        def mixer_2(x_done):
            own = ExitStack()
            tensor = lambda name, shape, dt=F32: own.enter_context(
                nc.sbuf_tensor("b2_" + name, shape, dt))
            entry = list(region_free)
            q_a = tensor("q_a", [P, A_HEADS, SEQ])
            k_a = tensor("k_a", [P, A_HEADS, LEN])
            v_a = tensor("v_a", [P, NB, A_HEADS, P])
            v_a_meta = tensor("v_a_meta", [META, A_HEADS, P])
            q_lat = tensor("q_lat", [P, B_HEADS, 2, SEQ])
            c_fm = tensor("c_fm", [P, 2, LEN])
            c_tm = tensor("c_tm", [P, NB, B_DC])
            c_tm_meta = tensor("c_tm_meta", [META, B_DC])
            q_i = tensor("q_i", [P, 4, SEQ])
            k_i = tensor("k_i", [P, LEN])
            w_i = tensor("w_i", [P, NB, IDX_HEADS])
            w_uk = tensor("w_uk", [P, B_HEADS * B_DC])
            w_uv = tensor("w_uv", [P, B_HEADS, 2, P])
            window = tensor("window", [P, A_HEADS + B_HEADS, WINDOW_2])
            rank = tensor("rank", [P, LEN])
            keep_at = [sum(META + P * (i + 1) for i in range(b)) for b in range(NB + 1)]
            keep = tensor("keep", [P, keep_at[NB]])
            attn_t = Slots([tensor(f"attn_t{i}", [P, NB + 1, P]) for i in range(TURNED)])
            flip = rank[:, 0:P]
            edge = tensor("edge", [P, P])
            spare = [tensor(f"spare{i}", [P, LEN]) for i in range(SPARE)]
            work = Slots([*scratch.bufs, *spare])
            work.free = [*scratch.free, *(list(entry) for _ in spare)]

            uk_loaded = load(act, "w_uk", w_uk[:], t["w_uk"], after=entry)
            uv_loaded = load(act, "w_uv", w_uv[:].rearrange("p h k d -> p (h k d)"), t["w_uv"])
            edge_loaded = load(act, "edge", edge[:], t["tables"][:, t["table_at"]["band"][0] + P:
                                                                 t["table_at"]["band"][1]])
            flip_loaded = load(act, "flip", flip, t["flip"], after=entry)
            heads = A_HEADS + B_HEADS
            mirrored = q_lat[:].rearrange("p h k n -> p (h k n)")[:, 0:heads * WINDOW_2]
            mirrored_in = [load(act, f"mirrored{h}", mirrored[:, h * WINDOW_2:(h + 1) * WINDOW_2],
                                bass.AP(t["bias_rows"].tensor, h * REL_N,
                                        [[1, P], [1, WINDOW_2]]),
                                after=[prepared["rows_stored"]]) for h in range(heads)]
            done_ = {}

            def windows():
                for _ in range(2):
                    yield
                for h in range(0, heads, 2):
                    b, free = yield from banks_for()
                    done_["turned"] = pe.do(lambda: nc.tensor.matmul(
                        bank(b), flip, mirrored[:, h * WINDOW_2:(h + 2) * WINDOW_2],
                        start=True, stop=True), after=[*mirrored_in[h:h + 2], flip_loaded] + free)
                    copied = copy_psum(window[:, h:h + 2, :].rearrange("p h j -> p (h j)"),
                                       bank(b), [done_["turned"], *entry])
                    release_banks(b, 1, [copied])
                done_["window"] = copied

            at = [0]

            def next_tile(wide):
                out = project("b2_in", at[0], KT, all_operand if wide else tokens_operand, wide)
                at[0] += 1
                return out

            def evacuate(dst, out, free=()):
                wide = dst.shape[-1] == LEN
                copied = copy_psum(halves(dst) if wide else dst,
                                   two_halves(out[0]) if wide else bank(out[0]),
                                   [out[1], *entry, *free])
                release_banks(out[0], 2 if wide else 1, [copied])
                return copied

            def normalise(dst, roots, wide, g, spread):
                view = halves if wide else (lambda tile: tile)
                return dve.do(lambda: nc.vector.scalar_tensor_tensor(
                    view(dst), view(dst), g, roots, ALU.mult, ALU.mult),
                    after=[spread, gains_loaded])

            def normed(dst, groups, wide, scale, g, key, after, factor=1.0):
                cols = slice(0, LEN if wide else SEQ)
                offset = 0 if wide else META
                stats, square = yield from squared(groups, wide, dst,
                                                   slice(offset, LEN), after)
                yield
                stats.add(*square, True)
                yield from stats.root_steps(scale, 1, factor)
                yield
                banks = yield from banks_for(2 if wide else 1)
                roots, spread = stats.spread(banks)
                done_[key] = normalise(dst[:, cols], roots, wide, g, spread)
                stats.release([done_[key]])

            def keys(b):
                return META + P * (b + 1)

            def bank_parts(n):
                return [(0, min(n, 512))] + ([(512, n)] if n > 512 else [])

            def two_banks(b, n):
                return psum[:, b:b + 2, :].rearrange("p b n -> p (b n)")[:, 0:n] if n > 512 \
                    else psum[:, b, 0:n]

            def indexer(b):
                n = keys(b)
                width = 2 if n > 512 else 1
                own_cols = slice(n - P, n)
                acc = None
                yield from made(done_, *(("q_i", j) for j in range(4)), "k_i", "w_i",
                                "window")
                for h in range(0, IDX_HEADS, 2):
                    scores = []
                    for s in range(2):
                        rows = slice(HD * s, HD * (s + 1))
                        ((slot, pos, pfree),) = yield from slots_for(work)
                        wb, free = yield from banks_for(width)
                        for c0, c1 in bank_parts(n):
                            dots = pe.do(lambda: nc.tensor.matmul(
                                psum[:, wb + c0 // 512, 0:c1 - c0],
                                q_i[rows, h // 2, b * P:(b + 1) * P], k_i[rows, c0:c1],
                                start=True, stop=True),
                                after=[done_["q_i", h // 2], done_["k_i"]] + free)
                        positive = act.do(lambda: nc.scalar.activation(
                            pos[:, 0:n], two_banks(wb, n), ACT.Relu, scale=HD ** -0.5),
                            after=[dots] + pfree)
                        release_banks(wb, width, [positive])
                        scores.append((w_i[:, b, h + s:h + s + 1], slot, pos, positive))
                    yield HOP
                    for weight, slot, pos, positive in scores:
                        if acc is None:
                            acc = dve.do(lambda: nc.vector.tensor_scalar(
                                rank[:, 0:n], pos[:, 0:n], weight, None, ALU.mult),
                                after=[positive, done_["w_i"],
                                       *([done_["kept", b - 1]] if b else
                                         [*entry, done_["turned"]])])
                        else:
                            acc = dve.do(lambda: nc.vector.scalar_tensor_tensor(
                                rank[:, 0:n], pos[:, 0:n], weight, rank[:, 0:n],
                                ALU.mult, ALU.add), after=[positive, acc])
                        work.free[slot] = [acc]
                    if h % 4:
                        yield
                done_["scored", b] = dots
                acc = dve.do(lambda: nc.vector.tensor_tensor(
                    rank[:, own_cols], rank[:, own_cols], edge[:], ALU.add),
                    after=[acc, edge_loaded])
                ((slot, best, bfree),) = yield from slots_for(small)
                for i in range(TOPK // 8):
                    found = dve.do(lambda: nc.vector.max(best[:, 0:8], rank[:, 0:n]),
                                   after=[acc] + bfree)
                    acc = dve.do(lambda: nc.vector.match_replace(
                        rank[:, 0:n], best[:, 0:8], rank[:, 0:n], -2.0 * BIG), after=[found])
                    if i % ROUNDS == ROUNDS - 1:
                        yield
                small.free[slot] = [acc]
                done_["kept", b] = dve.do(lambda: nc.vector.tensor_scalar(
                    keep[:, keep_at[b]:keep_at[b + 1]], rank[:, 0:n], -2.0 * BIG, -BIG,
                    ALU.not_equal, ALU.mult), after=[acc, *entry])
                yield

            def weights_t(tile, n, after):
                ((slot, out, free),) = yield from slots_for(attn_t)
                blocks = (n - META) // P
                sources = [(tile[:, META + P * j:META + P * (j + 1)], P, P)
                           for j in range(blocks)]
                meta_in = (tile[:, MET], P, META)
                banks = yield from banks_for()
                if blocks < 4:
                    copied, read = transposed(
                        banks, sources + [meta_in],
                        [(out[:, 0:blocks, :].rearrange("p n q -> p (n q)"), slice(0, P),
                          slice(0, blocks * P)),
                         (out[0:META, NB, :], slice(0, META),
                          slice(blocks * P, (blocks + 1) * P))], after, [*entry, *free])
                else:
                    transposed(banks, sources,
                               [(out[:, 0:blocks, :].rearrange("p n q -> p (n q)"),
                                 slice(0, P), slice(0, blocks * P))], after, [*entry, *free])
                    banks = yield from banks_for()
                    copied, read = transposed(banks, [meta_in],
                                              [(out[0:META, NB, :], slice(0, META),
                                                slice(0, P))], after, [])
                return slot, out, copied, read

            def top(s, n, st, ready_, free):
                found = dve.do(lambda: nc.vector.tensor_reduce(
                    st[:, 0:1], s[:, 0:n], AX.X, ALU.max), after=[ready_] + free)
                return dve.do(lambda: nc.vector.tensor_scalar(
                    st[:, 0:1], st[:, 0:1], -1.0, None, ALU.mult), after=[found])

            def exponentials(s, n, st, negated):
                return act.do(lambda: nc.scalar.activation(
                    s[:, 0:n], s[:, 0:n], ACT.Exp, bias=st[:, 0:1], accum_out=st[:, 1:2]),
                    after=[negated])

            def inverse_sum(st, exped):
                return dve.do(lambda: nc.vector.reciprocal(st[:, 1:2], st[:, 1:2]),
                              after=[exped])

            def latent_attention(items, lane):
                yield from made(done_, ("kept", 0))
                yield from made(done_, "window", "c", ("c_tm", 0), ("c_tm", 1), ("q_lat", 0, 1))
                for _ in range(lane):
                    yield
                for b, h in items:
                    yield from made(done_, ("q_lat", h, 0), ("q_lat", h, 1), ("kept", b))
                    n = keys(b)
                    width = 2 if n > 512 else 1
                    w0 = max(n - WINDOW_2, 0)
                    ((slot, s, sfree),) = yield from slots_for(work)
                    ((st_slot, st, st_free),) = yield from slots_for(small)
                    wb, free = yield from banks_for(width)
                    for c0, c1 in bank_parts(n):
                        for k in range(2):
                            done = pe.do(lambda: nc.tensor.matmul(
                                psum[:, wb + c0 // 512, 0:c1 - c0],
                                q_lat[:, h, k, b * P:(b + 1) * P], c_fm[:, k, c0:c1],
                                start=k == 0, stop=k == 1),
                                after=[done_["q_lat", h, k], done_["c", k]] + free)
                    masked = dve.do(lambda: nc.vector.scalar_tensor_tensor(
                        s[:, 0:n], two_banks(wb, n), B_DC ** -0.5,
                        keep[:, keep_at[b]:keep_at[b + 1]], ALU.mult, ALU.add),
                        after=[done, done_["kept", b]] + sfree)
                    release_banks(wb, width, [masked])
                    yield HOP
                    biased = pool.do(lambda: nc.gpsimd.tensor_tensor(
                        s[:, w0:n], s[:, w0:n], window[:, A_HEADS + h, WINDOW_2 - (n - w0):],
                        ALU.add), after=[masked, done_["window"]])
                    yield HOP
                    negated = top(s, n, st, biased, st_free)
                    yield HOP
                    exped = exponentials(s, n, st, negated)
                    yield HOP
                    inverse = inverse_sum(st, exped)
                    yield HOP
                    ready_ = act.do(lambda: nc.scalar.mul(
                        s[:, 0:n], s[:, 0:n], st[:, 1:2]), after=[inverse])
                    small.free[st_slot] = [ready_]
                    yield
                    aslot, a_t, copied, read = yield from weights_t(s, n, [ready_])
                    yield
                    blocks = (n - META) // P
                    wb, free = yield from banks_for()
                    for k in range(2):
                        cols = slice(k * P, (k + 1) * P)
                        for j in range(blocks):
                            pe.do(lambda: nc.tensor.matmul(
                                psum[:, wb, cols], c_tm[:, j, cols], a_t[:, j, :],
                                start=j == 0, stop=False),
                                after=[copied, done_["c_tm", k]] + free, mark=False)
                        done = pe.do(lambda: nc.tensor.matmul(
                            psum[:, wb, cols], c_tm_meta[:, cols], a_t[0:META, NB, :],
                            start=False, stop=True))
                    attn_t.free[aslot] = [done]
                    latent = copy_psum(s[:, 0:2 * P], psum[:, wb, 0:2 * P], [done, read])
                    release_banks(wb, 1, [latent])
                    yield
                    wb, free = yield from banks_for()
                    for k in range(2):
                        done = pe.do(lambda: nc.tensor.matmul(
                            psum[:, wb, 0:P], w_uv[:, h, k, :], s[:, k * P:(k + 1) * P],
                            start=k == 0, stop=k == 1), after=[latent, uv_loaded] + free)
                    work.free[slot] = [done]
                    done_["y_b", b, h] = copy_psum(
                        q_i[:, h, b * P:(b + 1) * P], psum[:, wb, 0:P],
                        [done, done_["scored", b]])
                    release_banks(wb, 1, [done_["y_b", b, h]])

            def differential(items, lane):
                yield from made(done_, "window", ("v_a", 0))
                for _ in range(lane):
                    yield
                for b, h in items:
                    yield from made(done_, ("q_a", h), ("k_a", h), ("v_a", h))
                    n = keys(b)
                    width = 2 if n > 512 else 1
                    w0 = max(n - WINDOW_2, 0)
                    (slot0, s0, free0), (slot1, s1, free1) = yield from slots_for(work, 2)
                    (st_slot0, st0, st_free0), (st_slot1, st1, st_free1) = \
                        yield from slots_for(small, 2)
                    negated = []
                    for m, s, sfree, st, st_free in ((0, s0, free0, st0, st_free0),
                                                     (1, s1, free1, st1, st_free1)):
                        rows = slice(HD * m, HD * (m + 1))
                        wb, free = yield from banks_for(width)
                        for c0, c1 in bank_parts(n):
                            done = pe.do(lambda: nc.tensor.matmul(
                                psum[:, wb + c0 // 512, 0:c1 - c0],
                                q_a[rows, h, b * P:(b + 1) * P], k_a[rows, h, c0:c1],
                                start=True, stop=True),
                                after=[done_["q_a", h], done_["k_a", h]] + free)
                        view = two_banks(wb, n)
                        biased = dve.do(lambda: nc.vector.scalar_tensor_tensor(
                            s[:, w0:n], view[:, w0:n], HD ** -0.5,
                            window[:, h, WINDOW_2 - (n - w0):], ALU.mult, ALU.add),
                            after=[done, done_["window"]] + sfree)
                        if w0:
                            biased = dve.do(lambda: nc.vector.tensor_scalar(
                                s[:, 0:w0], view[:, 0:w0], HD ** -0.5, None, ALU.mult))
                        release_banks(wb, width, [biased])
                        negated.append(top(s, n, st, biased, st_free))
                    yield HOP
                    exped = [exponentials(s, n, st, neg) for s, st, neg in
                             ((s0, st0, negated[0]), (s1, st1, negated[1]))]
                    yield HOP
                    inv0, inv1 = inverse_sum(st0, exped[0]), inverse_sum(st1, exped[1])
                    factor = dve.do(lambda: nc.vector.tensor_tensor(
                        st1[:, 1:2], st1[:, 1:2], lam[:, 6:7], ALU.mult),
                        after=[inv1, prepared["lambda"]])
                    yield HOP
                    second = act.do(lambda: nc.scalar.mul(
                        s1[:, 0:n], s1[:, 0:n], st1[:, 1:2]), after=[factor])
                    yield HOP
                    ready_ = dve.do(lambda: nc.vector.scalar_tensor_tensor(
                        s0[:, 0:n], s0[:, 0:n], st0[:, 1:2], s1[:, 0:n], ALU.mult, ALU.add),
                        after=[inv0, second])
                    small.free[st_slot0] = small.free[st_slot1] = [ready_]
                    work.free[slot1] = [ready_]
                    yield
                    aslot, a_t, copied, read = yield from weights_t(s0, n, [ready_])
                    work.free[slot0] = [read]
                    yield
                    blocks = (n - META) // P
                    wb, free = yield from banks_for()
                    for j in range(blocks):
                        pe.do(lambda: nc.tensor.matmul(
                            psum[:, wb, 0:P], v_a[:, j, h, :], a_t[:, j, :],
                            start=j == 0, stop=False), after=[copied, done_["v_a", h]] + free,
                            mark=False)
                    done = pe.do(lambda: nc.tensor.matmul(
                        psum[:, wb, 0:P], v_a_meta[:, h, :], a_t[0:META, NB, :],
                        start=False, stop=True))
                    attn_t.free[aslot] = [done]
                    done_["y_a", b, h] = copy_psum(q_a[:, h, b * P:(b + 1) * P],
                                                   psum[:, wb, 0:P], [done])
                    release_banks(wb, 1, [done_["y_a", b, h]])

            def head_weights(b, done):
                ((slot, raw, free),) = yield from slots_for(work)
                copied = evacuate(raw[:, 0:SEQ], (b, done), free)
                yield
                wb, wfree = yield from banks_for()
                for j in range(NB):
                    turned = pe.do(lambda: nc.tensor.transpose(
                        psum[:, wb, j * IDX_HEADS:(j + 1) * IDX_HEADS],
                        raw[0:IDX_HEADS, j * P:(j + 1) * P], ident[0:IDX_HEADS, 0:IDX_HEADS]),
                        after=[copied] + wfree)
                work.free[slot] = [turned]
                done_["w_i"] = act.do(lambda: nc.scalar.mul(
                    w_i[:].rearrange("p n h -> p (n h)"), psum[:, wb, 0:NB * IDX_HEADS],
                    IDX_HEADS ** -0.5), after=[turned, *entry])
                release_banks(wb, 1, [done_["w_i"]])

            def selection():
                for b in range(NB):
                    yield from indexer(b)

            def latent_c(copied):
                banks = yield from banks_for()
                stats = Stats(1, True, banks)
                for k in range(2):
                    ((slot, sq, free),) = yield from slots_for(squares)
                    done = act.do(lambda: nc.scalar.activation(sq[:], c_fm[:, k, :], ACT.Square),
                                  after=[copied[k]] + free)
                    yield
                    squares.free[slot] = [stats.add(sq, [done], k == 1)]
                yield from stats.root_steps(1.0 / B_DC, 1)
                yield
                banks = yield from banks_for(2)
                roots, spread = stats.spread(banks)
                for k in range(2):
                    done_["c", k] = normalise(c_fm[:, k, :], roots, True, gain("b_kv_norm", k),
                                              spread)
                stats.release([done_["c", 0], done_["c", 1]])
                done_["c"] = done_["c", 1]
                for k in range(2):
                    yield
                    cols = slice(k * P, (k + 1) * P)
                    banks = yield from banks_for()
                    transposed(banks, [(c_fm[:, k, META + P * j:META + P * (j + 1)], P, P)
                                       for j in range(NB)],
                               [(c_tm[:, :, cols], slice(0, P), slice(0, SEQ))],
                               [done_["c", k]], entry)
                    banks = yield from banks_for()
                    done_["c_tm", k], _ = transposed(
                        banks, [(c_fm[:, k, MET], P, META)],
                        [(c_tm_meta[:, cols], slice(0, META), slice(0, P))],
                        [done_["c", k]], entry)

            def latent_query(h, b, done):
                ((slot, raw, free),) = yield from slots_for(work)
                copied = evacuate(raw[:, 0:SEQ], (b, done), free)
                yield from made(done_, "turned")
                yield
                banks = yield from banks_for()
                stats = Stats(1, False, banks)
                square = []
                for k in range(2):
                    wb, wfree = yield from banks_for()
                    multiplied = pe.do(lambda: nc.tensor.matmul(
                        bank(wb), w_uk[:, h * B_DC + k * P:h * B_DC + (k + 1) * P],
                        raw[:, 0:SEQ], start=True, stop=True), after=[copied, uk_loaded] + wfree)
                    moved = copy_psum(q_lat[:, h, k, :], bank(wb),
                                      [multiplied, done_["turned"], *entry])
                    release_banks(wb, 1, [moved])
                    ((sq_slot, sq, free),) = yield from slots_for(squares)
                    squared_ = act.do(lambda: nc.scalar.activation(
                        sq[:, TOK], q_lat[:, h, k, :], ACT.Square), after=[moved] + free)
                    yield
                    squares.free[sq_slot] = [stats.add(sq, [squared_], k == 1)]
                work.free[slot] = [multiplied]
                yield from stats.root_steps(1.0 / B_DC, 1)
                yield
                banks = yield from banks_for()
                roots, spread = stats.spread(banks)
                for k in range(2):
                    done_["q_lat", h, k] = normalise(q_lat[:, h, k, :], roots, False,
                                                     gain("b_q_norm", k), spread)
                stats.release([done_["q_lat", h, 0], done_["q_lat", h, 1]])

            def values_token_major(h, b, done):
                ((slot, raw, free),) = yield from slots_for(work)
                copied = evacuate(raw, (b, done), free)
                yield
                banks = yield from banks_for()
                transposed(banks, [(raw[:, META + P * j:META + P * (j + 1)], P, P)
                                   for j in range(NB)],
                           [(v_a[:, :, h, :], slice(0, P), slice(0, SEQ))], [copied], entry)
                banks = yield from banks_for()
                done_["v_a", h], read = transposed(
                    banks, [(raw[:, MET], P, META)],
                    [(v_a_meta[:, h, :], slice(0, META), slice(0, P))], [copied], entry)
                work.free[slot] = [read]

            tasks.append(windows())
            group = project_group([("b2_in", i) for i in range(GROUP)], tokens_operand)
            at[0] = GROUP
            for j in range(4):
                done_["q_i", j] = evacuate(q_i[:, j, :],
                                           group[j] if j < GROUP else next_tile(False))
            done_["k_i"] = evacuate(k_i[:], next_tile(True))
            tasks.append(head_weights(*next_tile(False)))
            tasks.append(selection())
            order = iter([(b, h) for h in range(A_HEADS) for b in range(NB)])
            tasks.extend(differential(order, i) for i in range(LANES_A))
            for h in range(A_HEADS):
                copied = evacuate(q_a[:, h, :], next_tile(False))
                tasks.append(normed(q_a[:, h, :], 2, False, 1.0 / HD, gain("a_q_norm"),
                                    ("q_a", h), copied))
                copied = evacuate(k_a[:, h, :], next_tile(True))
                tasks.append(normed(k_a[:, h, :], 2, True, 1.0 / HD, gain("a_k_norm"),
                                    ("k_a", h), copied))
                tasks.append(values_token_major(h, *next_tile(True)))
            tasks.append(latent_c([evacuate(c_fm[:, k, :], next_tile(True)) for k in range(2)]))
            order = iter([(b, h) for b in range(NB) for h in range(B_HEADS)])
            tasks.extend(latent_attention(order, i) for i in range(LANES_B))
            for h in range(B_HEADS):
                tasks.append(latent_query(h, *next_tile(False)))

            read = piece_read[-1]
            y_ready = [None] * KT

            def differential_output(h):
                yield from made(done_, *(("y_a", b, h) for b in range(NB)))
                yield from normed(q_a[:, h, :], 1, False, 1.0 / P, gain("a_subln"),
                                  ("o_a", h), done_["y_a", NB - 1, h], 1.0 - LAM_INIT)
                y_ready[h] = list(split_into(x_hi[:, h, TOK], x_lo[:, h, TOK], q_a[:, h, :],
                                             after=[done_["o_a", h], read]))

            tasks.extend(differential_output(h) for h in range(A_HEADS))
            run_tasks(lambda: all(y_ready[h] for h in range(A_HEADS)))
            operand = lambda k: (x_hi[:, k, TOK], x_lo[:, k, TOK], y_ready[k])

            def add_to_x(m, b, done):
                z = dve.do(lambda: nc.vector.tensor_tensor(
                    x[:, m, TOK], x[:, m, TOK], bank(b), ALU.add), after=[done, *x_done[m]])
                release_banks(b, 1, [z])
                x_done[m] = [z]
                return z
            for m in range(KT - 1):
                add_to_x(m, *project("b2_out", m, KT, operand, k_range=(0, KT // 2)))
            run_tasks()
            for h in range(B_HEADS):
                y_ready[4 + h] = list(split_into(
                    x_hi[:, 4 + h, TOK], x_lo[:, 4 + h, TOK], q_i[:, h, :],
                    after=[*(done_["y_b", b, h] for b in range(NB)), read]))
            for i in range(len(scratch.free)):
                scratch.free[i] = work.free[i]
            gathered = RmsStats(KT - 1)
            for m in range(KT):
                z = add_to_x(m, *project("b2_out", m, KT, operand,
                                         k_range=(KT // 2, KT) if m < KT - 1 else None))
                tasks.append(square_task(gathered, m, z, x_done))
            run_tasks()
            own.close()
            region_ends()
            return gathered

        def block_2(norm):
            gathered = []

            def squares_of(k, done, _):
                if not gathered:
                    gathered.append(RmsStats(DIRECT_SQUARES))
                x_ready[k] = [done]
                return lambda: x_ready[k].append(gathered[0].square(k, [done, meta_loaded]))
            norm.finish(f"ln3_g{DEPTH - 1}", f"ln3_b{DEPTH - 1}", 2, squares_of,
                        split=False)
            x_done = [list(x_ready[k]) for k in range(KT)]
            rms_norm_x("ffn1_norm", x_done, gathered[0])
            later = []

            def second():
                if not later:
                    later.append(RmsStats(KT - 1))
                return later[0]
            ffn(("b2_gate1", 0), ("b2_up1", 0), ("b2_down1", 0), True,
                residual_both(x_done, second))
            rms_norm_x("mix_norm", x_done, later[0])
            gathered = mixer_2(x_done)
            rms_norm_x("ffn2_norm", x_done, gathered)

            def residual(m, b, done):
                z = dve.do(lambda: nc.vector.scalar_tensor_tensor(
                    x[:, m, TOK], bank(b), 0.5, x[:, m, TOK], ALU.mult, ALU.add),
                    after=[done, *x_done[m]])
                release_banks(b, 1, [z])
                x_done[m] = [z]
            ffn(("b2_gate2", 0), ("b2_up2", 0), ("b2_down2", 0), False, residual)
            for k in range(KT):
                x_ready[k] = x_done[k]
        stream_until(0)
        x_rows = t["x"].rearrange("(k p) n -> p k n", p=P)
        x_loaded = [load(sp, f"x{k}", x[:, k, TOK], x_rows[:, k, :]) for k in range(KT)]
        for k in range(KT):
            x_ready[k] = [x_loaded[k]]
            ready[k] = list(split_into(x_hi[:, k, TOK], x_lo[:, k, TOK], x[:, k, TOK],
                                       after=[x_loaded[k]]))
        tasks.append(bias_setup())
        for layer in range(DEPTH):
            norm = LayerNorm(2.0 * ALPHA, KT - 1)
            ffn(("ffn1_gu", layer * 2 * FT), ("ffn1_gu", layer * 2 * FT + FT),
                ("ffn1_down", layer * KT), False, norm.residual, group=GROUP if layer else 1)
            norm.finish(f"ln1_g{layer}", f"ln1_b{layer}", 2, split_x)
            mixer_1(layer)
            norm = LayerNorm(2.0 * ALPHA, KT - 1)
            ffn(("ffn2_gu", layer * 2 * FT), ("ffn2_gu", layer * 2 * FT + FT),
                ("ffn2_down", layer * KT), False, norm.residual)
            if layer < DEPTH - 1:
                norm.finish(f"ln3_g{layer}", f"ln3_b{layer}", 2, split_x)
        block_2(norm)
        out_sem = sem("out_stored")
        for k in range(KT):
            stored = sp.dma(out_sem, 16 * (k + 1), lambda k=k: nc.sync.dma_start(
                t["out"][k * P:(k + 1) * P, :], x[:, k, TOK]), after=x_ready[k])
        sp.wait([stored])



def weight_plan():
    plan = []

    def ffn(gate, up, down):
        for f in range(FT):
            plan.extend(pieces(gate[0], gate[1] + f, KT))
            plan.extend(pieces(up[0], up[1] + f, KT))
        for m in range(KT):
            plan.extend(pieces(down[0], down[1] + m, FT, 0, down_lead(m)))

    def matrix(name, first, n):
        for m in range(n):
            plan.extend(pieces(name, first + m, KT))

    def halves(name, first):
        for k in (0, KT // 2):
            for m in range(KT - 1):
                plan.extend(pieces(name, first + m, KT // 2, k))
        plan.extend(pieces(name, first + KT - 1, KT))

    for layer in range(DEPTH):
        ffn(("ffn1_gu", layer * 2 * FT), ("ffn1_gu", layer * 2 * FT + FT),
            ("ffn1_down", layer * KT))
        matrix("w_in", layer * IN_TILES_1, IN_TILES_1)
        halves("w_out", layer * KT)
        ffn(("ffn2_gu", layer * 2 * FT), ("ffn2_gu", layer * 2 * FT + FT),
            ("ffn2_down", layer * KT))
    ffn(("b2_gate1", 0), ("b2_up1", 0), ("b2_down1", 0))
    matrix("b2_in", 0, IN_TILES_2)
    halves("b2_out", 0)
    ffn(("b2_gate2", 0), ("b2_up2", 0), ("b2_down2", 0))
    return plan


def column_tiles(w):
    k, n = w.shape
    return np.ascontiguousarray(
        w.reshape(k // P, P, n // P, P).transpose(2, 1, 0, 3).reshape(n // P, P, k))


def head_pairs(w, axis):
    order = [h for j in range(HEADS // 2) for h in (j, HEADS // 2 + j)]
    shape = w.shape
    w = w.reshape(shape[:axis] + (HEADS, HD) + shape[axis + 1:])
    return np.take(w, order, axis=axis).reshape(shape)


def shape_tables():
    f = np.float32
    pos = np.arange(SEQ, dtype=f)
    freq_a = f(10000.0) ** (-np.arange(0, HD, 2, dtype=f) / f(HD))
    freq_r = f(1.0) / (f(10000.0) ** np.linspace(0.0, 1.0, HD // 2, dtype=f))
    ang_a, ang_r = pos[:, None] * freq_a[None], pos[:, None] * freq_r[None]
    row = np.arange(P) % HD
    at_a, at_r = row % (HD // 2), row // 2
    log_gamma = np.log1p(-np.exp2(f(-5.0) - np.arange(HEADS, dtype=f))).astype(f)
    idx = np.arange(P, dtype=f)
    diff = idx[:, None] - idx[None, :]
    decay = np.where(diff[None] >= 0,
                     np.exp(np.maximum(diff, 0)[None] * log_gamma[:, None, None]), 0).astype(f)
    w_k = np.exp((f(P) - 1 - idx)[None] * log_gamma[:, None]).astype(f)
    w_q = np.exp((idx + 1)[None] * log_gamma[:, None]).astype(f)
    g_chunk = np.exp(f(P) * log_gamma).astype(f)
    rot_a, rot_r = np.zeros((P, P), f), np.zeros((P, P), f)
    for m in range(P):
        rot_a[m + 32 if m % HD < 32 else m - 32, m] = -1 if m % HD < 32 else 1
        rot_r[m ^ 1, m] = -1 if m % 2 == 0 else 1
    q = np.arange(P)[:, None]
    rel = q - (np.arange(2 * P)[None] - P)
    parts = {
        "cos_a": np.cos(ang_a)[:, at_a].T, "sin_a": np.sin(ang_a)[:, at_a].T,
        "cos_r": np.cos(ang_r)[:, at_r].T, "sin_r": np.sin(ang_r)[:, at_r].T,
        "decay": decay.transpose(2, 0, 1).reshape(P, HEADS * P),
        "w_q": np.stack([np.repeat(w_q[2 * j:2 * j + 2], HD, axis=0) for j in range(4)], 1)
        .reshape(P, 4 * P),
        "w_k": np.repeat(w_k.T, HD, axis=1),
        "g_chunk": np.stack([np.repeat(g_chunk[2 * j:2 * j + 2], HD) for j in range(4)], 1),
        "band": np.where((rel >= 0) & (rel < P), 0.0, -BIG),
        "rot_a": rot_a, "rot_r": rot_r,
    }
    at, cols, n = {}, [], 0
    for name, v in parts.items():
        at[name] = (n, n + v.shape[1])
        n += v.shape[1]
        cols.append(v.astype(f))
    return np.ascontiguousarray(np.concatenate(cols, 1)), at


WINDOW_2 = 2 * P
REL_N = 3 * P - 1


def distance_buckets():
    f = np.float32
    n = 255 - np.arange(REL_N)
    nf = np.maximum(n, 1).astype(f)
    large = 16 + (np.log(nf / f(16)) / f(np.log(8.0)) * f(16)).astype(np.int32)
    bucket = np.where(n < 16, n, np.minimum(large, BUCKETS - 1))
    assert bucket[0] == BUCKETS - 1 and bucket[255 - (P + 1)] == BUCKETS - 1
    hot = np.zeros((BUCKETS, REL_N), f)
    for i in range(REL_N):
        if n[i] >= 0:
            hot[bucket[i], i] = 1
    return hot, np.broadcast_to(np.where(n >= 0, 0.0, -BIG).astype(f), (8, REL_N)).copy()


def kernel(**inputs):
    from concourse import bacc
    from concourse.bass_utils import run_bass_kernel_spmd

    v = {k: np.asarray(a) for k, a in inputs.items()}
    arrays = {}

    arrays["x"] = np.ascontiguousarray(v["x"][0].T)
    arrays["meta"] = np.ascontiguousarray(v["meta_tokens_2"].T)

    def stacked(name, per_layer):
        return np.concatenate([column_tiles(per_layer(w)) for w in v[name]], 0)

    aw, kw = HEADS * HD, 2 * HD
    cuts = np.cumsum([aw, kw, kw, 512, 512, 512])

    def in_1(w):
        qa, ka, va, qr, kr, vr, gr = np.split(w, cuts, axis=1)
        tiles = [head_pairs(qa, 1), ka, va]
        for j in range(4):
            tiles += [a[:, j * P:(j + 1) * P] for a in (qr, kr, vr)]
        return np.concatenate(tiles + [gr], 1)

    def in_2(w):
        qa, ka, va, qb, ckv, iq, ik, iw = np.split(
            w, np.cumsum([512, 512, 512, 512, 256, 512, 64]), axis=1)
        heads = [a[:, h * P:(h + 1) * P] for h in range(A_HEADS) for a in (qa, ka, va)]
        return np.concatenate([iq, ik, ik, np.tile(iw, (1, P // IDX_HEADS)), *heads,
                               ckv, qb], 1)

    same = lambda w: w
    arrays["w_in"] = stacked("w_in", in_1)
    arrays["w_out"] = stacked("w_out", lambda w: np.concatenate(
        [head_pairs(w[:aw], 0), w[aw:]], 0))
    for name in ("ffn1", "ffn2"):
        arrays[name + "_gu"] = stacked(name + "_w_gu", same)
        arrays[name + "_down"] = stacked(name + "_w_down", same)
    arrays["b2_in"] = stacked("w_in_2", in_2)
    arrays["b2_out"] = stacked("w_out_2", same)
    for i in "12":
        arrays["b2_gate" + i] = stacked(f"ffn{i}_w_gate_2", same)
        arrays["b2_up" + i] = stacked(f"ffn{i}_w_up_2", same)
        arrays["b2_down" + i] = stacked(f"ffn{i}_w_down_2", same)
    arrays["w_uk"] = np.ascontiguousarray(
        v["b_w_uk_2"][0].transpose(1, 0, 2).reshape(P, B_HEADS * B_DC))
    arrays["w_uv"] = np.ascontiguousarray(
        v["b_w_uv_2"][0].reshape(B_HEADS, 2, P, P).transpose(2, 0, 1, 3).reshape(P, -1))
    arrays["rel_bias"] = np.ascontiguousarray(v["rel_bias_2"])

    gain_at, cols = {}, []

    def column(name, a):
        gain_at[name] = sum(c.shape[1] for c in cols)
        cols.append(np.ascontiguousarray(a))

    for layer in range(DEPTH):
        for n in "123":
            column(f"ln{n}_g{layer}", v[f"ln{n}_g"][layer].reshape(KT, P).T)
            column(f"ln{n}_b{layer}", v[f"ln{n}_b"][layer].reshape(KT, P).T)
        column(f"sinks{layer}", np.broadcast_to(
            v["attn_sinks"][layer][None], (P, HEADS)))
    for n in ("ffn1_norm", "mix_norm", "ffn2_norm"):
        column(n, v[n + "_2"][0].reshape(KT, P).T)
    for n in ("a_q_norm", "a_k_norm"):
        column(n, np.tile(v[n + "_2"][0], 2)[:, None])
    column("a_subln", v["a_subln_2"][0][:, None])
    for n in ("b_kv_norm", "b_q_norm"):
        column(n, v[n + "_2"][0].reshape(2, P).T)
    for n in ("q1", "k1", "q2", "k2"):
        column("lambda_" + n, np.tile(v[f"a_lambda_{n}_2"][0], 2)[:, None])
    arrays["gains"] = np.ascontiguousarray(np.concatenate(cols, 1))

    arrays["ident"] = np.eye(P, dtype=np.float32)
    arrays["flip"] = np.eye(P, dtype=np.float32)[::-1].copy()
    arrays["half"] = np.kron(np.eye(2, dtype=np.float32), np.ones((HD, HD), np.float32))
    arrays["tables"], table_at = shape_tables()
    arrays["distance_hot"], arrays["distance_mask"] = distance_buckets()

    nc = bacc.Bacc("TRN2", target_bir_lowering=False, num_devices=1)
    t = {"gain_at": gain_at, "table_at": table_at}
    feed = {}
    for name, a in arrays.items():
        feed["in_" + name] = a
        t[name] = nc.dram_tensor("in_" + name, a.shape, F32, kind="ExternalInput").ap()
    t["out"] = nc.dram_tensor("out", (D, SEQ), F32, kind="ExternalOutput").ap()
    t["bias_rows"] = nc.dram_tensor("bias_rows", (8, REL_N), F32, kind="Internal").ap()
    build(nc, t)
    result = run_bass_kernel_spmd(nc, [feed], core_ids=[0]).results[0]["out"]
    return np.ascontiguousarray(np.asarray(result).T)[None]
```
